# Optimizing a Trainium2 kernel written in Bass

```python
import jax, jax.numpy as jnp
from jax import lax
import numpy as np
import jax
import jax.numpy as jnp

D_MODEL = 2048
BATCH = 1
SEQ = 256
DEPTH = 1

GRID_W = 64
D_ATTN = D_MODEL // 2
HEAD_DIM = 128
N_ATTN_HEADS = D_ATTN // HEAD_DIM
WIN_R = 8
WIN_C = 16
D_REC = D_MODEL - D_ATTN
REC_BLOCKS = 8
REC_BLOCK_W = D_REC // REC_BLOCKS
CONV_W = 4
C_RG = 8.0
D_IN_PROJ = 3 * D_ATTN + 2 * D_REC
D_FF = -(-8 * D_MODEL // (3 * 256)) * 256
D_PLE = 256
EPS = 1e-6
NEG_INF = -1e9


def rms_norm(x, g):
    x32 = x.astype(jnp.float32)
    y = x32 * lax.rsqrt(jnp.mean(x32 * x32, axis=-1, keepdims=True) + EPS)
    return (y * g.astype(jnp.float32)).astype(x.dtype)

def neighborhood_attention(q, k, v, rpb):
    B, S, H, Dh = q.shape
    rows = S // GRID_W
    kr = min(WIN_R, rows)
    cols = jnp.arange(GRID_W)
    cstart = jnp.clip(cols - WIN_C // 2, 0, GRID_W - WIN_C)
    col_ok = (cols[None, :] >= cstart[:, None]) & (cols[None, :] < cstart[:, None] + WIN_C)
    dc_idx = jnp.clip(cols[None, :] - cols[:, None] + WIN_C - 1, 0, 2 * WIN_C - 2)
    bias_col = jnp.where(col_ok[None, None], rpb.astype(jnp.float32)[:, :, dc_idx], NEG_INF)
    scale = HEAD_DIM ** -0.5
    qg = (q * scale).reshape(B, rows, GRID_W, H, Dh)
    kg = k.reshape(B, rows, GRID_W, H, Dh)
    vg = v.reshape(B, rows, GRID_W, H, Dh)

    def row_block(r):
        rstart = jnp.clip(r - kr // 2, 0, rows - kr)
        q_r = lax.dynamic_index_in_dim(qg, r, axis=1, keepdims=False)
        k_r = lax.dynamic_slice_in_dim(kg, rstart, kr, axis=1)
        v_r = lax.dynamic_slice_in_dim(vg, rstart, kr, axis=1)
        dr_idx = rstart + jnp.arange(kr) - r + WIN_R - 1
        bias = jnp.take(bias_col, dr_idx, axis=1)
        s = jnp.einsum('bqhd,bkwhd->bhkqw', q_r, k_r,
                       preferred_element_type=jnp.float32) + bias
        pr = jax.nn.softmax(s, axis=(2, 4)).astype(v.dtype)
        return jnp.einsum('bhkqw,bkwhd->bqhd', pr, v_r)

    out = lax.map(row_block, jnp.arange(rows))
    return out.transpose(1, 0, 2, 3, 4).reshape(B, S, H * Dh)

def linear_scan(a, b):
    def combine(l, r):
        return (l[0] * r[0], r[0] * l[1] + r[1])
    return lax.associative_scan(combine, (a, b), axis=1)[1]

def rglru_bidirectional(xr, conv_w, conv_b, w_a, b_a, w_i, b_i, lam):
    B, S, _ = xr.shape
    left = CONV_W // 2
    xp = jnp.pad(xr, ((0, 0), (left, CONV_W - 1 - left), (0, 0)))
    xc = conv_b + xp[:, 0:S] * conv_w[0]
    for j in range(1, CONV_W):
        xc = xc + xp[:, j:j + S] * conv_w[j]
    xb = xc.reshape(B, S, REC_BLOCKS, REC_BLOCK_W)
    r_gate = jax.nn.sigmoid(
        jnp.einsum('bsnc,zncd->zbsnd', xb, w_a).reshape(2, B, S, D_REC) + b_a[:, None, None, :])
    i_gate = jax.nn.sigmoid(
        jnp.einsum('bsnc,zncd->zbsnd', xb, w_i).reshape(2, B, S, D_REC) + b_i[:, None, None, :])
    log_a = -C_RG * r_gate.astype(jnp.float32) * jax.nn.softplus(-lam.astype(jnp.float32))[:, None, None, :]
    a = jnp.exp(log_a)
    bterm = jnp.sqrt(-jnp.expm1(2.0 * log_a)) * i_gate.astype(jnp.float32) * xc.astype(jnp.float32)[None]
    h_fwd = linear_scan(a[0], bterm[0])
    h_bwd = jnp.flip(linear_scan(jnp.flip(a[1], axis=1), jnp.flip(bterm[1], axis=1)), axis=1)
    return (h_fwd + h_bwd).astype(xr.dtype)

def first_inputs(seed: int = 0) -> dict:
    key = jax.random.key(seed)
    ks = jax.random.split(key, 32)
    f32 = jnp.float32

    def nrm(k, shape, scale):
        return jax.random.normal(k, shape, f32) * scale

    def gain(k, n):
        return 1.0 + 0.02 * jax.random.normal(k, (DEPTH, n), f32)

    u = jax.random.uniform(ks[10], (DEPTH, 2, D_REC), f32, minval=0.9, maxval=0.999)
    a0 = u ** (1.0 / C_RG)
    lam = jnp.log(a0) - jnp.log1p(-a0)
    return {
        "x": nrm(ks[0], (BATCH, SEQ, D_MODEL), 1.0),
        "p": nrm(ks[1], (DEPTH, BATCH, SEQ, D_PLE), 1.0),
        "g_mix_pre": gain(ks[2], D_MODEL),
        "w_in": nrm(ks[3], (DEPTH, D_MODEL, D_IN_PROJ), D_MODEL ** -0.5),
        "rpb": nrm(ks[4], (DEPTH, N_ATTN_HEADS, 2 * WIN_R - 1, 2 * WIN_C - 1), 0.02),
        "conv_w": nrm(ks[5], (DEPTH, CONV_W, D_REC), CONV_W ** -0.5),
        "conv_b": nrm(ks[6], (DEPTH, D_REC), 0.01),
        "w_rg_a": nrm(ks[7], (DEPTH, 2, REC_BLOCKS, REC_BLOCK_W, REC_BLOCK_W), REC_BLOCK_W ** -0.5),
        "b_rg_a": nrm(ks[8], (DEPTH, 2, D_REC), 0.01),
        "w_rg_i": nrm(ks[9], (DEPTH, 2, REC_BLOCKS, REC_BLOCK_W, REC_BLOCK_W), REC_BLOCK_W ** -0.5),
        "b_rg_i": nrm(ks[11], (DEPTH, 2, D_REC), 0.01),
        "lam": lam,
        "g_attn_out": gain(ks[12], D_ATTN),
        "g_rec_out": gain(ks[13], D_REC),
        "w_out": nrm(ks[14], (DEPTH, D_ATTN + D_REC, D_MODEL), (D_ATTN + D_REC) ** -0.5),
        "g_mix_post": gain(ks[15], D_MODEL),
        "g_ffn_pre": gain(ks[16], D_MODEL),
        "w_ffn_gate": nrm(ks[17], (DEPTH, D_MODEL, D_FF), D_MODEL ** -0.5),
        "w_ffn_up": nrm(ks[18], (DEPTH, D_MODEL, D_FF), D_MODEL ** -0.5),
        "w_ffn_down": nrm(ks[19], (DEPTH, D_FF, D_MODEL), D_FF ** -0.5),
        "g_ffn_post": gain(ks[20], D_MODEL),
        "g_ple_pre": gain(ks[21], D_MODEL),
        "w_ple_gate": nrm(ks[22], (DEPTH, D_MODEL, D_MODEL), D_MODEL ** -0.5),
        "w_ple_proj": nrm(ks[23], (DEPTH, D_PLE, D_MODEL), D_PLE ** -0.5),
        "g_ple_post": gain(ks[24], D_MODEL),
    }

def first_block(x, p, g_mix_pre, w_in, rpb, conv_w, conv_b, w_rg_a, b_rg_a, w_rg_i, b_rg_i,
              lam, g_attn_out, g_rec_out, w_out, g_mix_post, g_ffn_pre, w_ffn_gate,
              w_ffn_up, w_ffn_down, g_ffn_post, g_ple_pre, w_ple_gate, w_ple_proj, g_ple_post):
    B, S, _ = x.shape
    h = x
    for i in range(DEPTH):
        hn = rms_norm(h, g_mix_pre[i])
        u = hn @ w_in[i]
        q, k, v, xr, yg = jnp.split(
            u, [D_ATTN, 2 * D_ATTN, 3 * D_ATTN, 3 * D_ATTN + D_REC], axis=-1)
        attn = neighborhood_attention(
            q.reshape(B, S, N_ATTN_HEADS, HEAD_DIM),
            k.reshape(B, S, N_ATTN_HEADS, HEAD_DIM),
            v.reshape(B, S, N_ATTN_HEADS, HEAD_DIM), rpb[i])
        rec = rglru_bidirectional(xr, conv_w[i], conv_b[i], w_rg_a[i], b_rg_a[i],
                                  w_rg_i[i], b_rg_i[i], lam[i]) * jax.nn.gelu(yg)
        mixed = jnp.concatenate(
            [rms_norm(attn, g_attn_out[i]), rms_norm(rec, g_rec_out[i])], axis=-1) @ w_out[i]
        h = h + rms_norm(mixed, g_mix_post[i])
        fn = rms_norm(h, g_ffn_pre[i])
        ff = (jax.nn.silu(fn @ w_ffn_gate[i]) * (fn @ w_ffn_up[i])) @ w_ffn_down[i]
        h = h + rms_norm(ff, g_ffn_post[i])
        gate = jax.nn.sigmoid(rms_norm(h, g_ple_pre[i]) @ w_ple_gate[i])
        ple = p[i] @ w_ple_proj[i]
        h = h + rms_norm(gate * ple, g_ple_post[i])
    return h


GLA_HEADS = 4
GLA_DK = 64
GLA_DV = 128
GLA_GATE_RANK = 16
GLA_TAU = 16.0
GLA_CHUNK = 64

DIL_HEADS = 12
DIL_PATTERNS = ((128, 1), (512, 4), (2048, 16))
ROPE_THETA = 500000.0
ROPE_DIM = HEAD_DIM // 4
MASK_VALUE = -1e30

PEER_HEADS = 8
PEER_NKEYS = 128
PEER_NEXPERTS = PEER_NKEYS * PEER_NKEYS
PEER_QDIM = 256
PEER_TOPK = 16
PEER_TOKEN_BLOCK = 128

GLA_QK_W = GLA_HEADS * GLA_DK
GLA_V_W = GLA_HEADS * GLA_DV
DIL_W = DIL_HEADS * HEAD_DIM
MIX_W = GLA_V_W + DIL_W
IN_SPLITS = (GLA_QK_W, GLA_QK_W, GLA_V_W, GLA_GATE_RANK, GLA_GATE_RANK, GLA_V_W, DIL_W, DIL_W, DIL_W)
IN_W = sum(IN_SPLITS)


def rms_norm_2(x, g):
    xf = x.astype(jnp.float32)
    y = xf * lax.rsqrt(jnp.mean(xf * xf, axis=-1, keepdims=True) + EPS)
    return (y * g.astype(jnp.float32)).astype(x.dtype)

def partial_rope(t, positions):
    half = ROPE_DIM // 2
    inv_freq = ROPE_THETA ** (-jnp.arange(half, dtype=jnp.float32) / half)
    ang = positions.astype(jnp.float32)[:, None] * inv_freq[None, :]
    cos = jnp.cos(ang)[None, :, None, :]
    sin = jnp.sin(ang)[None, :, None, :]
    tf = t.astype(jnp.float32)
    x1 = tf[..., :half]
    x2 = tf[..., half:ROPE_DIM]
    return jnp.concatenate([x1 * cos - x2 * sin, x2 * cos + x1 * sin, tf[..., ROPE_DIM:]], axis=-1)

def gla_direction(q, k, v, log_a, include_diag):
    Bsz, H, S, dk = q.shape
    dv = v.shape[-1]
    C = GLA_CHUNK
    N = S // C
    q = q.reshape(Bsz, H, N, C, dk)
    k = k.reshape(Bsz, H, N, C, dk)
    v = v.reshape(Bsz, H, N, C, dv)
    b = jnp.cumsum(log_a.reshape(Bsz, H, N, C, dk), axis=3)
    b_last = b[:, :, :, -1:, :]
    q_in = q * jnp.exp(b)
    k_in = k * jnp.exp(-b)
    scores = jnp.einsum('bhnik,bhnjk->bhnij', q_in, k_in)
    mask = jnp.tril(jnp.ones((C, C), dtype=bool), k=0 if include_diag else -1)
    o_intra = jnp.einsum('bhnij,bhnjv->bhniv', jnp.where(mask, scores, 0.0), v)
    k_state = k * jnp.exp(b_last - b)
    inc = jnp.einsum('bhnjk,bhnjv->bhnkv', k_state, v)
    decay = jnp.exp(b_last[:, :, :, 0, :])

    def step(state, inp):
        dec, add = inp
        return dec[..., None] * state + add, state

    s0 = jnp.zeros((Bsz, H, dk, dv), jnp.float32)
    _, s_before = lax.scan(step, s0, (jnp.moveaxis(decay, 2, 0), jnp.moveaxis(inc, 2, 0)))
    s_before = jnp.moveaxis(s_before, 0, 2)
    o_inter = jnp.einsum('bhnik,bhnkv->bhniv', q_in, s_before)
    return (o_intra + o_inter).reshape(Bsz, H, S, dv)

def gla_mixer(q, k, v, gate_down_f, gate_down_b, r, up_f, bias_f, up_b, bias_b, out_g):
    Bsz, S, _ = q.shape
    f32 = jnp.float32

    def heads(t, d):
        return t.astype(f32).reshape(Bsz, S, GLA_HEADS, d).transpose(0, 2, 1, 3)

    qh = heads(q, GLA_DK) * (GLA_DK ** -0.5)
    kh = heads(k, GLA_DK)
    vh = heads(v, GLA_DV)
    la_f = heads(jax.nn.log_sigmoid(gate_down_f.astype(f32) @ up_f.astype(f32) + bias_f.astype(f32)) / GLA_TAU, GLA_DK)
    la_b = heads(jax.nn.log_sigmoid(gate_down_b.astype(f32) @ up_b.astype(f32) + bias_b.astype(f32)) / GLA_TAU, GLA_DK)

    def rev(t):
        return jnp.flip(t, axis=2)

    o_fwd = gla_direction(qh, kh, vh, la_f, True)
    o_bwd = rev(gla_direction(rev(qh), rev(kh), rev(vh), rev(la_b), False))
    o = (o_fwd + o_bwd).transpose(0, 2, 1, 3)
    o = rms_norm_2(o, out_g.reshape(GLA_HEADS, GLA_DV))
    return o.reshape(Bsz, S, GLA_V_W) * jax.nn.silu(r.astype(f32))

def dilated_window_attention(q, k, v, window, dilation):
    Bsz, S, H, hd = q.shape
    half = window // (2 * dilation)
    L = S // dilation
    nb = -(-L // half)
    Lp = nb * half

    def to_blocks(t):
        t = t.reshape(Bsz, L, dilation, H, hd)
        t = jnp.pad(t, ((0, 0), (0, Lp - L), (0, 0), (0, 0), (0, 0)))
        return t.reshape(Bsz, nb, half, dilation, H, hd)

    def with_neighbours(t):
        tp = jnp.pad(t, ((0, 0), (1, 1), (0, 0), (0, 0), (0, 0), (0, 0)))
        return jnp.concatenate([tp[:, :-2], tp[:, 1:-1], tp[:, 2:]], axis=2)

    qb = to_blocks(q)
    kn = with_neighbours(to_blocks(k))
    vn = with_neighbours(to_blocks(v))
    s = jnp.einsum('bnqrhe,bnkrhe->bnrhqk', qb, kn)
    qpos = jnp.arange(nb)[:, None] * half + jnp.arange(half)[None, :]
    kpos = jnp.arange(nb)[:, None] * half - half + jnp.arange(3 * half)[None, :]
    rel = kpos[:, None, :] - qpos[:, :, None]
    valid = (jnp.abs(rel) <= half) & (kpos[:, None, :] >= 0) & (kpos[:, None, :] < L)
    s = jnp.where(valid[None, :, None, None], s, MASK_VALUE)
    m = jnp.max(s, axis=-1)
    p = jnp.exp(s - m[..., None])
    den = jnp.sum(p, axis=-1)
    m_t = jnp.moveaxis(m, (2, 3, 4), (3, 4, 2))
    den_t = jnp.moveaxis(den, (2, 3, 4), (3, 4, 2))
    o = jnp.einsum('bnrhqk,bnkrhe->bnqrhe', p, vn) / den_t[..., None]

    def back(t):
        t = t.reshape((Bsz, Lp, dilation, H) + t.shape[5:])[:, :L]
        return t.reshape((Bsz, S, H) + t.shape[4:])

    return back(o), back(m_t), back(den_t)

def dilated_mixer(q, k, v, q_norm_g, k_norm_g, positions):
    Bsz, S, _ = q.shape
    shp = (Bsz, S, DIL_HEADS, HEAD_DIM)
    qh = partial_rope(rms_norm_2(q.reshape(shp), q_norm_g), positions) * (HEAD_DIM ** -0.5)
    kh = partial_rope(rms_norm_2(k.reshape(shp), k_norm_g), positions)
    vh = v.reshape(shp).astype(jnp.float32)
    outs, maxes, dens = [], [], []
    for window, dilation in DIL_PATTERNS:
        o, m, d = dilated_window_attention(qh, kh, vh, window, dilation)
        outs.append(o)
        maxes.append(m)
        dens.append(d)
    m_all = jnp.stack(maxes)
    w = jnp.stack(dens) * jnp.exp(m_all - jnp.max(m_all, axis=0, keepdims=True))
    w = w / jnp.sum(w, axis=0, keepdims=True)
    o = jnp.sum(w[..., None] * jnp.stack(outs), axis=0)
    return o.reshape(Bsz, S, DIL_W)

def peer_ffn(xn, w_query, sub_keys, expert_down, expert_up):
    Bsz, S, D = xn.shape
    f32 = jnp.float32
    T = Bsz * S
    xt = xn.reshape(T, D)
    qry = (xt @ w_query).reshape(T, PEER_HEADS, 2, PEER_QDIM // 2)
    sc = jnp.einsum('thcd,hckd->thck', qry.astype(f32), sub_keys.astype(f32))
    top_s, top_i = lax.top_k(sc, PEER_TOPK)
    kk = PEER_TOPK * PEER_TOPK
    cand_s = (top_s[:, :, 0, :, None] + top_s[:, :, 1, None, :]).reshape(T, PEER_HEADS, kk)
    cand_i = (top_i[:, :, 0, :, None] * PEER_NKEYS + top_i[:, :, 1, None, :]).reshape(T, PEER_HEADS, kk)
    best_s, best_pos = lax.top_k(cand_s, PEER_TOPK)
    idx = jnp.take_along_axis(cand_i, best_pos, axis=-1)
    gates = jax.nn.softmax(best_s, axis=-1)
    K = PEER_HEADS * PEER_TOPK
    nblk = T // PEER_TOKEN_BLOCK

    def block(args):
        xb, ib, gb = args
        u = expert_down[ib]
        act = jax.nn.gelu(jnp.einsum('tkd,td->tk', u, xb).astype(f32))
        vv = expert_up[ib]
        return jnp.einsum('tk,tkd->td', (gb * act).astype(vv.dtype), vv)

    out = lax.map(block, (xt.reshape(nblk, PEER_TOKEN_BLOCK, D),
                          idx.reshape(nblk, PEER_TOKEN_BLOCK, K),
                          gates.reshape(nblk, PEER_TOKEN_BLOCK, K)))
    return out.reshape(Bsz, S, D).astype(xn.dtype)

def second_inputs(seed: int = 0) -> dict:
    key = jax.random.key(seed)
    ks = jax.random.split(key, 16)
    f32 = jnp.float32

    def nrm(k, shape, scale):
        return jax.random.normal(k, shape, f32) * scale

    def gain(k, shape):
        return 1.0 + 0.02 * jax.random.normal(k, shape, f32)

    L = DEPTH
    return {
        'x': nrm(ks[0], (BATCH, SEQ, D_MODEL), 1.0),
        'norm1_g': gain(ks[1], (L, D_MODEL)),
        'w_in': nrm(ks[2], (L, D_MODEL, IN_W), D_MODEL ** -0.5),
        'gla_up_f': nrm(ks[3], (L, GLA_GATE_RANK, GLA_QK_W), GLA_GATE_RANK ** -0.5),
        'gla_bias_f': nrm(ks[4], (L, GLA_QK_W), 0.1),
        'gla_up_b': nrm(ks[5], (L, GLA_GATE_RANK, GLA_QK_W), GLA_GATE_RANK ** -0.5),
        'gla_bias_b': nrm(ks[6], (L, GLA_QK_W), 0.1),
        'gla_out_g': gain(ks[7], (L, GLA_V_W)),
        'q_norm_g': gain(ks[8], (L, HEAD_DIM)),
        'k_norm_g': gain(ks[9], (L, HEAD_DIM)),
        'w_out': nrm(ks[10], (L, MIX_W, D_MODEL), MIX_W ** -0.5),
        'norm2_g': gain(ks[11], (L, D_MODEL)),
        'peer_w_query': nrm(ks[12], (L, D_MODEL, PEER_HEADS * PEER_QDIM), D_MODEL ** -0.5),
        'peer_sub_keys': nrm(ks[13], (L, PEER_HEADS, 2, PEER_NKEYS, PEER_QDIM // 2), (PEER_QDIM // 2) ** -0.5),
        'peer_down': nrm(ks[14], (L, PEER_NEXPERTS, D_MODEL), D_MODEL ** -0.5),
        'peer_up': nrm(ks[15], (L, PEER_NEXPERTS, D_MODEL), PEER_HEADS ** -0.5),
    }

def second_block(x, norm1_g, w_in, gla_up_f, gla_bias_f, gla_up_b, gla_bias_b, gla_out_g, q_norm_g, k_norm_g, w_out, norm2_g, peer_w_query, peer_sub_keys, peer_down, peer_up):
    positions = jnp.arange(x.shape[1], dtype=jnp.int32)
    split_points = [int(c) for c in np.cumsum(IN_SPLITS)[:-1]]
    for l in range(DEPTH):
        xn = rms_norm_2(x, norm1_g[l])
        h = xn @ w_in[l]
        qa, ka, va, gdf, gdb, ra, qd, kd, vd = jnp.split(h, split_points, axis=-1)
        oa = gla_mixer(qa, ka, va, gdf, gdb, ra, gla_up_f[l], gla_bias_f[l], gla_up_b[l], gla_bias_b[l], gla_out_g[l])
        od = dilated_mixer(qd, kd, vd, q_norm_g[l], k_norm_g[l], positions)
        mixed = jnp.concatenate([oa, od], axis=-1).astype(x.dtype)
        x = x + mixed @ w_out[l]
        x = x + peer_ffn(rms_norm_2(x, norm2_g[l]), peer_w_query[l], peer_sub_keys[l], peer_down[l], peer_up[l])
    return x


def setup_inputs(seed=0):
    out = dict(first_inputs(seed))
    for name, value in second_inputs(seed + 1).items():
        if name != "x":
            out[name + "_2"] = value
    return out


def reference(
    x, p, g_mix_pre, w_in, rpb, conv_w, conv_b, w_rg_a, b_rg_a, w_rg_i, b_rg_i, lam, g_attn_out,
    g_rec_out, w_out, g_mix_post, g_ffn_pre, w_ffn_gate, w_ffn_up, w_ffn_down, g_ffn_post,
    g_ple_pre, w_ple_gate, w_ple_proj, g_ple_post, norm1_g_2, w_in_2, gla_up_f_2, gla_bias_f_2,
    gla_up_b_2, gla_bias_b_2, gla_out_g_2, q_norm_g_2, k_norm_g_2, w_out_2, norm2_g_2,
    peer_w_query_2, peer_sub_keys_2, peer_down_2, peer_up_2,
):
    x = first_block(
        x, p, g_mix_pre, w_in, rpb, conv_w, conv_b, w_rg_a, b_rg_a, w_rg_i, b_rg_i, lam,
        g_attn_out, g_rec_out, w_out, g_mix_post, g_ffn_pre, w_ffn_gate, w_ffn_up, w_ffn_down,
        g_ffn_post, g_ple_pre, w_ple_gate, w_ple_proj, g_ple_post,
    )
    return second_block(
        x, norm1_g_2, w_in_2, gla_up_f_2, gla_bias_f_2, gla_up_b_2, gla_bias_b_2, gla_out_g_2,
        q_norm_g_2, k_norm_g_2, w_out_2, norm2_g_2, peer_w_query_2, peer_sub_keys_2,
        peer_down_2, peer_up_2,
    )


_drawn_inputs = setup_inputs


def setup_inputs(seed=0):
    import zlib

    import numpy as np

    out = dict(_drawn_inputs(seed))
    spreads = {}
    factors = {'rpb': 4.123,
     'b_rg_a': 8.0,
     'b_rg_i': 8.0,
     'g_attn_out': 3.862,
     'g_rec_out': 3.746,
     'g_mix_post': 2.938,
     'g_ffn_pre': 3.043,
     'g_ffn_post': 3.99,
     'g_ple_pre': 7.586,
     'g_ple_post': 4.067,
     'norm1_g_2': 5.567,
     'gla_up_f_2': 3.262,
     'gla_bias_f_2': 6.991,
     'gla_up_b_2': 3.577,
     'gla_bias_b_2': 7.076,
     'gla_out_g_2': 25.692,
     'q_norm_g_2': 8.0,
     'k_norm_g_2': 8.0,
     'norm2_g_2': 33.68}
    for name, (base, spread) in spreads.items():
        noise = np.random.default_rng([zlib.crc32(name.encode()), seed]).standard_normal(out[name].shape)
        drawn = base * np.exp(spread * noise) if base else spread * noise
        out[name] = jnp.asarray(drawn.astype(out[name].dtype))
    for name, factor in factors.items():
        out[name] = (out[name] * factor).astype(out[name].dtype)
    return out
```

```python
import numpy as np
import concourse.bass as bass
from concourse import mybir
from contextlib import ExitStack

F32 = mybir.dt.float32
F32R = mybir.dt.float32r
U32 = mybir.dt.uint32
ALU = mybir.AluOpType
ACT = mybir.ActivationFunctionType
AX = mybir.AxisListType

P = 128
T = 256
TT = T // P
D = 2048
KB = D // P
DFF = 5632
FB = DFF // P
EPS = 1e-6
NCH = 512
HD = 128
SCALE = HD ** -0.5
HEADS1 = 8
HEADS2 = 12
GLA_W = 512
EXPERTS = 16384
NKEY = 128
PIECE = 1024

STAGES = [("in1", 80), ("out1", 32), ("ffn", 176), ("down", 88), ("gate", 32), ("in2", 96),
          ("out2", 32), ("query", 32), ("peer_down", 256), ("peer_up", 256)]
ROUND0, _n = {}, 0
for _name, _pieces in STAGES:
    ROUND0[_name] = _n // 4
    _n += _pieces
PIECES = _n
ROUNDS = PIECES // 4


def after(name, pieces):
    return 4 * ROUND0[name] + pieces


COLS, _n = {}, 0
for _name, _w in [("g_mix", 16), ("g_ffn", 16), ("g_ple", 16), ("g_n1", 16), ("g_n2", 16),
                  ("g_mo", 16), ("g_gla", 4), ("conv_w", 32), ("conv_b", 8), ("b_a", 16),
                  ("b_i", 16), ("lam", 16), ("gla_b", 4)]:
    COLS[_name] = (_n, _w)
    _n += _w
NCOLS = _n
CONS, _n = {}, 0
for _name, _w in [("ident", 128), ("iota", 128), ("ones", 128), ("cos", 32), ("sin", 32),
                  ("scan", 256), ("causal", 256)]:
    CONS[_name] = (_n, _w)
    _n += _w
NCONS = _n


def shape_constants():
    c = np.zeros((P, NCONS), np.float32)
    lane = np.arange(P)

    def put(name, a):
        o, w = CONS[name]
        c[:, o:o + w] = np.asarray(a, np.float32).reshape(P, w)

    put("ident", np.eye(P))
    put("ones", np.ones((P, P)))
    put("iota", np.broadcast_to(lane, (P, P)))
    half = 16
    inv = np.float32(500000.0) ** (-np.arange(half, dtype=np.float32) / np.float32(half))
    ang = (np.arange(T, dtype=np.float32)[:, None] * inv[None, :]).astype(np.float32)
    put("cos", np.cos(ang).reshape(TT, P, half).transpose(1, 0, 2))
    put("sin", np.sin(ang).reshape(TT, P, half).transpose(1, 0, 2))
    put("scan", np.broadcast_to(np.arange(T) % 64 != 0, (P, T)))
    same = lane[:, None] // 64 == lane[None, :] // 64
    key, query = lane[:, None], lane[None, :]
    put("causal", np.stack([same & (key <= query), same & (key > query)], 1))
    col = np.arange(64)
    start = np.clip(col - 8, 0, 48)
    near = (col[None] >= start[:, None]) & (col[None] < start[:, None] + 16)
    band = np.where(near, 0.0, -1e9)[lane % 64].astype(np.float32)
    q = np.arange(T)
    gap = np.abs(q[:, None] - q[None, :])
    times = (gap <= 64).astype(np.float32) + (gap % 4 == 0) + (gap % 16 == 0)
    times = times.reshape(TT, P, T).transpose(1, 0, 2).astype(np.float32)
    dil = np.stack([np.where(times == 0, -1e30, 0.0), times], 1).astype(np.float32)
    return c, band, dil


def build(nc, stream, cols, cons, band, dil, x, rpb, w_gates, gains, p_t, w_proj, w_gd, up_fb,
          qk_gain, sub_keys, spill, out):
    ctx = ExitStack()
    with ctx:
        def sem(name):
            return ctx.enter_context(nc.semaphore(name))

        base = -(-nc.sbuf_base // 32) * 32
        ctx.enter_context(nc.sbuf_tensor("whole", [P, (nc.sbuf_top - nc.sbuf_base - 32) // 4], F32))

        def place(name, shape, at, dt=F32):
            return nc.alloc_sbuf_tensor_at(name, shape, dt, offset=base + at)

        cons_sb = place("cons_sb", [P, NCONS], 0)
        cols_sb = place("cols_sb", [P, NCOLS], NCONS * 4)
        X_AT = 8032
        STATS = 320
        small = place("small", [P, STATS], X_AT - 4 * STATS)
        assert (NCONS + NCOLS + STATS) * 4 <= X_AT
        hot_at = 256 * 4
        i_t, j_t, gate_t = (place(n, [P, T], hot_at + 1024 * k)
                            for k, n in enumerate(("i_t", "j_t", "gate_t")))
        hot = place("hot", [P, 2, 2, P], hot_at + 3072)
        act_t = place("act_t", [P, 2, T], hot_at + 3072)
        assert hot_at + 5120 <= X_AT - 4 * STATS
        RING_AT = X_AT + 32768
        W_AT = RING_AT + 40960
        assert base + W_AT + 131072 <= nc.sbuf_usable_end, (base, nc.sbuf_usable_end)
        xh = place("xh", [P, KB, T], X_AT, F32R)
        xl = place("xl", [P, KB, T], X_AT + 16384, F32R)
        raw = place("raw", [P, 4, PIECE], RING_AT)
        hi = place("hi", [P, 4, PIECE], RING_AT + 16384, F32R)
        lo = place("lo", [P, 2, PIECE], RING_AT + 32768, F32R)
        hx = place("hx", [P, TT, D], W_AT)
        xn = place("xn", [P, TT, D], W_AT + 16384)
        Z_AT = W_AT + 40960

        def con(name, *dims):
            o, w = CONS[name]
            return cons_sb[:, o:o + w]

        def col(name, i, n=1):
            o, _ = COLS[name]
            return cols_sb[:, o + i:o + i + n]

        ident, ones, iota = con("ident"), con("ones"), con("iota")

        def st(i, n=1):
            return small[:, i:i + n]

        ps = ctx.enter_context(nc.psum_tensor("ps", [P, 8, 512], F32))

        loaded = [sem(f"loaded{k}") for k in range(4)]
        hi_done, unit_used = sem("hi_done"), sem("unit_used")
        lo_done = [sem(f"lo_done{k}") for k in range(4)]
        free_d, free_a = sem("free_d"), sem("free_a")
        x_hi, x_lo = sem("x_hi"), sem("x_lo")
        dch, ach = sem("dve_chain"), sem("act_chain")
        got_const, got_x, got_wg, got_bias, got_gain = (sem(n) for n in (
            "got_const", "got_x", "got_gate_weights", "got_bias", "got_gain"))
        got_ple, got_in2 = sem("got_ple"), sem("got_in2")
        spilled, got_h = sem("spilled"), sem("got_h")
        h_new, ss_done, ms_done, rms_done, xn_done, tr_done = (sem(n) for n in (
            "h_new", "ss_done", "ms_done", "rms_done", "xn_done", "tr_done"))
        conv_done, gates_done, tanh_done, decay_done, z_done, sqrt_done, gelu_done = (
            sem(n) for n in ("conv_done", "gates_done", "tanh_done", "decay_done", "z_done",
                             "sqrt_done", "gelu_done"))
        soft_e, soft_c = sem("soft_e"), sem("soft_c")
        at_s, at_b, at_m, at_e, at_p, at_t, at_c, at_o, at_f = (sem(n) for n in (
            "scores_done", "bias_added", "max_done", "exp_done", "probs_ready", "probs_turned",
            "probs_copied", "heads_done", "heads_copied"))
        mo_sq, mo_sum, mo_ms, mo_rt, mo_ready = (sem(n) for n in (
            "mo_sq", "mo_sum", "mo_ms", "mo_rt", "mo_ready"))
        sq_done, act_post, silu_done, prod_done = (sem(n) for n in (
            "sq_done", "act_post", "silu_done", "prod_done"))
        sig_done, ple_done, ple_free = sem("sig_done"), sem("ple_done"), sem("ple_free")
        hid_hi = sem("hid_hi")
        out_stored = sem("out_stored")
        g_pe, g_dve, g_act = sem("gla_pe"), sem("gla_dve"), sem("gla_act")
        qk_squared, qk_reduced, qk_ms, qk_rt, qk_ready, qk_turned, q_copied, k_copied = (
            sem(n) for n in ("qk_squared", "qk_reduced", "qk_ms", "qk_rt", "qk_ready",
                             "qk_turned", "q_copied", "k_copied"))
        got_dil, got_keys = sem("got_dil"), sem("got_keys")
        key_scores, route_m, route_e, route_ready, route_turned, routed = (
            sem(n) for n in ("key_scores", "route_m", "route_e", "route_ready", "route_turned",
                             "routed"))
        hot_done, gmat_done, gmat_copied = sem("hot_done"), sem("gmat_done"), sem("gmat_copied")
        gelu2_done, gated_done, hh_done, hl_done, up_done = (sem(n) for n in (
            "gelu2_done", "gated_done", "hh_done", "hl_done", "up_done"))
        fin_done = sem("fin_done")

        block = ctx.enter_context(nc.Block())

        XRW = 260
        xr = place("xr", [P, 8, XRW], Z_AT)
        t_z0 = place("t_z0", [P, 8, T], Z_AT)
        xc = place("xc", [P, 8, T], Z_AT + 8320)
        q_t = place("q_t", [P, 8, T], Z_AT + 8320 + 8192)
        k_t = place("k_t", [P, 8, T], Z_AT + 8320 + 2 * 8192)
        v_n = place("v_n", [P, TT, 1024], Z_AT + 8320 + 3 * 8192)
        yg = place("yg", [P, 8, T], Z_AT + 8320 + 4 * 8192)
        th_a = place("th_a", [P, 2, 8, T], Z_AT + 8320 + 5 * 8192)
        th_i = place("th_i", [P, 2, 8, T], Z_AT + 8320 + 7 * 8192)
        band_sb = place("band_sb", [P, 64], Z_AT + 8320 + 9 * 8192)
        mo_r = place("mo_r", [P, 2, T], Z_AT + 8320 + 9 * 8192 + 256)
        wg = place("wg", [P, 32, P], W_AT + 16384)
        bias = place("bias", [P, HEADS1, TT, T], W_AT + 16384)
        t_z1 = place("t_z1", [P, 8, T], W_AT + 32768)
        attn_t = place("attn_t", [P, 8, T], W_AT + 32768)
        A1 = Z_AT + 8320 + 5 * 8192
        at1 = [place(f"at1_{i}", [P, 2, TT, T], A1 + 4096 * i) for i in range(3)]
        y = place("y", [P, TT, D], W_AT + 16384)
        gbc = place("gbc", [P, D], W_AT + 32768)
        sil = place("sil", [P, 2, T], W_AT + 16384)
        prod = place("prod", [P, 2, T], W_AT + 16384 + 2048)
        hid_h = place("hid_h", [P, FB, T], Z_AT, F32R)
        hid_l = place("hid_l", [P, FB, T], Z_AT + FB * T * 4, F32R)
        w_pr = place("w_pr", [P, 2, D], Z_AT)
        p_sb = place("p_sb", [P, 2, T], Z_AT + 16384)
        sig = place("sig", [P, 2, TT, NCH], Z_AT + 18432)
        pz = place("pz", [P, TT, NCH], Z_AT + 26624)
        junk = place("junk", [P, NCH], Z_AT + 30720)
        SS, MS, RT, RI = 0, 2, 4, 6
        SSP = 8
        NM, SM, SI = 16, 24, 32
        LAMW = 40
        CSP = 104
        SSQ = 136
        SRT = 184
        GDEC = 232
        GSS = 248
        GRT = 256
        BA2 = 264
        GH = 296

        qn, kn, vn = (place(n, [P, TT, HEADS2 * HD], Z_AT + 12288 * k)
                      for k, n in enumerate(("qn", "kn", "vn")))
        qk_n = (qn, kn)
        GZ = Z_AT + 36864
        qa_t = place("qa_t", [P, 2, T], GZ)
        ka_t = place("ka_t", [P, 2, T], GZ + 2048)
        va = place("va", [P, TT, GLA_W], GZ + 4096)
        sra = place("sra", [P, TT, GLA_W], GZ + 8192)
        g1, g2, g3, g4 = (place(f"g{k + 1}", [P, 4, T], GZ + 12288 + 4096 * k) for k in range(4))
        kst = place("kst", [P, TT, 4, P], GZ + 12288)
        sc_t = place("sc_t", [P, 4, 512], GZ + 28672)
        state = place("state", [P, 2, 3, 2, P], GZ + 36864)
        o_n = place("o_n", [P, TT, GLA_W], GZ + 43008)
        sqt = place("sqt", [P, TT, NCH], GZ + 47104)
        rope_t = place("rope_t", [P, 4, 12, 16], GZ + 47104)
        qkg = place("qkg", [P, 2, HD], GZ + 51200)
        wgd = place("wgd", [P, KB, 32], GZ + 28672)
        wgd_h = place("wgd_h", [P, KB, 32], GZ + 28672 + 2048, F32R)
        wgd_l = place("wgd_l", [P, KB, 32], GZ + 28672 + 4096, F32R)
        gd_n = place("gd_n", [P, TT, 32], GZ + 28672 + 6144)
        gd_t = place("gd_t", [32, T], GZ + 28672 + 6400)
        up = place("up", [32, 512], GZ + 28672 + 7424)
        q_t2 = place("q_t2", [P, HEADS2, T], W_AT + 16384)
        k_t2 = place("k_t2", [P, HEADS2, T], W_AT + 28672)
        dil_sb = place("dil_sb", [P, 2, TT, T], GZ + 12288)
        at2 = [place(f"at2_{i}", [P, 2, TT, T], GZ + 16384 + 4096 * i) for i in range(3)]
        qry_t = place("qry_t", [P, KB, T], W_AT + 16384)
        keys_t = place("keys_t", [P, KB, NKEY], W_AT + 32768)
        sc_rest = place("sc_rest", [P, 32, NKEY], Z_AT)
        cand = place("cand", [P, 16, 256], Z_AT + 16384)
        cand_rest = place("cand_rest", [P, 16, 256], Z_AT + 32768)
        pick = place("pick", [P, 256, 16], Z_AT)
        top = place("top", [P, 32, 16], Z_AT + 49152)
        top_u = place("top_u", [P, 32, 16], Z_AT + 51200, U32)
        top_i = place("top_i", [P, 32, 16], Z_AT + 53248)
        best = place("best", [P, 16, 16], Z_AT + 55296)
        pos = place("pos", [P, 16, 16], Z_AT + 56320, U32)
        pos_a = place("pos_a", [P, 16, 16], Z_AT + 57344, U32)
        pos_b = place("pos_b", [P, 16, 16], Z_AT + 58368, U32)
        pos_f = place("pos_f", [P, 2, 256], Z_AT + 59392)
        route = place("route", [P, 3, 256], Z_AT + 61440)
        RSUM = 296
        gm = place("gm", [P, NKEY, T], W_AT)
        hg_h = place("hg_h", [P, 4, T], X_AT, F32R)
        hg_l = place("hg_l", [P, 4, T], X_AT + 4096, F32R)

        class Chain:

            def __init__(self, eng, s):
                self.eng, self.s, self.n, self.reg, self.per, self.k = eng, s, 0, None, 0, 0

            def value(self):
                return self.n if self.reg is None else self.reg * self.per + (self.n + self.k)

            def inc(self, ins):
                if self.reg is None:
                    self.n += 1
                else:
                    self.k += 1
                ins.then_inc(self.s, 1)

            def wait(self):
                self.eng.wait_ge(self.s, self.value())

            def link(self, ins):
                self.inc(ins)
                self.wait()

            def enter(self, reg, per):
                self.reg, self.per, self.k = reg, per, 0

            def leave(self, times):
                assert self.k == self.per, (self.k, self.per)
                self.n += self.per * times
                self.reg = None

        def t_bank(b):
            return ps[:, b, 0:T]

        def inc_at(d, c, half):
            nth = 1 if (d, c) in ((0, 2), (1, 1)) else 0
            return ps[:, 4 + c % 2 + 2 * nth, half * T:(half + 1) * T]

        def tr_slot(s):
            return ps[:, 4 + s % 4, (s // 4) * T:(s // 4) * T + T]

        @block.sync
        def _(sp):
            for k in range(4):
                sp.dma_start(raw[:, k, :], stream[k]).then_inc(loaded[k], 16)
            with sp.Fori(1, ROUNDS) as i:
                for k in range(4):
                    sp.wait_ge(lo_done[k], i)
                    sp.dma_start(raw[:, k, :], stream[bass.ds(i * 4 + k, 1)].rearrange(
                        "a p n -> p (a n)")).then_inc(loaded[k], 16)
            for b in range(8):
                sp.wait_ge(fin_done, b + 1)
                tt, c = b // 4, b % 4
                sp.dma_start(out[tt * P:(tt + 1) * P, c * NCH:(c + 1) * NCH],
                             hx[:, tt, c * NCH:(c + 1) * NCH]).then_inc(out_stored, 16)
            sp.wait_ge(out_stored, 16 * 8)

        @block.gpsimd
        def _(pool):
            def take_lo(i, k, first):
                pool.wait_ge(hi_done, i * 4 + (k + 1))
                if not (first and k < 2):
                    pool.wait_ge(unit_used, i * 4 + (k - 1))
                nc.gpsimd.tensor_tensor(lo[:, k % 2, :], raw[:, k, :], hi[:, k, :].bitcast(F32),
                                        ALU.subtract).then_inc(lo_done[k], 1)

            for k in range(4):
                take_lo(0, k, True)
            with pool.Fori(1, ROUNDS) as i:
                for k in range(4):
                    take_lo(i, k, False)

        @block.scalar
        def _(act):
            chain = Chain(act, ach)
            act.dma_start(cons_sb[:], cons).then_inc(got_const, 16)
            act.dma_start(cols_sb[:], cols).then_inc(got_const, 16)
            for tt in range(TT):
                act.dma_start(hx[:, tt, :], x[tt * P:(tt + 1) * P, :]).then_inc(got_x, 16)

            def take_hi(i, k, first=False):
                act.wait_ge(loaded[k], i * 16 + 16)
                if not first:
                    act.wait_ge(unit_used, i * 4 + (k - 3))
                nc.scalar.activation(hi[:, k, :], raw[:, k, :], ACT.Copy).then_inc(hi_done, 1)

            def norm(n, gain, partial=False):
                for tt in range(TT):
                    if n == 0:
                        if tt == 0:
                            act.wait_ge(got_x, 16 * TT)
                    else:
                        act.wait_ge(h_new, 2 * (n - 1) + tt + 1)
                    nc.scalar.activation(xn[:, tt, :], hx[:, tt, :], ACT.Square,
                                         accum_out=st(SS + tt)).then_inc(ss_done, 1)
                act.wait_ge(ms_done, n + 1)
                nc.scalar.activation(st(RT, 2), st(MS, 2), ACT.Sqrt).then_inc(rms_done, 1)
                for kb in range(KB):
                    act.wait_ge(tr_done, 16 * n + kb + 1)
                    nc.scalar.activation(xh[:, kb, :], tr_slot(kb % 8), ACT.Copy,
                                         scale=col(gain, kb)).then_inc(x_hi, 1)

            act.wait_ge(got_const, 32)
            lam = col("lam", 0, 16)
            chain.link(nc.scalar.activation(st(LAMW, 16), lam, ACT.Abs))
            nc.scalar.activation(st(LAMW, 16), st(LAMW, 16), ACT.Exp, scale=-1.0).then_inc(soft_e, 1)
            for k in range(4):
                take_hi(0, k, True)
            norm(0, "g_mix")
            act.wait_ge(tr_done, 16)
            act.dma_start(wg[:], w_gates).then_inc(got_wg, 16)
            act.dma_start(band_sb[:], band).then_inc(got_wg, 16)

            def tanh_group(g, n):
                z, which = g // 2, g % 2
                if n == 0:
                    act.wait_ge(gates_done, g + 1)
                    if g == 0:
                        act.wait_ge(soft_c, 1)
                to = (th_a, th_i)[which][:, z, n, :]
                nc.scalar.activation(to, ps[:, 4 + n // 2, (n % 2) * T:(n % 2) * T + T], ACT.Tanh,
                                     scale=0.5, bias=st(BA2 + 16 * which + 8 * z + n))\
                    .then_inc(tanh_done, 1)

            def decay(z, n):
                c, t = 8 * z + n, (t_z0, t_z1)[z]
                if n == 0:
                    act.wait_ge(tanh_done, 16 * z + 8)
                    act.wait_ge(conv_done, 8)
                nc.scalar.activation(t[:, n, :], th_a[:, z, n, :], ACT.Tanh, scale=st(CSP + c),
                                     bias=st(CSP + c)).then_inc(ach, 1)
                chain.n += 1
                chain.wait()
                nc.scalar.activation(th_a[:, z, n, :], th_a[:, z, n, :], ACT.Exp,
                                     scale=st(CSP + 16 + c), bias=st(CSP + 16 + c))\
                    .then_inc(decay_done, 1)

            def root(z):
                t = (t_z0, t_z1)[z]
                act.wait_ge(z_done, z + 1)
                nc.scalar.activation(t[:], t[:], ACT.Sqrt).then_inc(sqrt_done, 1)

            def gelu(b):
                act.wait_ge(unit_used, after("in1", 66 + 2 * b))
                nc.scalar.activation(yg[:, b, :], t_bank(b % 4), ACT.Gelu_apprx_tanh)\
                    .then_inc(free_a, 1)

            tasks = {}
            for g, u0 in enumerate((27, 35, 43, 51)):
                for n in range(8):
                    tasks.setdefault(u0 + n // 2, []).append((tanh_group, g, n))
            for z, u0 in enumerate((39, 55)):
                for n in range(8):
                    tasks.setdefault(u0 + n // 2, []).append((decay, z, n))
            tasks.setdefault(66, []).extend([(root, 0), (root, 1)])
            for b in range(8):
                tasks.setdefault(2 * b + 69, []).append((gelu, b))
            for u in range(4, 80):
                take_hi(u // 4, u % 4)
                for f, *a in tasks.pop(u, []):
                    f(*a)
            for u in sorted(tasks):
                for f, *a in tasks[u]:
                    f(*a)
            act.wait_ge(gates_done, 4)
            act.dma_start(bias[:], rpb).then_inc(got_bias, 16)

            def attend(n0, heads, slots, times):
                s_sb, p_sb_, pt = slots

                def exps(h):
                    n = n0 + h
                    act.wait_ge(at_m, n + 1)
                    for qt in range(TT):
                        if times is None:
                            ins = nc.scalar.activation(
                                p_sb_[:, h % 2, qt, :], s_sb[:, h % 2, qt, :], ACT.Exp,
                                bias=st(NM + 2 * (h % 4) + qt),
                                accum_out=st(SM + 2 * (h % 4) + qt))
                        else:
                            ins = nc.scalar.activation(
                                p_sb_[:, h % 2, qt, :], s_sb[:, h % 2, qt, :], ACT.Exp,
                                bias=st(NM + 2 * (h % 4) + qt))
                    ins.then_inc(at_e, 1)

                def copy_turned(h):
                    n = n0 + h
                    act.wait_ge(at_t, n + 1)
                    if h >= 2:
                        act.wait_ge(at_o, n - 1)
                    nc.scalar.activation(pt[:, h % 2, :, :],
                                         ps[:, 6, :].rearrange("p (a b) -> p a b", a=2),
                                         ACT.Copy).then_inc(at_c, 1)
                    if times is not None:
                        act.wait_ge(at_o, n + 1)
                        nc.scalar.activation(xh[:, 4 + h, :], ps[:, 7, 0:T], ACT.Copy)\
                            .then_inc(x_hi, 1)

                exps(0)
                for h in range(heads):
                    if h + 1 < heads:
                        exps(h + 1)
                    copy_turned(h)

            attend(0, HEADS1, at1, None)
            for branch in range(2):
                act.wait_ge(mo_ms, branch + 1)
                nc.scalar.activation(mo_r[:, branch, :], mo_r[:, branch, :], ACT.Sqrt)\
                    .then_inc(mo_rt, 1)
            for kb in range(KB):
                act.wait_ge(mo_ready, 1 + kb // 8)
                src = attn_t[:, kb, :] if kb < 8 else xc[:, kb - 8, :]
                nc.scalar.activation(xh[:, kb, :], src, ACT.Copy, scale=col("g_mo", kb))\
                    .then_inc(x_hi, 1)
            act.wait_ge(x_lo, 32)
            act.dma_start(gbc[:], gains[0]).then_inc(got_gain, 16)

            def post_squares(name, n):
                per = 22 if name == "down" else 8
                a0 = {"out1": 8, "down": 56}[name]

                def squares(where):
                    pair = where % 2
                    act.wait_ge(unit_used, after(name, per * (where + 1)))
                    if where >= 2:
                        act.wait_ge(free_a, a0 + where - 1)
                    for tt in range(TT):
                        ins = nc.scalar.activation(ps[:, 4 + 2 * pair + tt, :],
                                                   ps[:, 2 * pair + tt, :],
                                                   ACT.Square, accum_out=st(SSP + 4 * tt + where))
                    ins.then_inc(free_a, 1)
                return squares

            squares = post_squares("out1", 0)
            r0 = ROUND0["out1"]
            for c in range(4):
                for k in range(4):
                    take_hi(r0 + 2 * c, k)
                if c:
                    squares(c - 1)
                for k in range(4):
                    take_hi(r0 + 2 * c + 1, k)
            squares(3)

            def post_root(n):
                act.wait_ge(act_post, 2 * n + 1)
                nc.scalar.activation(st(RT, 2), st(MS, 2), ACT.Sqrt).then_inc(act_post, 1)

            post_root(0)
            norm(1, "g_ffn")

            r0 = ROUND0["ffn"]

            def silu(f, s):
                act.wait_ge(unit_used, f * 4 + after("ffn", 2))
                act.wait_ge(prod_done, f - 1) if not isinstance(f, int) or f >= 2 else None
                nc.scalar.activation(sil[:, s, :], t_bank(2 * s), ACT.Silu).then_inc(free_a, 1)

            def ffn_pair(f0, r, first=False, last=False):
                for k in range(4):
                    take_hi(r, k)
                if not first:
                    silu(f0 - 1, 1)
                for k in range(4):
                    take_hi(r + 1, k)
                silu(f0, 0)
                if last:
                    silu(f0 + 1, 1)

            ffn_pair(0, r0, first=True)
            with act.Fori(1, FB // 2 - 1) as i:
                ffn_pair(i * 2, i * 2 + r0)
            ffn_pair(FB - 2, r0 + FB - 2, last=True)
            act.dma_start(gbc[:], gains[1]).then_inc(got_gain, 16)
            squares = post_squares("down", 1)
            r0 = ROUND0["down"]
            for c in range(4):
                with act.Fori(0, 5) as i:
                    for k in range(4):
                        q = 22 * c + k
                        take_hi(i + (r0 + q // 4), q % 4)
                for u in range(22 * c + 20, 22 * c + 22):
                    take_hi(r0 + u // 4, u % 4)
                if c:
                    squares(c - 1)
            squares(3)
            act.dma_start(w_pr[:], w_proj).then_inc(got_ple, 16)
            act.dma_start(p_sb[:], p_t).then_inc(got_ple, 16)
            act.dma_start(wgd[:], w_gd).then_inc(got_in2, 16)
            act.dma_start(up[:], up_fb).then_inc(got_in2, 16)
            act.dma_start(qkg[:], qk_gain).then_inc(got_in2, 16)
            post_root(1)
            norm(2, "g_ple")
            act.wait_ge(h_new, 4)
            act.dma_start(gbc[:], gains[2]).then_inc(got_gain, 16)
            r0 = ROUND0["gate"]

            def sigmoids(c):
                act.wait_ge(unit_used, after("gate", 8 * c + 8))
                if c >= 2:
                    act.wait_ge(ple_free, c - 1)
                for tt in range(TT):
                    ins = nc.scalar.activation(sig[:, c % 2, tt, :], ps[:, 2 * (c % 2) + tt, :],
                                               ACT.Sigmoid)
                ins.then_inc(free_a, 1)

            for c in range(4):
                for k in range(4):
                    take_hi(r0 + 2 * c, k)
                if c:
                    sigmoids(c - 1)
                for k in range(4):
                    take_hi(r0 + 2 * c + 1, k)
            sigmoids(3)
            post_root(2)
            norm(3, "g_n1")

            def log_sigmoid_parts():
                act.wait_ge(g_pe, 3)
                for m in range(4):
                    ins = nc.scalar.activation(g1[:, m, :], tr_slot(4 + m), ACT.Abs,
                                               bias=col("gla_b", m))
                chain.link(ins)
                chain.link(nc.scalar.activation(g1[:], g1[:], ACT.Exp, scale=-1.0))
                nc.scalar.activation(g1[:], g1[:], ACT.Ln, bias=1.0).then_inc(g_act, 1)

            def last_of(d):
                v = g1[:, 2 * d:2 * d + 2, :].rearrange("p m (c t) -> p m c t", t=64)
                return v[:, :, :, 63 if d == 0 else 0]

            def decays():
                act.wait_ge(g_dve, 4)
                nc.scalar.activation(g2[:], g1[:], ACT.Exp, scale=1.0 / 16)
                nc.scalar.activation(g3[:], g1[:], ACT.Exp, scale=-1.0 / 16)
                for d in range(2):
                    nc.scalar.activation(st(GDEC + 8 * d, 8).rearrange("p (m c) -> p m c", c=4),
                                         last_of(d), ACT.Exp, scale=1.0 / 16)
                nc.scalar.activation(g4[:], g4[:], ACT.Exp, scale=1.0 / 16).then_inc(g_act, 1)

            def silu_r():
                act.wait_ge(unit_used, after("in2", 24))
                for tt in range(TT):
                    ins = nc.scalar.activation(sra[:, tt, :], ps[:, 2 + tt, :], ACT.Silu)
                ins.then_inc(free_a, 1)

            def qk_squares(c):
                act.wait_ge(unit_used, after("in2", 32 + 8 * c))
                if c:
                    act.wait_ge(qk_reduced, c)
                if c == 4:
                    act.wait_ge(qk_ready, 1)
                for tt in range(TT):
                    ins = nc.scalar.activation(sqt[:, tt, :], ps[:, 2 * (c % 2) + tt, :],
                                               ACT.Square)
                ins.then_inc(free_a, 1)

            def qk_root(which):
                act.wait_ge(qk_ms, which + 1)
                nc.scalar.activation(st(SRT, 24), st(SRT, 24), ACT.Sqrt).then_inc(qk_rt, 1)

            def o_squares():
                act.wait_ge(g_dve, 10)
                nc.scalar.activation(g3[:], o_n[:].rearrange("p a (b c) -> p (a b) c", c=T),
                                     ACT.Square).then_inc(g_act, 1)

            def o_root():
                act.wait_ge(g_dve, 11)
                nc.scalar.activation(st(GRT, 8), st(GRT, 8), ACT.Sqrt).then_inc(g_act, 1)

            def q_copy(h):
                act.wait_ge(qk_turned, h + 1)
                nc.scalar.activation(q_t2[:, h, :], tr_slot(h % 8), ACT.Copy).then_inc(q_copied, 1)

            act.wait_ge(got_in2, 48)
            nc.scalar.activation(wgd_h[:], wgd[:], ACT.Copy).then_inc(g_act, 1)
            tasks = {11: [(log_sigmoid_parts,)], 15: [(decays,)], 27: [(silu_r,)],
                     61: [(qk_root, 0)], 69: [(o_squares,)], 72: [(o_root,)], 83: [(qk_root, 1)]}
            for c in range(6):
                tasks[35 + 8 * c] = [(qk_squares, c)]
            for h in range(HEADS2):
                tasks[75].append((q_copy, h))
            for u in range(96):
                take_hi(ROUND0["in2"] + u // 4, u % 4)
                for f, *a in tasks.get(u, []):
                    f(*a)
            act.wait_ge(g_pe, 8)
            act.dma_start(dil_sb[:], dil).then_inc(got_dil, 16)
            for kb in range(4):
                act.wait_ge(g_pe, 9 + kb)
                nc.scalar.activation(xh[:, kb, :], tr_slot(kb), ACT.Copy, scale=col("g_gla", kb))\
                    .then_inc(x_hi, 1)
            attend(HEADS1, HEADS2, at2, dil_sb)
            act.dma_start(keys_t[:], sub_keys).then_inc(got_keys, 16)
            with act.Fori(0, 8) as i:
                for k in range(4):
                    take_hi(i + ROUND0["out2"], k)
            norm(4, "g_n2")
            act.dma_start(spill, hx[:]).then_inc(spilled, 16)
            with act.Fori(0, 8) as i:
                for k in range(4):
                    take_hi(i + ROUND0["query"], k)
            act.wait_ge(route_m, 1)
            nc.scalar.activation(route[:, 2, :], route[:, 2, :], ACT.Exp).then_inc(route_e, 1)
            act.wait_ge(spilled, 16)
            act.wait_ge(routed, 1)
            with act.Fori(0, T // 16) as i:
                for b in range(4):
                    act.wait_ge(gmat_done, i * 16 + (4 * b + 4))
                    nc.scalar.activation(
                        gm[:, :, bass.ds(i * 16 + 4 * b, 4)].rearrange("p j t -> p t j"),
                        ps[:, 4 + b, :].rearrange("p (t j) -> p t j", j=NKEY), ACT.Copy)\
                        .then_inc(gmat_copied, 1)
            act.wait_ge(gmat_copied, T // 4)
            act.wait_ge(hot_done, T)

            def expert_gelu(j, s, bank, first=False):
                act.wait_ge(unit_used, j * 2 + after("peer_down", 2))
                if not first:
                    act.wait_ge(gated_done, j - 1)
                nc.scalar.activation(act_t[:, s, :], t_bank(bank), ACT.Gelu_apprx_tanh)\
                    .then_inc(free_a, 1)

            r0 = ROUND0["peer_down"]

            def gelu_rounds(j0, r, first=False):
                for half in range(2):
                    for k in range(2):
                        take_hi(r + half, k)
                    if not (first and half == 0):
                        expert_gelu(j0 + 2 * half - 1, 1, (2 * half - 1) % 4, first and half == 1)
                    for k in range(2, 4):
                        take_hi(r + half, k)
                    expert_gelu(j0 + 2 * half, 0, 2 * half, first and half == 0)

            gelu_rounds(0, r0, True)
            with act.Fori(1, 32) as i:
                gelu_rounds(i * 4, i * 2 + r0)
            expert_gelu(127, 1, 3)
            r0 = ROUND0["peer_up"]

            def hidden_hi(j, s, first=False):
                if not first:
                    act.wait_ge(unit_used, j * 2 + after("peer_up", -6))
                nc.scalar.activation(hg_h[:, s, :], gm[:, bass.ds(j, 1), :].rearrange(
                    "p a t -> p (a t)") if not isinstance(j, int) else gm[:, j, :], ACT.Copy)\
                    .then_inc(hh_done, 1)

            act.wait_ge(unit_used, after("peer_up", 0))
            act.wait_ge(gated_done, 128)

            def up_rounds(j0, r, first=False):
                for half in range(2):
                    for k in range(4):
                        if k % 2 == 0:
                            s = 2 * half + k // 2
                            hidden_hi(j0 + s, s, first)
                        take_hi(r + half, k)

            up_rounds(0, r0, True)
            with act.Fori(1, 30) as i:
                up_rounds(i * 4, i * 2 + r0)
            act.wait_ge(hl_done, 100)
            act.dma_start(hx[:], spill).then_inc(got_h, 16)
            with act.Fori(30, 32) as i:
                up_rounds(i * 4, i * 2 + r0)

        @block.vector
        def _(dve):
            chain = Chain(dve, dch)
            link = chain.link
            V = nc.vector

            def norm(n, gain):
                dve.wait_ge(ss_done, 2 * n + 2)
                V.tensor_scalar(st(MS, 2), st(SS, 2), 1.0 / D, EPS, ALU.mult, ALU.add)\
                    .then_inc(ms_done, 1)
                dve.wait_ge(rms_done, n + 1)
                link(V.reciprocal(st(RI, 2), st(RT, 2)))
                for tt in range(TT):
                    V.tensor_scalar(xn[:, tt, :], hx[:, tt, :], st(RI + tt), None, ALU.mult)\
                        .then_inc(xn_done, 1)
                for kb in range(KB):
                    dve.wait_ge(x_hi, 16 * BUILD[n] + kb + 1)
                    V.scalar_tensor_tensor(out=xl[:, kb, :], in0=tr_slot(kb % 8),
                                           scalar=col(gain, kb), in1=xh[:, kb, :].bitcast(F32),
                                           op0=ALU.mult, op1=ALU.subtract).then_inc(x_lo, 1)

            BUILD = [0, 2, 3, 4, 6]

            V.memset(xr[:, :, 0:2], 0.0).then_inc(dch, 1)
            V.memset(xr[:, :, 258:260], 0.0).then_inc(dch, 1)
            chain.n += 2
            dve.wait_ge(got_const, 32)
            dve.wait_ge(soft_e, 1)
            e, s, s2, acc = (st(LAMW + 16 * i, 16) for i in range(4))
            link(V.tensor_scalar(s, e, 2.0, None, ALU.add))
            link(V.reciprocal(s, s))
            link(V.tensor_tensor(s, s, e, ALU.mult))
            link(V.tensor_tensor(s2, s, s, ALU.mult))
            link(V.tensor_scalar(acc, s2, 2.0 / 15, 2.0 / 13, ALU.mult, ALU.add))
            for odd in (11, 9, 7, 5, 3, 1):
                link(V.tensor_tensor(acc, acc, s2, ALU.mult))
                link(V.tensor_scalar(acc, acc, 2.0 / odd, None, ALU.add))
            link(V.tensor_tensor(acc, acc, s, ALU.mult))
            link(V.tensor_scalar(s, col("lam", 0, 16), -1.0, 0.0, ALU.mult, ALU.max))
            link(V.tensor_tensor(acc, acc, s, ALU.add))
            V.tensor_scalar(st(CSP, 16), acc, 4.0, None, ALU.mult).then_inc(dch, 1)
            V.tensor_scalar(st(CSP + 16, 16), acc, -4.0, None, ALU.mult).then_inc(dch, 1)
            V.tensor_scalar(st(BA2, 32), col("b_a", 0, 32), 0.5, None, ALU.mult).then_inc(dch, 1)
            chain.n += 3
            chain.wait()
            V.memset(st(LAMW), 0.0).then_inc(soft_c, 1)

            norm(0, "g_mix")

            def block_copy(b, to, scale=None):
                dve.wait_ge(unit_used, after("in1", 2 * b + 2))
                if scale is None:
                    ins = V.tensor_copy(to, t_bank(b % 4))
                else:
                    ins = V.tensor_scalar(to, t_bank(b % 4), scale, None, ALU.mult)
                ins.then_inc(free_d, 1)
                return ins

            for n in range(8):
                block_copy(n, xr[:, n, 2:258])
                dve.wait_ge(free_d, n + 1)
                link(V.tensor_scalar(xc[:, n, :], xr[:, n, 0:T], col("conv_w", n),
                                     col("conv_b", n), ALU.mult, ALU.add))
                for j in range(1, 4):
                    ins = V.scalar_tensor_tensor(out=xc[:, n, :], in0=xr[:, n, j:j + T],
                                                 scalar=col("conv_w", 8 * j + n),
                                                 in1=xc[:, n, :], op0=ALU.mult, op1=ALU.add)
                    if j < 3:
                        link(ins)
                    else:
                        ins.then_inc(conv_done, 1)
            for b in range(8):
                block_copy(8 + b, q_t[:, b, :], SCALE)
            for b in range(4):
                block_copy(16 + b, k_t[:, b, :])

            def z_step(z):
                t = (t_z0, t_z1)[z]
                dve.wait_ge(decay_done, 8 * z + 8)
                dve.wait_ge(tanh_done, 16 * z + 16)
                dve.wait_ge(conv_done, 8)
                sq = yg
                link(V.tensor_tensor(sq[:], th_a[:, z], th_a[:, z], ALU.mult))
                V.scalar_tensor_tensor(out=t[:], in0=sq[:], scalar=1.0, in1=t[:], op0=ALU.add,
                                       op1=ALU.mult).then_inc(z_done, 1)
                link(V.scalar_tensor_tensor(out=th_i[:, z], in0=th_i[:, z], scalar=1.0, in1=xc[:],
                                            op0=ALU.add, op1=ALU.mult))
                dve.wait_ge(z_done, z + 1)

            z_step(0)
            for b in range(4, 8):
                block_copy(16 + b, k_t[:, b, :])

            def v_copy(c):
                dve.wait_ge(unit_used, after("in1", 56 + 8 * c))
                for tt in range(TT):
                    ins = V.tensor_copy(v_n[:, tt, c * NCH:(c + 1) * NCH], ps[:, 2 * c + tt, :])
                ins.then_inc(free_d, 1)

            v_copy(0)
            z_step(1)
            v_copy(1)
            for z in range(2):
                t = (t_z0, t_z1)[z]
                dve.wait_ge(sqrt_done, z + 1)
                link(V.scalar_tensor_tensor(out=t[:], in0=t[:], scalar=0.5, in1=th_i[:, z],
                                            op0=ALU.mult, op1=ALU.mult))
                for n in range(8):
                    if z == 0:
                        a, b, o = th_a[:, z, n, :], t[:, n, :], th_i[:, z, n, :]
                    else:
                        a, b, o = (m[:, n, ::-1] for m in (th_a[:, z], t, th_i[:, z]))
                    chain.inc(V.tensor_tensor_scan(o, a, b, 0.0, ALU.mult, ALU.add))
            chain.wait()
            link(V.tensor_tensor(th_i[:, 0], th_i[:, 0], th_i[:, 1], ALU.add))
            dve.wait_ge(free_a, 8)
            link(V.tensor_tensor(xc[:], th_i[:, 0], yg[:], ALU.mult))
            V.tensor_tensor(th_i[:, 1], xc[:], xc[:], ALU.mult).then_inc(mo_sq, 1)
            dve.wait_ge(got_bias, 16)
            dve.wait_ge(got_wg, 32)
            for h in range(HEADS1):
                chain.inc(V.tensor_tensor(
                    bias[:, h].rearrange("p a (r c) -> p (a r) c", c=64),
                    bias[:, h].rearrange("p a (r c) -> p (a r) c", c=64),
                    band_sb[:].unsqueeze(1).to_broadcast([P, 8, 64]), ALU.add))

            def attend(n0, heads, slots, bias_of, times, copy_out):
                s_sb, p_sb_, pt = slots

                def first(h):
                    n = n0 + h
                    dve.wait_ge(at_s, n + 1)
                    if h >= 2:
                        dve.wait_ge(at_e, n - 1)
                    V.tensor_tensor(s_sb[:, h % 2], ps[:, 4 + h % 2, :].rearrange(
                        "p (a b) -> p a b", a=2), bias_of(h), ALU.add).then_inc(at_b, 1)
                    dve.wait_ge(at_b, n + 1)
                    V.tensor_reduce(st(NM + 2 * (h % 4), 2), s_sb[:, h % 2], AX.X, ALU.max,
                                    negate=True).then_inc(at_m, 1)

                def second(h):
                    n = n0 + h
                    dve.wait_ge(at_e, n + 1)
                    sm, si = SM + 2 * (h % 4), SI + 2 * (h % 4)
                    if times is not None:
                        for qt in range(TT):
                            chain.inc(V.scalar_tensor_tensor(
                                out=p_sb_[:, h % 2, qt], in0=p_sb_[:, h % 2, qt], scalar=1.0,
                                in1=times[:, qt], op0=ALU.mult, op1=ALU.mult,
                                accum_out=st(sm + qt)))
                        chain.wait()
                    link(V.reciprocal(st(si, 2), st(sm, 2)))
                    for qt in range(TT):
                        ins = V.tensor_scalar(p_sb_[:, h % 2, qt], p_sb_[:, h % 2, qt],
                                              st(si + qt), None, ALU.mult)
                        if qt == 0:
                            chain.inc(ins)
                    ins.then_inc(at_p, 1)

                first(0)
                for h in range(heads):
                    if h + 1 < heads:
                        first(h + 1)
                    second(h)
                    if h:
                        copy_out(h - 1)
                copy_out(heads - 1)

            def head_out(h):
                dve.wait_ge(at_o, h + 1)
                V.tensor_copy(attn_t[:, h, :], ps[:, 7, 0:T]).then_inc(at_f, 1)

            chain.wait()
            attend(0, HEADS1, at1, lambda h: bias[:, h], None, head_out)
            dve.wait_ge(at_f, HEADS1)
            dve.wait_ge(at_o, HEADS1)
            sqa = th_a[:, 1]
            V.tensor_tensor(sqa, attn_t[:], attn_t[:], ALU.mult).then_inc(mo_sq, 1)
            for branch in range(2):
                dve.wait_ge(mo_sum, branch + 1)
                V.tensor_scalar(mo_r[:, branch, :], ps[:, 4 + branch, 0:T], 1.0 / 1024, EPS,
                                ALU.mult, ALU.add).then_inc(mo_ms, 1)
            for branch in (1, 0):
                dve.wait_ge(mo_rt, branch + 1)
                link(V.reciprocal(mo_r[:, branch, :], mo_r[:, branch, :]))
                m = (xc, attn_t)[branch]
                V.tensor_tensor(m[:], m[:], mo_r[:, branch, :].unsqueeze(1).to_broadcast([P, 8, T]),
                                ALU.mult).then_inc(mo_ready, 1)
            for kb in range(KB):
                dve.wait_ge(x_hi, 16 + kb + 1)
                src = attn_t[:, kb, :] if kb < 8 else xc[:, kb - 8, :]
                V.scalar_tensor_tensor(out=xl[:, kb, :], in0=src, scalar=col("g_mo", kb),
                                       in1=xh[:, kb, :].bitcast(F32), op0=ALU.mult,
                                       op1=ALU.subtract).then_inc(x_lo, 1)

            def post_chunks(name, n):
                dve.wait_ge(got_gain, 16 * (n + 1))
                for c in range(4):
                    dve.wait_ge(free_a, {"out1": 8, "down": 56}[name] + c + 1)
                    for tt in range(TT):
                        ins = V.tensor_tensor(y[:, tt, c * NCH:(c + 1) * NCH],
                                              ps[:, 2 * (c % 2) + tt, :],
                                              gbc[:, c * NCH:(c + 1) * NCH], ALU.mult)
                        if tt == 0:
                            chain.inc(ins)
                    ins.then_inc(free_d, 1)
                chain.wait()

            def post(n, frees):
                dve.wait_ge(free_d, frees)
                link(V.tensor_reduce(st(SS, 2), st(SSP, 8).rearrange("p (a b) -> p a b", a=2),
                                     AX.X, ALU.add))
                V.tensor_scalar(st(MS, 2), st(SS, 2), 1.0 / D, EPS, ALU.mult, ALU.add)\
                    .then_inc(act_post, 1)
                dve.wait_ge(act_post, 2 * n + 2)
                link(V.reciprocal(st(RI, 2), st(RT, 2)))
                for tt in range(TT):
                    V.scalar_tensor_tensor(out=hx[:, tt], in0=y[:, tt], scalar=st(RI + tt),
                                           in1=hx[:, tt], op0=ALU.mult, op1=ALU.add)\
                        .then_inc(h_new, 1)

            post_chunks("out1", 0)
            dve.wait_ge(free_a, 12)
            post(0, 30)
            norm(1, "g_ffn")

            def hidden(f, s, first=False):
                dve.wait_ge(unit_used, f * 4 + after("ffn", 4))
                dve.wait_ge(free_a, f + 13)
                V.tensor_tensor(prod[:, s, :], t_bank(2 * s + 1), sil[:, s, :], ALU.mult)\
                    .then_inc(prod_done, 1)
                dve.wait_ge(prod_done, f + 1)
                V.tensor_copy(hid_h[:, bass.ds(f, 1), :].rearrange("p a t -> p (a t)")
                              if not isinstance(f, int) else hid_h[:, f, :], prod[:, s, :])\
                    .then_inc(hid_hi, 1)
                dve.wait_ge(hid_hi, f + 1)
                V.tensor_tensor(hid_l[:, bass.ds(f, 1), :].rearrange("p a t -> p (a t)")
                                if not isinstance(f, int) else hid_l[:, f, :], prod[:, s, :],
                                (hid_h[:, bass.ds(f, 1), :].rearrange("p a t -> p (a t)")
                                 if not isinstance(f, int) else hid_h[:, f, :]).bitcast(F32),
                                ALU.subtract).then_inc(free_d, 1)
                dve.wait_ge(free_d, f + 31)

            with dve.Fori(0, FB // 2) as i:
                for s in range(2):
                    hidden(i * 2 + s, s)
            post_chunks("down", 1)
            dve.wait_ge(free_a, 60)
            post(1, 78)
            norm(2, "g_ple")
            dve.wait_ge(got_gain, 48)
            for c in range(4):
                dve.wait_ge(free_a, 60 + c + 1)
                dve.wait_ge(ple_done, c + 1)
                for tt in range(TT):
                    chain.inc(V.tensor_tensor(pz[:, tt, :], ps[:, 4 + 2 * (c % 2) + tt, :],
                                              sig[:, c % 2, tt, :], ALU.mult))
                chain.wait()
                for tt in range(TT):
                    link(V.scalar_tensor_tensor(out=junk[:], in0=pz[:, tt, :], scalar=1.0,
                                                in1=pz[:, tt, :], op0=ALU.mult, op1=ALU.mult,
                                                accum_out=st(SSP + 4 * tt + c)))
                    link(V.tensor_tensor(y[:, tt, c * NCH:(c + 1) * NCH], pz[:, tt, :],
                                         gbc[:, c * NCH:(c + 1) * NCH], ALU.mult))
                V.memset(junk[:, 0:1], 0.0).then_inc(ple_free, 1)
                dve.wait_ge(ple_free, c + 1)
            post(2, 78)
            norm(3, "g_n1")

            dve.wait_ge(g_act, 1)
            V.tensor_tensor(wgd_l[:], wgd[:], wgd_h[:].bitcast(F32), ALU.subtract).then_inc(g_dve, 1)
            dve.wait_ge(g_pe, 1)
            V.tensor_copy(gd_n[:], ps[:, 4, 0:64].rearrange("p (a b) -> p a b", a=2))\
                .then_inc(g_dve, 1)

            def t_copy(b, to):
                dve.wait_ge(unit_used, after("in2", 2 * b + 2))
                V.tensor_copy(to, t_bank(b)).then_inc(free_d, 1)

            t_copy(0, qa_t[:, 0, :])
            t_copy(1, qa_t[:, 1, :])
            dve.wait_ge(g_pe, 2)
            V.tensor_copy(gd_t[:], ps[0:32, 5, 0:T]).then_inc(g_dve, 1)
            t_copy(2, ka_t[:, 0, :])
            t_copy(3, ka_t[:, 1, :])
            dve.wait_ge(g_act, 2)
            for m in range(4):
                chain.inc(V.tensor_scalar(g2[:, m, :], tr_slot(4 + m), col("gla_b", m), 0.0,
                                          ALU.add, ALU.min))
            chain.wait()
            link(V.tensor_tensor(g2[:], g2[:], g1[:], ALU.subtract))
            for m in range(4):
                if m < 2:
                    o, a = g1[:, m, :], g2[:, m, :]
                else:
                    o, a = g1[:, m, ::-1], g2[:, m, ::-1]
                chain.inc(V.tensor_tensor_scan(o, con("scan"), a, 0.0, ALU.mult, ALU.add))
            chain.wait()
            for d in range(2):
                v = g1[:, 2 * d:2 * d + 2, :].rearrange("p m (c t) -> p (m c) t", t=64)
                at_end = v[:, :, 63:64] if d == 0 else v[:, :, 0:1]
                ins = V.tensor_tensor(
                    g4[:, 2 * d:2 * d + 2, :].rearrange("p m (c t) -> p (m c) t", t=64),
                    at_end.to_broadcast([P, 8, 64]), v, ALU.subtract)
                if d == 0:
                    chain.inc(ins)
            ins.then_inc(g_dve, 1)

            def n_copy(n, to):
                dve.wait_ge(unit_used, after("in2", 16 + 8 * n))
                for tt in range(TT):
                    ins = V.tensor_copy(to(tt), ps[:, 2 * (n % 2) + tt, :])
                ins.then_inc(free_d, 1)

            def qk_chunk(c):
                dve.wait_ge(free_a, 66 + c)
                n_copy(2 + c, lambda tt: qk_n[c // 3][:, tt, (c % 3) * NCH:(c % 3 + 1) * NCH])

            def qk_reduce(c):
                dve.wait_ge(free_a, 66 + c)
                for tt in range(TT):
                    ins = V.tensor_reduce(st(SSQ + 24 * (c // 3) + 12 * tt + 4 * (c % 3), 4),
                                          sqt[:, tt, :].rearrange("p (h e) -> p h e", e=HD),
                                          AX.X, ALU.add)
                    if tt == 0:
                        chain.inc(ins)
                ins.then_inc(qk_reduced, 1)

            def qk_mean(which):
                dve.wait_ge(qk_reduced, 3 * which + 3)
                if which:
                    dve.wait_ge(qk_ready, 1)
                V.tensor_scalar(st(SRT, 24), st(SSQ + 24 * which, 24), 1.0 / HD, EPS, ALU.mult,
                                ALU.add).then_inc(qk_ms, 1)

            def qk_normalise(which):
                dve.wait_ge(qk_rt, which + 1)
                inv = st(SSQ + 24 * which, 24)
                link(V.reciprocal(inv, st(SRT, 24)))
                if which == 0:
                    link(V.tensor_scalar(inv, inv, SCALE, None, ALU.mult))
                full = qk_n[which][:].rearrange("p a (h e) -> p (a h) e", e=HD)
                link(V.tensor_tensor(full, full, inv.unsqueeze(2).to_broadcast([P, 24, HD]),
                                     ALU.mult))
                link(V.tensor_tensor(full, full, qkg[:, which, :].unsqueeze(1).to_broadcast(
                    [P, 24, HD]), ALU.mult))
                for tt in range(TT):
                    v = qk_n[which][:, tt, :].rearrange("p (h e) -> p h e", e=HD)
                    x1, x2 = v[:, :, 0:16], v[:, :, 16:32]
                    cos, sin = (con(n)[:, 16 * tt:16 * tt + 16].unsqueeze(1).to_broadcast(
                        [P, 12, 16]) for n in ("cos", "sin"))
                    for k, (a, b) in enumerate(((x1, cos), (x2, sin), (x2, cos), (x1, sin))):
                        chain.inc(V.tensor_tensor(rope_t[:, k], a, b, ALU.mult))
                    chain.wait()
                    chain.inc(V.tensor_tensor(x1, rope_t[:, 0], rope_t[:, 1], ALU.subtract))
                    ins = V.tensor_tensor(x2, rope_t[:, 2], rope_t[:, 3], ALU.add)
                    if tt == 0:
                        link(ins)
                ins.then_inc(qk_ready, 1)

            n_copy(0, lambda tt: va[:, tt, :])
            dve.wait_ge(g_act, 3)
            for d in range(2):
                h = slice(2 * d, 2 * d + 2)
                chain.inc(V.scalar_tensor_tensor(
                    out=g2[:, h, :], in0=g2[:, h, :], scalar=64 ** -0.5, in1=qa_t[:], op0=ALU.mult,
                    op1=ALU.mult))
                chain.inc(V.tensor_tensor(g3[:, h, :], g3[:, h, :], ka_t[:], ALU.mult))
                ins = V.tensor_tensor(g4[:, h, :], g4[:, h, :], ka_t[:], ALU.mult)
                if d == 0:
                    chain.inc(ins)
            ins.then_inc(g_dve, 1)
            qk_chunk(0)
            dve.wait_ge(g_pe, 4)
            link(V.tensor_scalar(sc_t[:], ps[:, 4:8, :], 3e38, -3e38, ALU.min, ALU.max))
            for b in range(4):
                v = sc_t[:, b, :].rearrange("p (d h q) -> p d h q", d=2, h=2)
                ins = V.tensor_tensor(v, v, con("causal").rearrange("p (d q) -> p d q", d=2)
                                      .unsqueeze(2).to_broadcast([P, 2, 2, P]), ALU.mult)
                if b < 3:
                    chain.inc(ins)
            ins.then_inc(g_dve, 1)
            qk_reduce(0)
            qk_chunk(1)
            qk_reduce(1)
            dve.wait_ge(g_pe, 5)
            V.tensor_copy(kst[:].rearrange("p a m k -> p a (m k)"), ps[:, 4:6, :]).then_inc(g_dve, 1)
            qk_chunk(2)
            qk_reduce(2)
            qk_mean(0)

            def states(d):
                dve.wait_ge(g_pe, 6 + d)
                for n in range(3):
                    c = n if d == 0 else 3 - n
                    for half in range(2):
                        at, m = inc_at(d, c, half), 2 * d + half
                        for hd in range(2):
                            rows = slice(64 * hd, 64 * hd + 64)
                            add = at[rows, hd * P:(hd + 1) * P]
                            new = state[rows, d, n, half, :]
                            if n == 0:
                                ins = V.tensor_copy(new, add)
                            else:
                                ins = V.scalar_tensor_tensor(
                                    out=new, in0=state[rows, d, n - 1, half, :],
                                    scalar=small[rows, GDEC + 4 * m + c:GDEC + 4 * m + c + 1],
                                    in1=add, op0=ALU.mult, op1=ALU.add)
                            if (n, half, hd) != (2, 1, 1):
                                chain.inc(ins)
                    if n < 2:
                        chain.wait()
                ins.then_inc(g_dve, 1)

            states(0)
            qk_chunk(3)
            qk_reduce(3)
            states(1)
            qk_normalise(0)
            qk_chunk(4)
            qk_reduce(4)
            dve.wait_ge(g_pe, 8)
            for tt in range(TT):
                ins = V.tensor_copy(
                    o_n[:, tt, :].rearrange("p (b a e) -> p a b e", a=2, b=2),
                    ps[:, 4 + 2 * tt:6 + 2 * tt, 0:T].rearrange("p a (b e) -> p a b e", b=2))
                if tt == 0:
                    chain.inc(ins)
            ins.then_inc(g_dve, 1)
            dve.wait_ge(g_act, 4)
            link(V.tensor_reduce(st(GSS, 8), g3[:].rearrange("p a (b e) -> p (a b) e", e=HD),
                                 AX.X, ALU.add))
            V.tensor_scalar(st(GRT, 8), st(GSS, 8), 1.0 / HD, EPS, ALU.mult, ALU.add)\
                .then_inc(g_dve, 1)
            qk_chunk(5)
            qk_reduce(5)
            qk_mean(1)
            dve.wait_ge(g_act, 5)
            link(V.reciprocal(st(GSS, 8), st(GRT, 8)))
            o_v = o_n[:].rearrange("p a (h e) -> p (a h) e", e=HD)
            link(V.tensor_tensor(o_v, o_v, st(GSS, 8).unsqueeze(2).to_broadcast([P, 8, HD]),
                                 ALU.mult))
            V.tensor_tensor(o_n[:], o_n[:], sra[:], ALU.mult).then_inc(g_dve, 1)
            n_copy(8, lambda tt: vn[:, tt, 0:NCH])
            qk_normalise(1)
            n_copy(9, lambda tt: vn[:, tt, NCH:2 * NCH])
            for h in range(HEADS2):
                dve.wait_ge(qk_turned, HEADS2 + h + 1)
                V.tensor_copy(k_t2[:, h, :], tr_slot((HEADS2 + h) % 8)).then_inc(k_copied, 1)
            n_copy(10, lambda tt: vn[:, tt, 2 * NCH:3 * NCH])

            for kb in range(4):
                dve.wait_ge(x_hi, 80 + kb + 1)
                V.scalar_tensor_tensor(out=xl[:, kb, :], in0=tr_slot(kb), scalar=col("g_gla", kb),
                                       in1=xh[:, kb, :].bitcast(F32), op0=ALU.mult,
                                       op1=ALU.subtract).then_inc(x_lo, 1)

            def head_out2(h):
                dve.wait_ge(x_hi, 80 + 4 + h + 1)
                V.tensor_tensor(xl[:, 4 + h, :], ps[:, 7, 0:T], xh[:, 4 + h, :].bitcast(F32),
                                ALU.subtract).then_inc(x_lo, 1)

            dve.wait_ge(got_dil, 16)
            attend(HEADS1, HEADS2, at2, lambda h: dil_sb[:, 0], dil_sb[:, 1], head_out2)
            for c in range(4):
                dve.wait_ge(unit_used, after("out2", 8 * c + 8))
                for tt in range(TT):
                    v = hx[:, tt, c * NCH:(c + 1) * NCH]
                    ins = V.tensor_tensor(v, ps[:, 2 * (c % 2) + tt, :], v, ALU.add)
                    if c == 3:
                        ins.then_inc(h_new, 1)
                if c < 3:
                    ins.then_inc(free_d, 1)
            dve.wait_ge(h_new, 8)
            norm(4, "g_n2")
            for b in range(KB):
                dve.wait_ge(unit_used, after("query", 2 * b + 2))
                V.tensor_copy(qry_t[:, b, :], t_bank(b % 4)).then_inc(free_d, 1)
            lists = [ps[:, 4 + r // 4 if r < 16 else (r - 16) // 4, (r % 4) * P:(r % 4 + 1) * P]
                     for r in range(32)]
            dve.wait_ge(key_scores, 1)
            for r in range(32):
                chain.inc(V.max(top[:, r, 0:8], lists[r]))
            chain.wait()
            for r in range(32):
                chain.inc(V.max_index(top_u[:, r, 0:8], top[:, r, 0:8], lists[r]))
                chain.inc(V.match_replace(sc_rest[:, r, :], top[:, r, 0:8], lists[r], -3e38))
            chain.wait()
            for r in range(32):
                chain.inc(V.max(top[:, r, 8:16], sc_rest[:, r, :]))
            chain.wait()
            for r in range(32):
                chain.inc(V.max_index(top_u[:, r, 8:16], top[:, r, 8:16], sc_rest[:, r, :]))
            pairs = top[:].rearrange("p (n c) k -> p n c k", c=2)
            cand_v = cand[:].rearrange("p n (a b) -> p n a b", b=16)
            link(V.tensor_tensor(cand_v, pairs[:, :, 0, :].unsqueeze(3).to_broadcast([P, 16, 16, 16]),
                                 pairs[:, :, 1, :].unsqueeze(2).to_broadcast([P, 16, 16, 16]),
                                 ALU.add))
            link(V.tensor_copy(top_i[:], top_u[:]))
            for r in range(16):
                chain.inc(V.max(best[:, r, 0:8], cand[:, r, :]))
            chain.wait()
            for r in range(16):
                chain.inc(V.max_index(pos[:, r, 0:8], best[:, r, 0:8], cand[:, r, :]))
                chain.inc(V.match_replace(cand_rest[:, r, :], best[:, r, 0:8], cand[:, r, :],
                                          -3e38))
            chain.wait()
            for r in range(16):
                chain.inc(V.max(best[:, r, 8:16], cand_rest[:, r, :]))
            chain.wait()
            for r in range(16):
                chain.inc(V.max_index(pos[:, r, 8:16], best[:, r, 8:16], cand_rest[:, r, :]))
            V.tensor_tensor(route[:, 2, :].rearrange("p (n k) -> p n k", k=16), best[:],
                            best[:, :, 0:1].to_broadcast([P, 16, 16]), ALU.subtract)\
                .then_inc(route_m, 1)
            chain.wait()
            chain.inc(V.tensor_scalar(pos_a[:], pos[:], 4, None, ALU.logical_shift_right))
            link(V.tensor_scalar(pos_b[:], pos[:], 15, None, ALU.bitwise_and))
            chain.inc(V.tensor_copy(pos_f[:, 0, :], pos_a[:].rearrange("p a b -> p (a b)")))
            link(V.tensor_copy(pos_f[:, 1, :], pos_b[:].rearrange("p a b -> p (a b)")))
            keys_i = top_i[:].rearrange("p (n c) k -> p n c k", c=2)
            for c in range(2):
                link(V.tensor_tensor(pick[:], pos_f[:, c, :].unsqueeze(2).to_broadcast([P, 256, 16]),
                                     iota[:, 0:16].unsqueeze(1).to_broadcast([P, 256, 16]),
                                     ALU.is_equal))
                pv = pick[:].rearrange("p (n k) a -> p n k a", k=16)
                link(V.tensor_tensor(pv, pv, keys_i[:, :, c, :].unsqueeze(2).to_broadcast(
                    [P, 16, 16, 16]), ALU.mult))
                link(V.tensor_reduce(route[:, c, :], pick[:], AX.X, ALU.add))
            dve.wait_ge(route_e, 1)
            gates_v = route[:, 2, :].rearrange("p (n k) -> p n k", k=16)
            link(V.tensor_reduce(st(RSUM, 16), gates_v, AX.X, ALU.add))
            link(V.reciprocal(st(RSUM, 16), st(RSUM, 16)))
            V.tensor_tensor(gates_v, gates_v, st(RSUM, 16).unsqueeze(2).to_broadcast([P, 16, 16]),
                            ALU.mult).then_inc(route_ready, 1)
            dve.wait_ge(route_turned, 1)
            for k, to in enumerate((i_t, j_t, gate_t)):
                ins = V.tensor_copy(to[:], ps[:, 4 + k, 0:T])
            ins.then_inc(routed, 1)
            dve.wait_ge(routed, 1)

            def one_hots(t, s, first=False):
                if not first:
                    dve.wait_ge(gmat_done, t - 1)
                at_ = bass.ds(t, 1)
                V.tensor_scalar(hot[:, s, 0, :], iota, i_t[:, at_], gate_t[:, at_], ALU.is_equal,
                                ALU.mult)
                V.tensor_scalar(hot[:, s, 1, :], iota, j_t[:, at_], None, ALU.is_equal)\
                    .then_inc(hot_done, 1)

            one_hots(0, 0, True)
            one_hots(1, 1, True)
            with dve.Fori(1, T // 2) as i:
                for s in range(2):
                    one_hots(i * 2 + s, s)
            dve.wait_ge(gmat_copied, T // 4)
            with dve.Fori(0, 64) as i:
                for s in range(2):
                    dve.wait_ge(free_a, i * 2 + (72 + s))
                    v = gm[:, bass.ds(i * 2 + s, 1), :].rearrange("p a t -> p (a t)")
                    V.tensor_tensor(v, v, act_t[:, s, :], ALU.mult).then_inc(gated_done, 1)
            dve.wait_ge(gated_done, 128)
            with dve.Fori(0, 32) as i:
                for s in range(4):
                    dve.wait_ge(hh_done, i * 4 + (s + 1))
                    V.tensor_tensor(hg_l[:, s, :], gm[:, bass.ds(i * 4 + s, 1), :].rearrange(
                        "p a t -> p (a t)"), hg_h[:, s, :].bitcast(F32), ALU.subtract)\
                        .then_inc(hl_done, 1)
            dve.wait_ge(got_h, 16)
            dve.wait_ge(unit_used, PIECES)
            for b in range(8):
                v = hx[:, b // 4, (b % 4) * NCH:(b % 4 + 1) * NCH]
                V.tensor_tensor(v, ps[:, b, :], v, ALU.add).then_inc(fin_done, 1)

        @block.tensor
        def _(pe):
            M = nc.tensor

            def exact(out_ap, a, b, n, start, stop, group=True):
                M.matmul(out_ap, a[0], b[0], start=start, stop=False)
                M.matmul(out_ap, a[0], b[1], start=False, stop=False)
                return M.matmul(out_ap, a[1], b[0], start=False, stop=stop)

            def ready(i, k):
                pe.wait_ge(lo_done[k], i + 1)

            def t_block(i, k0, bank):
                for half in range(2):
                    k = k0 + half
                    ready(i, k)
                    for j in range(8):
                        kb = 8 * half + j
                        w = [m[:, s, j * P:(j + 1) * P] for m, s in ((hi, k), (lo, k % 2))]
                        ins = exact(t_bank(bank), w, (xh[:, kb, :], xl[:, kb, :]), T,
                                    kb == 0, kb == KB - 1)
                    ins.then_inc(unit_used, 1)

            def n_piece(i, k, pair, kb0, first, last, a=None, nkb=2):
                ready(i, k)
                ah, al = a or (xh, xl)
                for j in range(nkb):
                    for tt in range(TT):
                        act_ = [m[:, kb0 + j, tt * P:(tt + 1) * P] for m in (ah, al)]
                        w = [m[:, s, j * NCH:(j + 1) * NCH] for m, s in ((hi, k), (lo, k % 2))]
                        ins = exact(ps[:, 2 * pair + tt, :], act_, w, NCH, first and j == 0,
                                    last and j == nkb - 1)
                ins.then_inc(unit_used, 1)
                return ins

            def n_chunk(i, pair):
                for q in range(8):
                    n_piece(i + q // 4, q % 4, pair, 2 * q, q == 0, q == 7)

            def turn(n):
                pe.wait_ge(xn_done, 2 * n + 2)
                b = [0, 2, 3, 4, 6][n]
                for kb in range(KB):
                    if kb >= 4:
                        pe.wait_ge(x_lo, 16 * b + kb - 3)
                    for tt in range(TT):
                        ins = M.transpose(tr_slot(kb % 8)[:, tt * P:(tt + 1) * P],
                                          xn[:, tt, kb * P:(kb + 1) * P], ident)
                    ins.then_inc(tr_done, 1)

            def plain(out_ap, a, b, start, stop, **kw):
                return M.matmul(out_ap, a, b, start=start, stop=stop, **kw)

            pe.wait_ge(got_const, 32)
            turn(0)
            pe.wait_ge(x_lo, 16)

            def gates(g):
                z, which = g // 2, g % 2
                if g == 0:
                    pe.wait_ge(got_wg, 32)
                    pe.wait_ge(conv_done, 8)
                else:
                    pe.wait_ge(tanh_done, 8 * g)
                for n in range(8):
                    ins = plain(ps[:, 4 + n // 2, (n % 2) * T:(n % 2) * T + T],
                                wg[:, 16 * which + 8 * z + n, :], xc[:, n, :], True, True)
                ins.then_inc(gates_done, 1)

            for b in range(24):
                if b >= 4:
                    pe.wait_ge(free_d, b - 3)
                t_block(b // 2, 2 * (b % 2), b % 4)
                if b in (11, 15, 19, 23):
                    gates((b - 11) // 4)
            for c in range(2):
                pe.wait_ge(free_d, 22 + 2 * c)
                n_chunk(12 + 2 * c, c)
            for b in range(8):
                if b < 4:
                    pe.wait_ge(free_d, 25 + b // 2)
                else:
                    pe.wait_ge(free_a, b - 3)
                t_block(16 + b // 2, 2 * (b % 2), b % 4)

            def sums(branch):
                pe.wait_ge(mo_sq, branch + 1)
                if branch == 0:
                    pe.wait_ge(tanh_done, 32)
                sq = (th_i, th_a)[branch][:, 1]
                for n in range(8):
                    ins = plain(ps[:, 4 + branch, 0:T], ones, sq[:, n, :], n == 0, n == 7)
                return ins

            def attend(n0, heads, slots, q_of, k_of, v_of, exp_sem):
                _, p_sb_, pt = slots

                def scores(h):
                    if h >= 2:
                        pe.wait_ge(at_b, n0 + h - 1)
                    for qt in range(TT):
                        ins = plain(ps[:, 4 + h % 2, qt * T:(qt + 1) * T],
                                    q_of(h)[:, qt * P:(qt + 1) * P], k_of(h), True, True)
                    ins.then_inc(at_s, 1)

                def turned(h):
                    pe.wait_ge(at_p, n0 + h + 1)
                    if h:
                        pe.wait_ge(at_c, n0 + h)
                    for kt in range(TT):
                        for qt in range(TT):
                            ins = M.transpose(
                                ps[:, 6, kt * T + qt * P:kt * T + (qt + 1) * P],
                                p_sb_[:, h % 2, qt, kt * P:(kt + 1) * P], ident)
                    ins.then_inc(at_t, 1)

                def heads_out(h):
                    pe.wait_ge(at_c, n0 + h + 1)
                    if h:
                        exp_sem(h)
                    for kt in range(TT):
                        ins = plain(ps[:, 7, 0:T], v_of(h, kt), pt[:, h % 2, kt, :], kt == 0,
                                    kt == TT - 1)
                    ins.then_inc(at_o, 1)

                scores(0)
                scores(1)
                for h in range(heads):
                    turned(h)
                    if h + 2 < heads:
                        scores(h + 2)
                    heads_out(h)

            pe.wait_ge(tanh_done, 32)
            attend(0, HEADS1, at1, lambda h: q_t[:, h, :], lambda h: k_t[:, h, :],
                   lambda h, kt: v_n[:, kt, h * P:(h + 1) * P],
                   lambda h: pe.wait_ge(at_f, h))
            pe.wait_ge(at_b, HEADS1)
            sums(0).then_inc(mo_sum, 1)
            sums(1).then_inc(mo_sum, 1)

            def n_stage(name, free):
                r0 = ROUND0[name]
                for c in range(4):
                    free(c)
                    n_chunk(r0 + 2 * c, c % 2)

            def both(d0, a0):
                def free(c):
                    if c >= 2:
                        pe.wait_ge(free_d, d0 + c - 1)
                        pe.wait_ge(free_a, a0 + c - 1)
                return free

            pe.wait_ge(x_lo, 32)
            pe.wait_ge(free_a, 8)
            pe.wait_ge(mo_ms, 2)
            n_stage("out1", both(26, 8))
            turn(1)
            pe.wait_ge(x_lo, 48)
            pe.wait_ge(free_a, 12)
            r0 = ROUND0["ffn"]
            with pe.Fori(0, FB // 2) as i:
                for s in range(2):
                    pe.wait_ge(free_a, i * 2 + (11 + s))
                    t_block(i * 2 + (r0 + s), 0, 2 * s)
                    pe.wait_ge(free_d, i * 2 + (29 + s))
                    t_block(i * 2 + (r0 + s), 2, 2 * s + 1)
            pe.wait_ge(free_d, 74)
            pe.wait_ge(free_a, 56)
            r0 = ROUND0["down"]
            with pe.Fori(0, 2) as i:
                for c in range(2):
                    pe.wait_ge(free_d, i * 2 + (73 + c))
                    pe.wait_ge(free_a, i * 2 + (55 + c))
                    for q in range(22):
                        u = 22 * c + q
                        n_piece(i * 11 + (r0 + u // 4), u % 4, c, 2 * q, q == 0, q == 21,
                                (hid_h, hid_l))
            turn(2)
            pe.wait_ge(x_lo, 64)
            pe.wait_ge(got_ple, 32)
            r0 = ROUND0["gate"]
            for c in range(4):
                if c >= 2:
                    pe.wait_ge(free_a, 60 + c - 1)
                    pe.wait_ge(ple_free, c - 1)
                else:
                    pe.wait_ge(free_d, 78)
                    pe.wait_ge(free_a, 60)
                for tt in range(TT):
                    for j in range(2):
                        ins = plain(ps[:, 4 + 2 * (c % 2) + tt, :], p_sb[:, j, tt * P:(tt + 1) * P],
                                    w_pr[:, j, c * NCH:(c + 1) * NCH], j == 0, j == 1)
                ins.then_inc(ple_done, 1)
                n_chunk(r0 + 2 * c, c % 2)
            turn(3)

            pe.wait_ge(x_lo, 80)
            pe.wait_ge(g_dve, 1)
            for tt in range(TT):
                for kb in range(KB):
                    ins = exact(ps[:, 4, 32 * tt:32 * tt + 32],
                                [m[:, kb, tt * P:(tt + 1) * P] for m in (xh, xl)],
                                [m[:, kb, :] for m in (wgd_h, wgd_l)], 32, kb == 0, kb == KB - 1)
            ins.then_inc(g_pe, 1)
            r0 = ROUND0["in2"]
            pe.wait_ge(free_a, 64)
            t_block(r0, 0, 0)
            t_block(r0, 2, 1)
            pe.wait_ge(g_dve, 2)
            for tt in range(TT):
                ins = plain(ps[0:32, 5, tt * P:(tt + 1) * P], gd_n[:, tt, :], ident, True, True)
            ins.then_inc(g_pe, 1)
            t_block(r0 + 1, 0, 2)
            t_block(r0 + 1, 2, 3)
            pe.wait_ge(g_dve, 3)
            for m in range(4):
                ins = plain(tr_slot(4 + m), up[:, m * P:(m + 1) * P], gd_t[:], True, True)
            ins.then_inc(g_pe, 1)

            def scores_in_chunks():
                pe.wait_ge(g_dve, 5)
                for d in range(2):
                    for tt in range(TT):
                        for h in range(4):
                            rows, m = slice(64 * (h % 2), 64 * (h % 2) + 64), 2 * d + h // 2
                            at_ = (2 * d + h // 2) * P
                            ins = plain(ps[:, 4 + 2 * tt + h % 2, at_:at_ + P],
                                        g3[rows, m, tt * P:(tt + 1) * P],
                                        g2[rows, m, tt * P:(tt + 1) * P], True, True)
                ins.then_inc(g_pe, 1)

            def turn_key_states():
                pe.wait_ge(g_dve, 6)
                for tt in range(TT):
                    for m in range(4):
                        ins = M.transpose(ps[:, 4 + tt, m * P:(m + 1) * P],
                                          g4[:, m, tt * P:(tt + 1) * P], ident)
                ins.then_inc(g_pe, 1)

            def increments(d):
                pe.wait_ge(g_dve, 7 + d)
                for n in range(3):
                    c = n if d == 0 else 3 - n
                    rows = slice(64 * (c % 2), 64 * (c % 2) + 64)
                    for half in range(2):
                        ins = plain(inc_at(d, c, half), kst[rows, c // 2, 2 * d + half, :],
                                    va[rows, c // 2, half * T:(half + 1) * T], True, True)
                ins.then_inc(g_pe, 1)

            def gla_out():
                pe.wait_ge(g_dve, 9)
                for tt in range(TT):
                    for h in range(4):
                        bank, at_ = 4 + 2 * tt + h % 2, (h // 2) * P
                        rows = slice(64 * (h % 2), 64 * (h % 2) + 64)
                        for d in range(2):
                            o = (2 * d + h // 2) * P
                            plain(ps[:, bank, at_:at_ + P], sc_t[:, 2 * tt + h % 2, o:o + P],
                                  va[:, tt, h * P:(h + 1) * P], d == 0, False,
                                  skip_group_check=True)
                        for c in (2 * tt, 2 * tt + 1):
                            for d in range(2):
                                before = c - 1 if d == 0 else 2 - c
                                if before < 0:
                                    continue
                                half = slice(64 * (c % 2), 64 * (c % 2) + 64)
                                ins = plain(ps[half, bank, at_:at_ + P],
                                            g2[rows, 2 * d + h // 2, 64 * c:64 * c + 64],
                                            state[rows, d, before, h // 2, :], False, True,
                                            skip_group_check=True)
                ins.then_inc(g_pe, 1)

            def turn_qk(which):
                pe.wait_ge(qk_ready, which + 1)
                for h in range(HEADS2):
                    n = HEADS2 * which + h
                    if n >= 4:
                        if n - 4 < HEADS2:
                            pe.wait_ge(q_copied, n - 3)
                        else:
                            pe.wait_ge(k_copied, n - 3 - HEADS2)
                    for tt in range(TT):
                        ins = M.transpose(tr_slot(n % 8)[:, tt * P:(tt + 1) * P],
                                          qk_n[which][:, tt, h * P:(h + 1) * P], ident)
                    ins.then_inc(qk_turned, 1)

            waits = [(80, 0), (82, 0), (83, 0), (0, 65), (84, 66), (85, 67), (86, 68), (87, 69),
                     (88, 70), (89, 71), (90, 0)]
            then = {1: scores_in_chunks, 3: turn_key_states, 4: lambda: increments(0),
                    5: lambda: increments(1), 6: gla_out}
            for n in range(11):
                for s_, v_ in zip((free_d, free_a), waits[n]):
                    if v_:
                        pe.wait_ge(s_, v_)
                n_chunk(r0 + 2 + 2 * n, n % 2)
                if n in then:
                    then[n]()
                if n == 7:
                    pe.wait_ge(g_dve, 10)
                    turn_qk(0)
                if n == 9:
                    turn_qk(1)
            pe.wait_ge(g_dve, 12)
            pe.wait_ge(k_copied, HEADS2)
            for kb in range(4):
                for tt in range(TT):
                    ins = M.transpose(tr_slot(kb)[:, tt * P:(tt + 1) * P],
                                      o_n[:, tt, kb * P:(kb + 1) * P], ident)
                ins.then_inc(g_pe, 1)
            pe.wait_ge(x_lo, 84)
            pe.wait_ge(free_d, 92)
            attend(HEADS1, HEADS2, at2, lambda h: q_t2[:, h, :], lambda h: k_t2[:, h, :],
                   lambda h, kt: vn[:, kt, h * P:(h + 1) * P],
                   lambda h: pe.wait_ge(x_lo, 84 + h))
            pe.wait_ge(x_lo, 96)
            r0 = ROUND0["out2"]
            for c in range(4):
                if c >= 2:
                    pe.wait_ge(free_d, 92 + c - 1)
                n_chunk(r0 + 2 * c, c % 2)
            turn(4)
            pe.wait_ge(x_lo, 112)
            for b in range(KB):
                if b >= 4:
                    pe.wait_ge(free_d, 95 + b - 3)
                t_block(ROUND0["query"] + b // 2, 2 * (b % 2), b % 4)
            pe.wait_ge(free_d, 111)
            pe.wait_ge(got_keys, 16)
            for r in range(32):
                tt, hc = r // 16, r % 16
                bank = 4 + r // 4 if r < 16 else (r - 16) // 4
                ins = plain(ps[:, bank, (r % 4) * P:(r % 4 + 1) * P],
                            qry_t[:, hc, tt * P:(tt + 1) * P], keys_t[:, hc, :], True, True)
            ins.then_inc(key_scores, 1)
            pe.wait_ge(route_ready, 1)
            for k in range(3):
                for tt in range(TT):
                    ins = M.transpose(ps[:, 4 + k, tt * P:(tt + 1) * P],
                                      route[:, k, tt * P:(tt + 1) * P], ident)
            ins.then_inc(route_turned, 1)

            def gate_matrix(i, n):
                pe.wait_ge(hot_done, i * 16 + (n + 1))
                plain(ps[:, 4 + n // 4, (n % 4) * P:(n % 4 + 1) * P], hot[:, n % 2, 0, :],
                      hot[:, n % 2, 1, :], True, True).then_inc(gmat_done, 1)

            pe.wait_ge(routed, 1)
            for n in range(16):
                gate_matrix(0, n)
            with pe.Fori(1, T // 16) as i:
                for n in range(16):
                    if n % 4 == 0:
                        pe.wait_ge(gmat_copied, i * 4 + (n // 4 - 3))
                    gate_matrix(i, n)
            r0 = ROUND0["peer_down"]
            for j in range(4):
                t_block(r0 + j // 2, 2 * (j % 2), j)
            with pe.Fori(1, 32) as i:
                for j in range(4):
                    pe.wait_ge(free_a, i * 4 + (71 + j - 3))
                    t_block(i * 2 + (r0 + j // 2), 2 * (j % 2), j)
            pe.wait_ge(free_a, 71 + 128)
            pe.wait_ge(gmat_copied, T // 4)

            def up_block(j, i, k0, s, first=False, last=False):
                pe.wait_ge(hl_done, j + 1)
                for half in range(2):
                    k = k0 + half
                    ready(i, k)
                    for n in range(2):
                        for tt in range(TT):
                            ins = exact(ps[:, 4 * tt + 2 * half + n, :],
                                        [m[:, s, tt * P:(tt + 1) * P] for m in (hg_h, hg_l)],
                                        [m[:, q, n * NCH:(n + 1) * NCH]
                                         for m, q in ((hi, k), (lo, k % 2))], NCH, first, last)
                    ins.then_inc(unit_used, 1)

            r0 = ROUND0["peer_up"]
            for j in range(4):
                up_block(j, r0 + j // 2, 2 * (j % 2), j, first=j == 0)
            with pe.Fori(1, 31) as i:
                for j in range(4):
                    up_block(i * 4 + j, i * 2 + (r0 + j // 2), 2 * (j % 2), j)
            for j in range(4):
                up_block(124 + j, r0 + 62 + j // 2, 2 * (j % 2), j, last=j == 3)


def pieces_t(w, blocks):
    w = w.reshape(2, 8, P, -1, P)[:, :, :, blocks]
    return w.transpose(3, 0, 2, 1, 4).reshape(-1, P, PIECE)


def pieces_n(w, first, chunks):
    w = w[:, first:first + chunks * NCH].reshape(-1, 2, P, chunks, NCH)
    return w.transpose(3, 0, 2, 1, 4).reshape(-1, P, PIECE)


def lay_out(x, p, g_mix_pre, w_in, rpb, conv_w, conv_b, w_rg_a, b_rg_a, w_rg_i, b_rg_i, lam,
            g_attn_out, g_rec_out, w_out, g_mix_post, g_ffn_pre, w_ffn_gate, w_ffn_up, w_ffn_down,
            g_ffn_post, g_ple_pre, w_ple_gate, w_ple_proj, g_ple_post, norm1_g_2, w_in_2,
            gla_up_f_2, gla_bias_f_2, gla_up_b_2, gla_bias_b_2, gla_out_g_2, q_norm_g_2,
            k_norm_g_2, w_out_2, norm2_g_2, peer_w_query_2, peer_sub_keys_2, peer_down_2,
            peer_up_2):
    c, band, dil = shape_constants()
    win, win2 = w_in[0], w_in_2[0]
    gate_up = np.stack([pieces_t(w_ffn_gate[0], np.arange(FB)).reshape(FB, 2, P, PIECE),
                        pieces_t(w_ffn_up[0], np.arange(FB)).reshape(FB, 2, P, PIECE)], 1)
    rest = np.concatenate([win2[:, 512:1024], win2[:, 1056:]], 1)
    down = peer_down_2[0].reshape(P, NKEY, 2, 8, P).transpose(1, 2, 4, 3, 0)
    up = peer_up_2[0].reshape(P, NKEY, 2, PIECE).transpose(1, 2, 0, 3)
    stream = np.concatenate([
        pieces_t(win, np.r_[24:32, 0:16]), pieces_n(win, 2048, 2), pieces_t(win, np.arange(32, 40)),
        pieces_n(w_out[0], 0, 4), gate_up.reshape(-1, P, PIECE), pieces_n(w_ffn_down[0], 0, 4),
        pieces_n(w_ple_gate[0], 0, 4), pieces_t(win2[:, 0:512], np.arange(4)),
        pieces_n(rest, 0, 11), pieces_n(w_out_2[0], 0, 4),
        pieces_t(peer_w_query_2[0], np.arange(KB)), down.reshape(-1, P, PIECE),
        up.reshape(-1, P, PIECE)])
    assert stream.shape[0] == PIECES

    def columns(*vectors):
        return np.concatenate([v.reshape(-1, P) for v in vectors]).T

    cols = columns(g_mix_pre, g_ffn_pre, g_ple_pre, norm1_g_2, norm2_g_2, g_attn_out, g_rec_out,
                   gla_out_g_2, conv_w, conv_b, b_rg_a, b_rg_i, lam, gla_bias_f_2, gla_bias_b_2)
    col_, row = np.arange(64), np.arange(4)
    gap = col_[None, :] - col_[:, None] + 15
    wide = rpb[0][:, (row[None, :] - row[:, None] + 7)[:, :, None, None],
                  np.clip(gap, 0, 30)[None, None]]
    wide = np.where((gap >= 0) & (gap <= 30), wide, np.zeros((), rpb.dtype))
    wide = wide.transpose(1, 3, 0, 2, 4).reshape(TT, P, HEADS1, T).transpose(1, 2, 0, 3)
    up_fb = np.zeros((32, 512), np.float32)
    up_fb[0:16, 0:256] = gla_up_f_2[0]
    up_fb[16:32, 256:512] = gla_up_b_2[0]
    gains = np.stack([np.broadcast_to(g[0], (P, D)) for g in (g_mix_post, g_ffn_post, g_ple_post)])
    return {
        "stream": stream,
        "cols": cols,
        "cons": c,
        "band": band,
        "dil": dil,
        "x": x[0],
        "rpb": wide,
        "w_gates": np.concatenate([w_rg_a[0].reshape(16, P, P), w_rg_i[0].reshape(16, P, P)])
        .transpose(1, 0, 2),
        "gains": gains,
        "p_t": p[0, 0].T.reshape(2, P, T).transpose(1, 0, 2),
        "w_proj": w_ple_proj[0].reshape(2, P, D).transpose(1, 0, 2),
        "w_gd": win2[:, 1024:1056].reshape(KB, P, 32).transpose(1, 0, 2),
        "up_fb": up_fb,
        "qk_gain": np.broadcast_to(np.stack([q_norm_g_2[0], k_norm_g_2[0]]), (P, 2, HD)),
        "sub_keys": peer_sub_keys_2[0].transpose(3, 0, 1, 2).reshape(P, KB, NKEY),
    }


def kernel(**inputs):
    import concourse.bacc as bacc
    from concourse.bass_utils import run_bass_kernel_spmd

    nc = bacc.Bacc("TRN2", target_bir_lowering=False, num_devices=1)
    laid = lay_out(**{k: np.asarray(v) for k, v in inputs.items()})
    arrays, args = {}, {}
    for name, a in laid.items():
        a = np.ascontiguousarray(a)
        arrays[f"in_{name}"] = a
        args[name] = nc.dram_tensor(f"in_{name}", a.shape, mybir.dt.from_np(a.dtype),
                                    kind="ExternalInput").ap()
    spill = nc.dram_tensor("spill", [P, TT, D], F32).ap()
    out = nc.dram_tensor("out", [T, D], F32, kind="ExternalOutput").ap()
    build(nc, spill=spill, out=out, **args)
    r = run_bass_kernel_spmd(nc, [arrays], core_ids=[0])
    return r.results[0]["out"].reshape(1, T, D)
```

```python
import numpy as np
import concourse.bass as bass
from concourse import mybir
from contextlib import ExitStack

F32 = mybir.dt.float32
F32R = mybir.dt.float32r
U32 = mybir.dt.uint32
ALU = mybir.AluOpType
ACT = mybir.ActivationFunctionType
AX = mybir.AxisListType

P = 128
T = 256
TT = T // P
D = 2048
KB = D // P
DFF = 5632
FB = DFF // P
EPS = 1e-6
NCH = 512
HD = 128
SCALE = HD ** -0.5
HEADS1 = 8
HEADS2 = 12
GLA_W = 512
EXPERTS = 16384
NKEY = 128
PIECE = 1024

STAGES = [("in1", 80), ("out1", 32), ("ffn", 176), ("down", 88), ("gate", 32), ("in2", 96),
          ("out2", 32), ("query", 32), ("peer_down", 256), ("peer_up", 256)]
ROUND0, _n = {}, 0
for _name, _pieces in STAGES:
    ROUND0[_name] = _n // 4
    _n += _pieces
PIECES = _n
ROUNDS = PIECES // 4


def after(name, pieces):
    return 4 * ROUND0[name] + pieces


COLS, _n = {}, 0
for _name, _w in [("g_mix", 16), ("g_ffn", 16), ("g_ple", 16), ("g_n1", 16), ("g_n2", 16),
                  ("g_mo", 16), ("g_gla", 4), ("conv_w", 32), ("conv_b", 8), ("b_a", 16),
                  ("b_i", 16), ("lam", 16), ("gla_b", 4)]:
    COLS[_name] = (_n, _w)
    _n += _w
NCOLS = _n
CONS, _n = {}, 0
for _name, _w in [("ident", 128), ("iota", 128), ("ones", 128), ("cos", 32), ("sin", 32),
                  ("scan", 256), ("causal", 256)]:
    CONS[_name] = (_n, _w)
    _n += _w
NCONS = _n


def shape_constants():
    c = np.zeros((P, NCONS), np.float32)
    lane = np.arange(P)

    def put(name, a):
        o, w = CONS[name]
        c[:, o:o + w] = np.asarray(a, np.float32).reshape(P, w)

    put("ident", np.eye(P))
    put("ones", np.ones((P, P)))
    put("iota", np.broadcast_to(lane, (P, P)))
    half = 16
    inv = np.float32(500000.0) ** (-np.arange(half, dtype=np.float32) / np.float32(half))
    ang = (np.arange(T, dtype=np.float32)[:, None] * inv[None, :]).astype(np.float32)
    put("cos", np.cos(ang).reshape(TT, P, half).transpose(1, 0, 2))
    put("sin", np.sin(ang).reshape(TT, P, half).transpose(1, 0, 2))
    put("scan", np.broadcast_to(np.arange(T) % 64 != 0, (P, T)))
    same = lane[:, None] // 64 == lane[None, :] // 64
    key, query = lane[:, None], lane[None, :]
    put("causal", np.stack([same & (key <= query), same & (key > query)], 1))
    col = np.arange(64)
    start = np.clip(col - 8, 0, 48)
    near = (col[None] >= start[:, None]) & (col[None] < start[:, None] + 16)
    band = np.where(near, 0.0, -1e9)[lane % 64].astype(np.float32)
    q = np.arange(T)
    gap = np.abs(q[:, None] - q[None, :])
    times = (gap <= 64).astype(np.float32) + (gap % 4 == 0) + (gap % 16 == 0)
    times = times.reshape(TT, P, T).transpose(1, 0, 2).astype(np.float32)
    dil = np.stack([np.where(times == 0, -1e30, 0.0), times], 1).astype(np.float32)
    return c, band, dil


def build(nc, stream, cols, cons, band, dil, x, rpb, w_gates, gains, p_t, w_proj, w_gd, up_fb,
          qk_gain, sub_keys, spill, out):
    ctx = ExitStack()
    with ctx:
        def sem(name):
            return ctx.enter_context(nc.semaphore(name))

        base = -(-nc.sbuf_base // 32) * 32
        ctx.enter_context(nc.sbuf_tensor("whole", [P, (nc.sbuf_top - nc.sbuf_base - 32) // 4], F32))

        def place(name, shape, at, dt=F32):
            return nc.alloc_sbuf_tensor_at(name, shape, dt, offset=base + at)

        cons_sb = place("cons_sb", [P, NCONS], 0)
        cols_sb = place("cols_sb", [P, NCOLS], NCONS * 4)
        X_AT = 8032
        STATS = 320
        small = place("small", [P, STATS], X_AT - 4 * STATS)
        assert (NCONS + NCOLS + STATS) * 4 <= X_AT
        hot_at = 256 * 4
        i_t, j_t, gate_t = (place(n, [P, T], hot_at + 1024 * k)
                            for k, n in enumerate(("i_t", "j_t", "gate_t")))
        HOTS = 4
        hot_i = place("hot_i", [P, HOTS, P], hot_at + 3072)
        hot_j = place("hot_j", [P, HOTS, NKEY // 2], hot_at + 3072 + 512 * HOTS)
        assert hot_at + 3072 + 768 * HOTS <= X_AT
        RING_AT = X_AT + 32768
        W_AT = RING_AT + 40960
        assert base + W_AT + 131072 <= nc.sbuf_usable_end, (base, nc.sbuf_usable_end)
        xh = place("xh", [P, KB, T], X_AT, F32R)
        xl = place("xl", [P, KB, T], X_AT + 16384, F32R)
        raw = place("raw", [P, 4, PIECE], RING_AT)
        hi = place("hi", [P, 4, PIECE], RING_AT + 16384, F32R)
        lo = place("lo", [P, 2, PIECE], RING_AT + 32768, F32R)
        hx = place("hx", [P, TT, D], W_AT)
        xn = place("xn", [P, TT, D], W_AT + 16384)
        Z_AT = W_AT + 40960

        def con(name, *dims):
            o, w = CONS[name]
            return cons_sb[:, o:o + w]

        def col(name, i, n=1):
            o, _ = COLS[name]
            return cols_sb[:, o + i:o + i + n]

        ident, ones, iota = con("ident"), con("ones"), con("iota")

        def st(i, n=1):
            return small[:, i:i + n]

        ps = ctx.enter_context(nc.psum_tensor("ps", [P, 8, 512], F32))

        loaded = [sem(f"loaded{k}") for k in range(4)]
        hi_done, unit_used, half_used = sem("hi_done"), sem("unit_used"), sem("half_used")
        lo_done = [sem(f"lo_done{k}") for k in range(4)]
        free_d, free_a = sem("free_d"), sem("free_a")
        x_hi, x_lo = sem("x_hi"), sem("x_lo")
        dch, ach = sem("dve_chain"), sem("act_chain")
        got_const, got_x, got_wg, got_bias, got_gain = (sem(n) for n in (
            "got_const", "got_x", "got_gate_weights", "got_bias", "got_gain"))
        got_ple, got_in2 = sem("got_ple"), sem("got_in2")
        spilled, got_h = sem("spilled"), sem("got_h")
        h_new, ss_done, ms_done, rms_done, xn_done, tr_done = (sem(n) for n in (
            "h_new", "ss_done", "ms_done", "rms_done", "xn_done", "tr_done"))
        conv_done, gates_done, tanh_done, decay_done, z_done, sqrt_done, gelu_done = (
            sem(n) for n in ("conv_done", "gates_done", "tanh_done", "decay_done", "z_done",
                             "sqrt_done", "gelu_done"))
        soft_e, soft_c = sem("soft_e"), sem("soft_c")
        at_s, at_b, at_m, at_e, at_p, at_t, at_c, at_o, at_f = (sem(n) for n in (
            "scores_done", "bias_added", "max_done", "exp_done", "probs_ready", "probs_turned",
            "probs_copied", "heads_done", "heads_copied"))
        mo_sq, mo_sum, mo_ms, mo_rt, mo_ready = (sem(n) for n in (
            "mo_sq", "mo_sum", "mo_ms", "mo_rt", "mo_ready"))
        sq_done, act_post, silu_done, prod_done = (sem(n) for n in (
            "sq_done", "act_post", "silu_done", "prod_done"))
        sig_done, ple_done, ple_free = sem("sig_done"), sem("ple_done"), sem("ple_free")
        hid_hi = sem("hid_hi")
        out_stored = sem("out_stored")
        g_pe, g_dve, g_act = sem("gla_pe"), sem("gla_dve"), sem("gla_act")
        qk_squared, qk_reduced, qk_ms, qk_rt, qk_ready, qk_turned, q_copied, k_copied = (
            sem(n) for n in ("qk_squared", "qk_reduced", "qk_ms", "qk_rt", "qk_ready",
                             "qk_turned", "q_copied", "k_copied"))
        got_dil, got_keys = sem("got_dil"), sem("got_keys")
        lists_read = sem("lists_read")
        key_scores, route_m, route_e, route_ready, route_turned, routed = (
            sem(n) for n in ("key_scores", "route_m", "route_e", "route_ready", "route_turned",
                             "routed"))
        hot_done, gmat_done = sem("hot_done"), sem("gmat_done")
        gelu2_done, gated_done, hh_done, hl_done, up_done = (sem(n) for n in (
            "gelu2_done", "gated_done", "hh_done", "hl_done", "up_done"))
        fin_done = sem("fin_done")

        block = ctx.enter_context(nc.Block())

        XRW = 260
        xr = place("xr", [P, 8, XRW], Z_AT)
        t_z0 = place("t_z0", [P, 8, T], Z_AT)
        xc = place("xc", [P, 8, T], Z_AT + 8320)
        q_t = place("q_t", [P, 8, T], Z_AT + 8320 + 8192)
        k_t = place("k_t", [P, 8, T], Z_AT + 8320 + 2 * 8192)
        v_n = place("v_n", [P, TT, 1024], Z_AT + 8320 + 3 * 8192)
        yg = place("yg", [P, 8, T], Z_AT + 8320 + 4 * 8192)
        th_a = place("th_a", [P, 2, 8, T], Z_AT + 8320 + 5 * 8192)
        th_i = place("th_i", [P, 2, 8, T], Z_AT + 8320 + 7 * 8192)
        band_sb = place("band_sb", [P, 64], Z_AT + 8320 + 9 * 8192)
        mo_r = place("mo_r", [P, 2, T], Z_AT + 8320 + 9 * 8192 + 256)
        wg = place("wg", [P, 32, P], W_AT + 16384)
        bias = place("bias", [P, HEADS1, TT, T], W_AT + 16384)
        t_z1 = place("t_z1", [P, 8, T], W_AT + 32768)
        attn_t = place("attn_t", [P, 8, T], W_AT + 32768)
        A1 = Z_AT + 8320 + 5 * 8192
        at1 = [place(f"at1_{i}", [P, 2, TT, T], A1 + 4096 * i) for i in range(3)]
        y = place("y", [P, TT, D], W_AT + 16384)
        gbc = place("gbc", [P, D], W_AT + 32768)
        sil = place("sil", [P, 2, T], W_AT + 16384)
        prod = place("prod", [P, 2, T], W_AT + 16384 + 2048)
        hid_h = place("hid_h", [P, FB, T], Z_AT, F32R)
        hid_l = place("hid_l", [P, FB, T], Z_AT + FB * T * 4, F32R)
        w_pr = place("w_pr", [P, 2, D], Z_AT)
        p_sb = place("p_sb", [P, 2, T], Z_AT + 16384)
        sig = place("sig", [P, 2, TT, NCH], Z_AT + 18432)
        pz = place("pz", [P, TT, NCH], Z_AT + 26624)
        junk = place("junk", [P, NCH], Z_AT + 30720)
        SS, MS, RT, RI = 0, 2, 4, 6
        SSP = 8
        NM, SM, SI = 16, 24, 32
        LAMW = 40
        CSP = 104
        SSQ = 136
        SRT = 184
        GDEC = 232
        GSS = 248
        GRT = 256
        BA2 = 264
        GH = 296

        qn, kn, vn = (place(n, [P, TT, HEADS2 * HD], Z_AT + 12288 * k)
                      for k, n in enumerate(("qn", "kn", "vn")))
        qk_n = (qn, kn)
        GZ = Z_AT + 36864
        qa_t = place("qa_t", [P, 2, T], GZ)
        ka_t = place("ka_t", [P, 2, T], GZ + 2048)
        va = place("va", [P, TT, GLA_W], GZ + 4096)
        sra = place("sra", [P, TT, GLA_W], GZ + 8192)
        g1, g2, g3, g4 = (place(f"g{k + 1}", [P, 4, T], GZ + 12288 + 4096 * k) for k in range(4))
        kst = place("kst", [P, TT, 4, P], GZ + 12288)
        sc_t = place("sc_t", [P, 4, 512], GZ + 28672)
        state = place("state", [P, 2, 3, 2, P], GZ + 36864)
        o_n = place("o_n", [P, TT, GLA_W], GZ + 43008)
        sqt = place("sqt", [P, TT, NCH], GZ + 47104)
        rope_t = place("rope_t", [P, 4, 12, 16], GZ + 47104)
        qkg = place("qkg", [P, 2, HD], GZ + 51200)
        wgd = place("wgd", [P, KB, 32], GZ + 28672)
        wgd_h = place("wgd_h", [P, KB, 32], GZ + 28672 + 2048, F32R)
        wgd_l = place("wgd_l", [P, KB, 32], GZ + 28672 + 4096, F32R)
        gd_n = place("gd_n", [P, TT, 32], GZ + 28672 + 6144)
        gd_t = place("gd_t", [32, T], GZ + 28672 + 6400)
        up = place("up", [32, 512], GZ + 28672 + 7424)
        q_t2 = place("q_t2", [P, HEADS2, T], W_AT + 16384)
        k_t2 = place("k_t2", [P, HEADS2, T], W_AT + 28672)
        dil_sb = place("dil_sb", [P, 2, TT, T], GZ + 12288)
        at2 = [place(f"at2_{i}", [P, 2, TT, T], GZ + 16384 + 4096 * i) for i in range(3)]
        W2_AT = W_AT + 65536
        qry_t = place("qry_t", [P, KB, T], W2_AT)
        keys_t = place("keys_t", [P, KB, NKEY], W2_AT + 16384)
        sc_rest = place("sc_rest", [P, 32, NKEY], W2_AT + 24576)
        cand = place("cand", [P, 16, 256], W2_AT)
        cand_rest = place("cand_rest", [P, 16, 256], W2_AT + 24576)
        pick = place("pick", [P, 256, 16], W2_AT + 24576)
        R_AT = W2_AT + 40960
        top = place("top", [P, 32, 16], R_AT)
        top_u = place("top_u", [P, 32, 16], R_AT + 2048, U32)
        top_i = place("top_i", [P, 32, 16], R_AT + 4096)
        best = place("best", [P, 16, 16], R_AT + 6144)
        pos = place("pos", [P, 16, 16], R_AT + 7168, U32)
        pos_a = place("pos_a", [P, 16, 16], R_AT + 8192, U32)
        pos_b = place("pos_b", [P, 16, 16], R_AT + 9216, U32)
        pos_f = place("pos_f", [P, 2, 256], R_AT + 10240)
        route = place("route", [P, 3, 256], R_AT + 12288)
        RSUM = 296
        gm = place("gm", [P, NKEY, T], W_AT)
        hg_h = place("hg_h", [P, 4, T], X_AT, F32R)
        hg_l = place("hg_l", [P, 4, T], X_AT + 4096, F32R)
        hx_end = place("hx_end", [P, TT, D], X_AT + 8192)

        class Chain:

            def __init__(self, eng, s):
                self.eng, self.s, self.n, self.reg, self.per, self.k = eng, s, 0, None, 0, 0

            def value(self):
                return self.n if self.reg is None else self.reg * self.per + (self.n + self.k)

            def inc(self, ins):
                if self.reg is None:
                    self.n += 1
                else:
                    self.k += 1
                ins.then_inc(self.s, 1)

            def wait(self):
                self.eng.wait_ge(self.s, self.value())

            def link(self, ins):
                self.inc(ins)
                self.wait()

            def enter(self, reg, per):
                self.reg, self.per, self.k = reg, per, 0

            def leave(self, times):
                assert self.k == self.per, (self.k, self.per)
                self.n += self.per * times
                self.reg = None

        def t_bank(b):
            return ps[:, b, 0:T]

        def inc_at(d, c, half):
            nth = 1 if (d, c) in ((0, 2), (1, 1)) else 0
            return ps[:, 4 + c % 2 + 2 * nth, half * T:(half + 1) * T]

        def out_part(b):
            return b // 2 % 2, 2 * (b // 4) + b % 2

        def tr_slot(s):
            return ps[:, 4 + s % 4, (s // 4) * T:(s // 4) * T + T]

        @block.sync
        def _(sp):
            for k in range(4):
                sp.dma_start(raw[:, k, :], stream[k]).then_inc(loaded[k], 16)
            with sp.Fori(1, ROUNDS) as i:
                for k in range(4):
                    sp.wait_ge(lo_done[k], i * 2)
                    sp.dma_start(raw[:, k, :], stream[bass.ds(i * 4 + k, 1)].rearrange(
                        "a p n -> p (a n)")).then_inc(loaded[k], 16)
            for b in range(8):
                sp.wait_ge(fin_done, b + 1)
                tt, c = out_part(b)
                sp.dma_start(out[tt * P:(tt + 1) * P, c * NCH:(c + 1) * NCH],
                             hx_end[:, tt, c * NCH:(c + 1) * NCH]).then_inc(out_stored, 16)
            sp.wait_ge(out_stored, 16 * 8)

        @block.gpsimd
        def _(pool):
            def take_lo(i, k, first):
                pool.wait_ge(hi_done, i * 4 + (k + 1))
                for half, used in enumerate((half_used, unit_used)):
                    if not (first and k < 2):
                        pool.wait_ge(used, i * 4 + (k - 1))
                    n = slice(half * NCH, (half + 1) * NCH)
                    nc.gpsimd.tensor_tensor(lo[:, k % 2, n], raw[:, k, n],
                                            hi[:, k, n].bitcast(F32), ALU.subtract)\
                        .then_inc(lo_done[k], 1)

            for k in range(4):
                take_lo(0, k, True)
            with pool.Fori(1, ROUNDS) as i:
                for k in range(4):
                    take_lo(i, k, False)

        @block.scalar
        def _(act):
            chain = Chain(act, ach)
            act.dma_start(cons_sb[:], cons).then_inc(got_const, 16)
            act.dma_start(cols_sb[:], cols).then_inc(got_const, 16)
            for tt in range(TT):
                act.dma_start(hx[:, tt, :], x[tt * P:(tt + 1) * P, :]).then_inc(got_x, 16)

            def take_hi(i, k, first=False):
                act.wait_ge(loaded[k], i * 16 + 16)
                if not first:
                    act.wait_ge(unit_used, i * 4 + (k - 3))
                nc.scalar.activation(hi[:, k, :], raw[:, k, :], ACT.Copy).then_inc(hi_done, 1)

            def norm(n, gain, partial=False):
                for tt in range(TT):
                    if n == 0:
                        if tt == 0:
                            act.wait_ge(got_x, 16 * TT)
                    else:
                        act.wait_ge(h_new, 2 * (n - 1) + tt + 1)
                    nc.scalar.activation(xn[:, tt, :], hx[:, tt, :], ACT.Square,
                                         accum_out=st(SS + tt)).then_inc(ss_done, 1)
                act.wait_ge(ms_done, n + 1)
                nc.scalar.activation(st(RT, 2), st(MS, 2), ACT.Sqrt).then_inc(rms_done, 1)
                for kb in range(KB):
                    act.wait_ge(tr_done, 16 * n + kb + 1)
                    nc.scalar.activation(xh[:, kb, :], tr_slot(kb % 8), ACT.Copy,
                                         scale=col(gain, kb)).then_inc(x_hi, 1)

            act.wait_ge(got_const, 32)
            lam = col("lam", 0, 16)
            chain.link(nc.scalar.activation(st(LAMW, 16), lam, ACT.Abs))
            nc.scalar.activation(st(LAMW, 16), st(LAMW, 16), ACT.Exp, scale=-1.0).then_inc(soft_e, 1)
            for k in range(4):
                take_hi(0, k, True)
            norm(0, "g_mix")
            act.wait_ge(tr_done, 16)
            act.dma_start(wg[:], w_gates).then_inc(got_wg, 16)
            act.dma_start(band_sb[:], band).then_inc(got_wg, 16)

            def tanh_group(g, n):
                z, which = g // 2, g % 2
                if n == 0:
                    act.wait_ge(gates_done, g + 1)
                    if g == 0:
                        act.wait_ge(soft_c, 1)
                to = (th_a, th_i)[which][:, z, n, :]
                nc.scalar.activation(to, ps[:, 4 + n // 2, (n % 2) * T:(n % 2) * T + T], ACT.Tanh,
                                     scale=0.5, bias=st(BA2 + 16 * which + 8 * z + n))\
                    .then_inc(tanh_done, 1)

            def decay(z, n):
                c, t = 8 * z + n, (t_z0, t_z1)[z]
                if n == 0:
                    act.wait_ge(tanh_done, 16 * z + 8)
                    act.wait_ge(conv_done, 8)
                nc.scalar.activation(t[:, n, :], th_a[:, z, n, :], ACT.Tanh, scale=st(CSP + c),
                                     bias=st(CSP + c)).then_inc(ach, 1)
                chain.n += 1
                chain.wait()
                nc.scalar.activation(th_a[:, z, n, :], th_a[:, z, n, :], ACT.Exp,
                                     scale=st(CSP + 16 + c), bias=st(CSP + 16 + c))\
                    .then_inc(decay_done, 1)

            def root(z):
                t = (t_z0, t_z1)[z]
                act.wait_ge(z_done, z + 1)
                nc.scalar.activation(t[:], t[:], ACT.Sqrt).then_inc(sqrt_done, 1)

            def gelu(b):
                act.wait_ge(unit_used, after("in1", 66 + 2 * b))
                nc.scalar.activation(yg[:, b, :], t_bank(b % 4), ACT.Gelu_apprx_tanh)\
                    .then_inc(free_a, 1)

            tasks = {}
            for g, u0 in enumerate((27, 35, 43, 51)):
                for n in range(8):
                    tasks.setdefault(u0 + n // 2, []).append((tanh_group, g, n))
            for z, u0 in enumerate((39, 55)):
                for n in range(8):
                    tasks.setdefault(u0 + n // 2, []).append((decay, z, n))
            tasks.setdefault(66, []).extend([(root, 0), (root, 1)])
            for b in range(8):
                tasks.setdefault(2 * b + 69, []).append((gelu, b))
            for u in range(4, 80):
                take_hi(u // 4, u % 4)
                for f, *a in tasks.pop(u, []):
                    f(*a)
            for u in sorted(tasks):
                for f, *a in tasks[u]:
                    f(*a)
            act.wait_ge(gates_done, 4)
            act.dma_start(bias[:], rpb).then_inc(got_bias, 16)

            def attend(n0, heads, slots, times):
                s_sb, p_sb_, pt = slots

                def exps(h):
                    n = n0 + h
                    act.wait_ge(at_m, n + 1)
                    for qt in range(TT):
                        if times is None:
                            ins = nc.scalar.activation(
                                p_sb_[:, h % 2, qt, :], s_sb[:, h % 2, qt, :], ACT.Exp,
                                bias=st(NM + 2 * (h % 4) + qt),
                                accum_out=st(SM + 2 * (h % 4) + qt))
                        else:
                            ins = nc.scalar.activation(
                                p_sb_[:, h % 2, qt, :], s_sb[:, h % 2, qt, :], ACT.Exp,
                                bias=st(NM + 2 * (h % 4) + qt))
                    ins.then_inc(at_e, 1)

                def copy_turned(h):
                    n = n0 + h
                    act.wait_ge(at_t, n + 1)
                    if h >= 2:
                        act.wait_ge(at_o, n - 1)
                    nc.scalar.activation(pt[:, h % 2, :, :],
                                         ps[:, 6, :].rearrange("p (a b) -> p a b", a=2),
                                         ACT.Copy).then_inc(at_c, 1)
                    if times is not None:
                        act.wait_ge(at_o, n + 1)
                        nc.scalar.activation(xh[:, 4 + h, :], ps[:, 7, 0:T], ACT.Copy)\
                            .then_inc(x_hi, 1)

                exps(0)
                for h in range(heads):
                    if h + 1 < heads:
                        exps(h + 1)
                    copy_turned(h)

            attend(0, HEADS1, at1, None)
            for branch in range(2):
                act.wait_ge(mo_ms, branch + 1)
                nc.scalar.activation(mo_r[:, branch, :], mo_r[:, branch, :], ACT.Sqrt)\
                    .then_inc(mo_rt, 1)
            for kb in range(KB):
                act.wait_ge(mo_ready, 1 + kb // 8)
                src = attn_t[:, kb, :] if kb < 8 else xc[:, kb - 8, :]
                nc.scalar.activation(xh[:, kb, :], src, ACT.Copy, scale=col("g_mo", kb))\
                    .then_inc(x_hi, 1)
            act.wait_ge(x_lo, 32)
            act.dma_start(gbc[:], gains[0]).then_inc(got_gain, 16)

            def post_squares(name, n):
                per = 22 if name == "down" else 8
                a0 = {"out1": 8, "down": 56}[name]

                def squares(where):
                    pair = where % 2
                    act.wait_ge(unit_used, after(name, per * (where + 1)))
                    if where >= 2:
                        act.wait_ge(free_a, a0 + where - 1)
                    for tt in range(TT):
                        ins = nc.scalar.activation(ps[:, 4 + 2 * pair + tt, :],
                                                   ps[:, 2 * pair + tt, :],
                                                   ACT.Square, accum_out=st(SSP + 4 * tt + where))
                    ins.then_inc(free_a, 1)
                return squares

            squares = post_squares("out1", 0)
            r0 = ROUND0["out1"]
            for c in range(4):
                for k in range(4):
                    take_hi(r0 + 2 * c, k)
                if c:
                    squares(c - 1)
                for k in range(4):
                    take_hi(r0 + 2 * c + 1, k)
            squares(3)

            def post_root(n):
                act.wait_ge(act_post, 2 * n + 1)
                nc.scalar.activation(st(RT, 2), st(MS, 2), ACT.Sqrt).then_inc(act_post, 1)

            post_root(0)
            norm(1, "g_ffn")

            r0 = ROUND0["ffn"]

            def silu(f, s):
                act.wait_ge(unit_used, f * 4 + after("ffn", 2))
                act.wait_ge(prod_done, f - 1) if not isinstance(f, int) or f >= 2 else None
                nc.scalar.activation(sil[:, s, :], t_bank(2 * s), ACT.Silu).then_inc(free_a, 1)

            def ffn_pair(f0, r, first=False, last=False):
                for k in range(4):
                    take_hi(r, k)
                if not first:
                    silu(f0 - 1, 1)
                for k in range(4):
                    take_hi(r + 1, k)
                silu(f0, 0)
                if last:
                    silu(f0 + 1, 1)

            ffn_pair(0, r0, first=True)
            with act.Fori(1, FB // 2 - 1) as i:
                ffn_pair(i * 2, i * 2 + r0)
            ffn_pair(FB - 2, r0 + FB - 2, last=True)
            act.dma_start(gbc[:], gains[1]).then_inc(got_gain, 16)
            squares = post_squares("down", 1)
            r0 = ROUND0["down"]
            for c in range(4):
                with act.Fori(0, 5) as i:
                    for k in range(4):
                        q = 22 * c + k
                        take_hi(i + (r0 + q // 4), q % 4)
                for u in range(22 * c + 20, 22 * c + 22):
                    take_hi(r0 + u // 4, u % 4)
                if c:
                    squares(c - 1)
            squares(3)
            act.dma_start(w_pr[:], w_proj).then_inc(got_ple, 16)
            act.dma_start(p_sb[:], p_t).then_inc(got_ple, 16)
            act.dma_start(wgd[:], w_gd).then_inc(got_in2, 16)
            act.dma_start(up[:], up_fb).then_inc(got_in2, 16)
            act.dma_start(qkg[:], qk_gain).then_inc(got_in2, 16)
            post_root(1)
            norm(2, "g_ple")
            act.wait_ge(h_new, 4)
            act.dma_start(gbc[:], gains[2]).then_inc(got_gain, 16)
            r0 = ROUND0["gate"]

            def sigmoids(c):
                act.wait_ge(unit_used, after("gate", 8 * c + 8))
                if c >= 2:
                    act.wait_ge(ple_free, c - 1)
                for tt in range(TT):
                    ins = nc.scalar.activation(sig[:, c % 2, tt, :], ps[:, 2 * (c % 2) + tt, :],
                                               ACT.Sigmoid)
                ins.then_inc(free_a, 1)

            for c in range(4):
                for k in range(4):
                    take_hi(r0 + 2 * c, k)
                if c:
                    sigmoids(c - 1)
                for k in range(4):
                    take_hi(r0 + 2 * c + 1, k)
            sigmoids(3)
            post_root(2)
            norm(3, "g_n1")

            def log_sigmoid_parts():
                act.wait_ge(g_pe, 3)
                for m in range(4):
                    ins = nc.scalar.activation(g1[:, m, :], tr_slot(4 + m), ACT.Abs,
                                               bias=col("gla_b", m))
                chain.link(ins)
                chain.link(nc.scalar.activation(g1[:], g1[:], ACT.Exp, scale=-1.0))
                nc.scalar.activation(g1[:], g1[:], ACT.Ln, bias=1.0).then_inc(g_act, 1)

            def last_of(d):
                v = g1[:, 2 * d:2 * d + 2, :].rearrange("p m (c t) -> p m c t", t=64)
                return v[:, :, :, 63 if d == 0 else 0]

            def decays():
                act.wait_ge(g_dve, 4)
                nc.scalar.activation(g2[:], g1[:], ACT.Exp, scale=1.0 / 16)
                nc.scalar.activation(g3[:], g1[:], ACT.Exp, scale=-1.0 / 16)
                for d in range(2):
                    nc.scalar.activation(st(GDEC + 8 * d, 8).rearrange("p (m c) -> p m c", c=4),
                                         last_of(d), ACT.Exp, scale=1.0 / 16)
                nc.scalar.activation(g4[:], g4[:], ACT.Exp, scale=1.0 / 16).then_inc(g_act, 1)

            def silu_r():
                act.wait_ge(unit_used, after("in2", 24))
                for tt in range(TT):
                    ins = nc.scalar.activation(sra[:, tt, :], ps[:, 2 + tt, :], ACT.Silu)
                ins.then_inc(free_a, 1)

            def qk_squares(c):
                act.wait_ge(unit_used, after("in2", 32 + 8 * c))
                if c:
                    act.wait_ge(qk_reduced, c)
                if c == 4:
                    act.wait_ge(qk_ready, 1)
                for tt in range(TT):
                    ins = nc.scalar.activation(sqt[:, tt, :], ps[:, 2 * (c % 2) + tt, :],
                                               ACT.Square)
                ins.then_inc(free_a, 1)

            def qk_root(which):
                act.wait_ge(qk_ms, which + 1)
                nc.scalar.activation(st(SRT, 24), st(SRT, 24), ACT.Sqrt).then_inc(qk_rt, 1)

            def o_squares():
                act.wait_ge(g_dve, 10)
                nc.scalar.activation(g3[:], o_n[:].rearrange("p a (b c) -> p (a b) c", c=T),
                                     ACT.Square).then_inc(g_act, 1)

            def o_root():
                act.wait_ge(g_dve, 11)
                nc.scalar.activation(st(GRT, 8), st(GRT, 8), ACT.Sqrt).then_inc(g_act, 1)

            def q_copy(h):
                act.wait_ge(qk_turned, h + 1)
                nc.scalar.activation(q_t2[:, h, :], tr_slot(h % 8), ACT.Copy).then_inc(q_copied, 1)

            act.wait_ge(got_in2, 48)
            nc.scalar.activation(wgd_h[:], wgd[:], ACT.Copy).then_inc(g_act, 1)
            tasks = {11: [(log_sigmoid_parts,)], 15: [(decays,)], 27: [(silu_r,)],
                     61: [(qk_root, 0)], 69: [(o_squares,)], 72: [(o_root,)], 83: [(qk_root, 1)]}
            for c in range(6):
                tasks[35 + 8 * c] = [(qk_squares, c)]
            for h in range(HEADS2):
                tasks[75].append((q_copy, h))
            for u in range(96):
                take_hi(ROUND0["in2"] + u // 4, u % 4)
                for f, *a in tasks.get(u, []):
                    f(*a)
            act.wait_ge(g_pe, 8)
            act.dma_start(dil_sb[:], dil).then_inc(got_dil, 16)
            for kb in range(4):
                act.wait_ge(g_pe, 9 + kb)
                nc.scalar.activation(xh[:, kb, :], tr_slot(kb), ACT.Copy, scale=col("g_gla", kb))\
                    .then_inc(x_hi, 1)
            attend(HEADS1, HEADS2, at2, dil_sb)
            act.dma_start(keys_t[:], sub_keys).then_inc(got_keys, 16)
            with act.Fori(0, 8) as i:
                for k in range(4):
                    take_hi(i + ROUND0["out2"], k)
            norm(4, "g_n2")
            act.dma_start(spill, hx[:]).then_inc(spilled, 16)
            with act.Fori(0, 8) as i:
                for k in range(4):
                    take_hi(i + ROUND0["query"], k)
            act.wait_ge(spilled, 16)

            def expert_gelu(j, bank):
                act.wait_ge(unit_used, j * 2 + after("peer_down", 2))
                to = gm[:, j, :] if isinstance(j, int) else \
                    gm[:, bass.ds(j, 1), :].rearrange("p a t -> p (a t)")
                nc.scalar.activation(to, t_bank(bank), ACT.Gelu_apprx_tanh).then_inc(free_a, 1)

            r0 = ROUND0["peer_down"]

            def gelu_rounds(j0, r, first=False):
                for half in range(2):
                    for k in range(2):
                        take_hi(r + half, k)
                    if not (first and half == 0):
                        expert_gelu(j0 + (2 * half - 1), (2 * half - 1) % 4)
                    for k in range(2, 4):
                        take_hi(r + half, k)
                    expert_gelu(j0 + 2 * half, 2 * half)

            gelu_rounds(0, r0, True)
            with act.Fori(1, 7) as i:
                gelu_rounds(i * 4, i * 2 + r0)
            act.wait_ge(route_m, 1)
            nc.scalar.activation(route[:, 2, :], route[:, 2, :], ACT.Exp).then_inc(route_e, 1)
            with act.Fori(7, 16) as i:
                gelu_rounds(i * 4, i * 2 + r0)
            act.wait_ge(routed, 1)
            with act.Fori(16, 32) as i:
                gelu_rounds(i * 4, i * 2 + r0)
            expert_gelu(127, 3)
            r0 = ROUND0["peer_up"]
            act.wait_ge(unit_used, after("peer_up", 0))
            act.dma_start(hx_end[:], spill).then_inc(got_h, 16)

            def up_round(i, first=False, half=0):
                for k in range(4):
                    if not first:
                        act.wait_ge(unit_used, i * 4 + after("peer_up", k - 3))
                    j = i * 4 + (k - half * NKEY)
                    h = gm[:, j, :] if isinstance(j, int) else \
                        gm[:, bass.ds(j, 1), :].rearrange("p a t -> p (a t)")
                    nc.scalar.activation(hg_h[:, k, :], h, ACT.Copy).then_inc(hh_done, 1)
                    take_hi(i + r0, k)

            act.wait_ge(gated_done, T // 8)
            up_round(0, True)
            with act.Fori(1, 16) as i:
                up_round(i)
            act.wait_ge(gated_done, T // 4)
            with act.Fori(16, 32) as i:
                up_round(i)
            with act.Fori(32, 64) as i:
                up_round(i, half=1)

        @block.vector
        def _(dve):
            chain = Chain(dve, dch)
            link = chain.link
            V = nc.vector

            def norm(n, gain):
                dve.wait_ge(ss_done, 2 * n + 2)
                V.tensor_scalar(st(MS, 2), st(SS, 2), 1.0 / D, EPS, ALU.mult, ALU.add)\
                    .then_inc(ms_done, 1)
                dve.wait_ge(rms_done, n + 1)
                link(V.reciprocal(st(RI, 2), st(RT, 2)))
                for tt in range(TT):
                    V.tensor_scalar(xn[:, tt, :], hx[:, tt, :], st(RI + tt), None, ALU.mult)\
                        .then_inc(xn_done, 1)
                for kb in range(KB):
                    dve.wait_ge(x_hi, 16 * BUILD[n] + kb + 1)
                    V.scalar_tensor_tensor(out=xl[:, kb, :], in0=tr_slot(kb % 8),
                                           scalar=col(gain, kb), in1=xh[:, kb, :].bitcast(F32),
                                           op0=ALU.mult, op1=ALU.subtract).then_inc(x_lo, 1)

            BUILD = [0, 2, 3, 4, 6]

            V.memset(xr[:, :, 0:2], 0.0).then_inc(dch, 1)
            V.memset(xr[:, :, 258:260], 0.0).then_inc(dch, 1)
            chain.n += 2
            dve.wait_ge(got_const, 32)
            dve.wait_ge(soft_e, 1)
            e, s, s2, acc = (st(LAMW + 16 * i, 16) for i in range(4))
            link(V.tensor_scalar(s, e, 2.0, None, ALU.add))
            link(V.reciprocal(s, s))
            link(V.tensor_tensor(s, s, e, ALU.mult))
            link(V.tensor_tensor(s2, s, s, ALU.mult))
            link(V.tensor_scalar(acc, s2, 2.0 / 15, 2.0 / 13, ALU.mult, ALU.add))
            for odd in (11, 9, 7, 5, 3, 1):
                link(V.tensor_tensor(acc, acc, s2, ALU.mult))
                link(V.tensor_scalar(acc, acc, 2.0 / odd, None, ALU.add))
            link(V.tensor_tensor(acc, acc, s, ALU.mult))
            link(V.tensor_scalar(s, col("lam", 0, 16), -1.0, 0.0, ALU.mult, ALU.max))
            link(V.tensor_tensor(acc, acc, s, ALU.add))
            V.tensor_scalar(st(CSP, 16), acc, 4.0, None, ALU.mult).then_inc(dch, 1)
            V.tensor_scalar(st(CSP + 16, 16), acc, -4.0, None, ALU.mult).then_inc(dch, 1)
            V.tensor_scalar(st(BA2, 32), col("b_a", 0, 32), 0.5, None, ALU.mult).then_inc(dch, 1)
            chain.n += 3
            chain.wait()
            V.memset(st(LAMW), 0.0).then_inc(soft_c, 1)

            norm(0, "g_mix")

            def block_copy(b, to, scale=None):
                dve.wait_ge(unit_used, after("in1", 2 * b + 2))
                if scale is None:
                    ins = V.tensor_copy(to, t_bank(b % 4))
                else:
                    ins = V.tensor_scalar(to, t_bank(b % 4), scale, None, ALU.mult)
                ins.then_inc(free_d, 1)
                return ins

            for n in range(8):
                block_copy(n, xr[:, n, 2:258])
                dve.wait_ge(free_d, n + 1)
                link(V.tensor_scalar(xc[:, n, :], xr[:, n, 0:T], col("conv_w", n),
                                     col("conv_b", n), ALU.mult, ALU.add))
                for j in range(1, 4):
                    ins = V.scalar_tensor_tensor(out=xc[:, n, :], in0=xr[:, n, j:j + T],
                                                 scalar=col("conv_w", 8 * j + n),
                                                 in1=xc[:, n, :], op0=ALU.mult, op1=ALU.add)
                    if j < 3:
                        link(ins)
                    else:
                        ins.then_inc(conv_done, 1)
            for b in range(8):
                block_copy(8 + b, q_t[:, b, :], SCALE)
            for b in range(4):
                block_copy(16 + b, k_t[:, b, :])

            def z_step(z):
                t = (t_z0, t_z1)[z]
                dve.wait_ge(decay_done, 8 * z + 8)
                dve.wait_ge(tanh_done, 16 * z + 16)
                dve.wait_ge(conv_done, 8)
                sq = yg
                link(V.tensor_tensor(sq[:], th_a[:, z], th_a[:, z], ALU.mult))
                V.scalar_tensor_tensor(out=t[:], in0=sq[:], scalar=1.0, in1=t[:], op0=ALU.add,
                                       op1=ALU.mult).then_inc(z_done, 1)
                link(V.scalar_tensor_tensor(out=th_i[:, z], in0=th_i[:, z], scalar=1.0, in1=xc[:],
                                            op0=ALU.add, op1=ALU.mult))
                dve.wait_ge(z_done, z + 1)

            z_step(0)
            for b in range(4, 8):
                block_copy(16 + b, k_t[:, b, :])

            def v_copy(c):
                dve.wait_ge(unit_used, after("in1", 56 + 8 * c))
                for tt in range(TT):
                    ins = V.tensor_copy(v_n[:, tt, c * NCH:(c + 1) * NCH], ps[:, 2 * c + tt, :])
                ins.then_inc(free_d, 1)

            v_copy(0)
            z_step(1)
            v_copy(1)
            for z in range(2):
                t = (t_z0, t_z1)[z]
                dve.wait_ge(sqrt_done, z + 1)
                link(V.scalar_tensor_tensor(out=t[:], in0=t[:], scalar=0.5, in1=th_i[:, z],
                                            op0=ALU.mult, op1=ALU.mult))
                for n in range(8):
                    if z == 0:
                        a, b, o = th_a[:, z, n, :], t[:, n, :], th_i[:, z, n, :]
                    else:
                        a, b, o = (m[:, n, ::-1] for m in (th_a[:, z], t, th_i[:, z]))
                    chain.inc(V.tensor_tensor_scan(o, a, b, 0.0, ALU.mult, ALU.add))
            chain.wait()
            link(V.tensor_tensor(th_i[:, 0], th_i[:, 0], th_i[:, 1], ALU.add))
            dve.wait_ge(free_a, 8)
            link(V.tensor_tensor(xc[:], th_i[:, 0], yg[:], ALU.mult))
            V.tensor_tensor(th_i[:, 1], xc[:], xc[:], ALU.mult).then_inc(mo_sq, 1)
            dve.wait_ge(got_bias, 16)
            dve.wait_ge(got_wg, 32)
            for h in range(HEADS1):
                chain.inc(V.tensor_tensor(
                    bias[:, h].rearrange("p a (r c) -> p (a r) c", c=64),
                    bias[:, h].rearrange("p a (r c) -> p (a r) c", c=64),
                    band_sb[:].unsqueeze(1).to_broadcast([P, 8, 64]), ALU.add))

            def attend(n0, heads, slots, bias_of, times, copy_out):
                s_sb, p_sb_, pt = slots

                def first(h):
                    n = n0 + h
                    dve.wait_ge(at_s, n + 1)
                    if h >= 2:
                        dve.wait_ge(at_e, n - 1)
                    V.tensor_tensor(s_sb[:, h % 2], ps[:, 4 + h % 2, :].rearrange(
                        "p (a b) -> p a b", a=2), bias_of(h), ALU.add).then_inc(at_b, 1)
                    dve.wait_ge(at_b, n + 1)
                    V.tensor_reduce(st(NM + 2 * (h % 4), 2), s_sb[:, h % 2], AX.X, ALU.max,
                                    negate=True).then_inc(at_m, 1)

                def second(h):
                    n = n0 + h
                    dve.wait_ge(at_e, n + 1)
                    sm, si = SM + 2 * (h % 4), SI + 2 * (h % 4)
                    if times is not None:
                        for qt in range(TT):
                            chain.inc(V.scalar_tensor_tensor(
                                out=p_sb_[:, h % 2, qt], in0=p_sb_[:, h % 2, qt], scalar=1.0,
                                in1=times[:, qt], op0=ALU.mult, op1=ALU.mult,
                                accum_out=st(sm + qt)))
                        chain.wait()
                    link(V.reciprocal(st(si, 2), st(sm, 2)))
                    for qt in range(TT):
                        ins = V.tensor_scalar(p_sb_[:, h % 2, qt], p_sb_[:, h % 2, qt],
                                              st(si + qt), None, ALU.mult)
                        if qt == 0:
                            chain.inc(ins)
                    ins.then_inc(at_p, 1)

                first(0)
                for h in range(heads):
                    if h + 1 < heads:
                        first(h + 1)
                    second(h)
                    if h:
                        copy_out(h - 1)
                copy_out(heads - 1)

            def head_out(h):
                dve.wait_ge(at_o, h + 1)
                V.tensor_copy(attn_t[:, h, :], ps[:, 7, 0:T]).then_inc(at_f, 1)

            chain.wait()
            attend(0, HEADS1, at1, lambda h: bias[:, h], None, head_out)
            dve.wait_ge(at_f, HEADS1)
            dve.wait_ge(at_o, HEADS1)
            sqa = th_a[:, 1]
            V.tensor_tensor(sqa, attn_t[:], attn_t[:], ALU.mult).then_inc(mo_sq, 1)
            for branch in range(2):
                dve.wait_ge(mo_sum, branch + 1)
                V.tensor_scalar(mo_r[:, branch, :], ps[:, 4 + branch, 0:T], 1.0 / 1024, EPS,
                                ALU.mult, ALU.add).then_inc(mo_ms, 1)
            for branch in (1, 0):
                dve.wait_ge(mo_rt, branch + 1)
                link(V.reciprocal(mo_r[:, branch, :], mo_r[:, branch, :]))
                m = (xc, attn_t)[branch]
                V.tensor_tensor(m[:], m[:], mo_r[:, branch, :].unsqueeze(1).to_broadcast([P, 8, T]),
                                ALU.mult).then_inc(mo_ready, 1)
            for kb in range(KB):
                dve.wait_ge(x_hi, 16 + kb + 1)
                src = attn_t[:, kb, :] if kb < 8 else xc[:, kb - 8, :]
                V.scalar_tensor_tensor(out=xl[:, kb, :], in0=src, scalar=col("g_mo", kb),
                                       in1=xh[:, kb, :].bitcast(F32), op0=ALU.mult,
                                       op1=ALU.subtract).then_inc(x_lo, 1)

            def post_chunks(name, n):
                dve.wait_ge(got_gain, 16 * (n + 1))
                for c in range(4):
                    dve.wait_ge(free_a, {"out1": 8, "down": 56}[name] + c + 1)
                    for tt in range(TT):
                        ins = V.tensor_tensor(y[:, tt, c * NCH:(c + 1) * NCH],
                                              ps[:, 2 * (c % 2) + tt, :],
                                              gbc[:, c * NCH:(c + 1) * NCH], ALU.mult)
                        if tt == 0:
                            chain.inc(ins)
                    ins.then_inc(free_d, 1)
                chain.wait()

            def post(n, frees):
                dve.wait_ge(free_d, frees)
                link(V.tensor_reduce(st(SS, 2), st(SSP, 8).rearrange("p (a b) -> p a b", a=2),
                                     AX.X, ALU.add))
                V.tensor_scalar(st(MS, 2), st(SS, 2), 1.0 / D, EPS, ALU.mult, ALU.add)\
                    .then_inc(act_post, 1)
                dve.wait_ge(act_post, 2 * n + 2)
                link(V.reciprocal(st(RI, 2), st(RT, 2)))
                for tt in range(TT):
                    V.scalar_tensor_tensor(out=hx[:, tt], in0=y[:, tt], scalar=st(RI + tt),
                                           in1=hx[:, tt], op0=ALU.mult, op1=ALU.add)\
                        .then_inc(h_new, 1)

            post_chunks("out1", 0)
            dve.wait_ge(free_a, 12)
            post(0, 30)
            norm(1, "g_ffn")

            def hidden(f, s, first=False):
                dve.wait_ge(unit_used, f * 4 + after("ffn", 4))
                dve.wait_ge(free_a, f + 13)
                V.tensor_tensor(prod[:, s, :], t_bank(2 * s + 1), sil[:, s, :], ALU.mult)\
                    .then_inc(prod_done, 1)
                dve.wait_ge(prod_done, f + 1)
                V.tensor_copy(hid_h[:, bass.ds(f, 1), :].rearrange("p a t -> p (a t)")
                              if not isinstance(f, int) else hid_h[:, f, :], prod[:, s, :])\
                    .then_inc(hid_hi, 1)
                dve.wait_ge(hid_hi, f + 1)
                V.tensor_tensor(hid_l[:, bass.ds(f, 1), :].rearrange("p a t -> p (a t)")
                                if not isinstance(f, int) else hid_l[:, f, :], prod[:, s, :],
                                (hid_h[:, bass.ds(f, 1), :].rearrange("p a t -> p (a t)")
                                 if not isinstance(f, int) else hid_h[:, f, :]).bitcast(F32),
                                ALU.subtract).then_inc(free_d, 1)
                dve.wait_ge(free_d, f + 31)

            with dve.Fori(0, FB // 2) as i:
                for s in range(2):
                    hidden(i * 2 + s, s)
            post_chunks("down", 1)
            dve.wait_ge(free_a, 60)
            post(1, 78)
            norm(2, "g_ple")
            dve.wait_ge(got_gain, 48)
            for c in range(4):
                dve.wait_ge(free_a, 60 + c + 1)
                dve.wait_ge(ple_done, c + 1)
                for tt in range(TT):
                    chain.inc(V.tensor_tensor(pz[:, tt, :], ps[:, 4 + 2 * (c % 2) + tt, :],
                                              sig[:, c % 2, tt, :], ALU.mult))
                chain.wait()
                for tt in range(TT):
                    link(V.scalar_tensor_tensor(out=junk[:], in0=pz[:, tt, :], scalar=1.0,
                                                in1=pz[:, tt, :], op0=ALU.mult, op1=ALU.mult,
                                                accum_out=st(SSP + 4 * tt + c)))
                    link(V.tensor_tensor(y[:, tt, c * NCH:(c + 1) * NCH], pz[:, tt, :],
                                         gbc[:, c * NCH:(c + 1) * NCH], ALU.mult))
                V.memset(junk[:, 0:1], 0.0).then_inc(ple_free, 1)
                dve.wait_ge(ple_free, c + 1)
            post(2, 78)
            norm(3, "g_n1")

            dve.wait_ge(g_act, 1)
            V.tensor_tensor(wgd_l[:], wgd[:], wgd_h[:].bitcast(F32), ALU.subtract).then_inc(g_dve, 1)
            dve.wait_ge(g_pe, 1)
            V.tensor_copy(gd_n[:], ps[:, 4, 0:64].rearrange("p (a b) -> p a b", a=2))\
                .then_inc(g_dve, 1)

            def t_copy(b, to):
                dve.wait_ge(unit_used, after("in2", 2 * b + 2))
                V.tensor_copy(to, t_bank(b)).then_inc(free_d, 1)

            t_copy(0, qa_t[:, 0, :])
            t_copy(1, qa_t[:, 1, :])
            dve.wait_ge(g_pe, 2)
            V.tensor_copy(gd_t[:], ps[0:32, 5, 0:T]).then_inc(g_dve, 1)
            t_copy(2, ka_t[:, 0, :])
            t_copy(3, ka_t[:, 1, :])
            dve.wait_ge(g_act, 2)
            for m in range(4):
                chain.inc(V.tensor_scalar(g2[:, m, :], tr_slot(4 + m), col("gla_b", m), 0.0,
                                          ALU.add, ALU.min))
            chain.wait()
            link(V.tensor_tensor(g2[:], g2[:], g1[:], ALU.subtract))
            for m in range(4):
                if m < 2:
                    o, a = g1[:, m, :], g2[:, m, :]
                else:
                    o, a = g1[:, m, ::-1], g2[:, m, ::-1]
                chain.inc(V.tensor_tensor_scan(o, con("scan"), a, 0.0, ALU.mult, ALU.add))
            chain.wait()
            for d in range(2):
                v = g1[:, 2 * d:2 * d + 2, :].rearrange("p m (c t) -> p (m c) t", t=64)
                at_end = v[:, :, 63:64] if d == 0 else v[:, :, 0:1]
                ins = V.tensor_tensor(
                    g4[:, 2 * d:2 * d + 2, :].rearrange("p m (c t) -> p (m c) t", t=64),
                    at_end.to_broadcast([P, 8, 64]), v, ALU.subtract)
                if d == 0:
                    chain.inc(ins)
            ins.then_inc(g_dve, 1)

            def n_copy(n, to):
                dve.wait_ge(unit_used, after("in2", 16 + 8 * n))
                for tt in range(TT):
                    ins = V.tensor_copy(to(tt), ps[:, 2 * (n % 2) + tt, :])
                ins.then_inc(free_d, 1)

            def qk_chunk(c):
                dve.wait_ge(free_a, 66 + c)
                n_copy(2 + c, lambda tt: qk_n[c // 3][:, tt, (c % 3) * NCH:(c % 3 + 1) * NCH])

            def qk_reduce(c):
                dve.wait_ge(free_a, 66 + c)
                for tt in range(TT):
                    ins = V.tensor_reduce(st(SSQ + 24 * (c // 3) + 12 * tt + 4 * (c % 3), 4),
                                          sqt[:, tt, :].rearrange("p (h e) -> p h e", e=HD),
                                          AX.X, ALU.add)
                    if tt == 0:
                        chain.inc(ins)
                ins.then_inc(qk_reduced, 1)

            def qk_mean(which):
                dve.wait_ge(qk_reduced, 3 * which + 3)
                if which:
                    dve.wait_ge(qk_ready, 1)
                V.tensor_scalar(st(SRT, 24), st(SSQ + 24 * which, 24), 1.0 / HD, EPS, ALU.mult,
                                ALU.add).then_inc(qk_ms, 1)

            def qk_normalise(which):
                dve.wait_ge(qk_rt, which + 1)
                inv = st(SSQ + 24 * which, 24)
                link(V.reciprocal(inv, st(SRT, 24)))
                if which == 0:
                    link(V.tensor_scalar(inv, inv, SCALE, None, ALU.mult))
                full = qk_n[which][:].rearrange("p a (h e) -> p (a h) e", e=HD)
                link(V.tensor_tensor(full, full, inv.unsqueeze(2).to_broadcast([P, 24, HD]),
                                     ALU.mult))
                link(V.tensor_tensor(full, full, qkg[:, which, :].unsqueeze(1).to_broadcast(
                    [P, 24, HD]), ALU.mult))
                for tt in range(TT):
                    v = qk_n[which][:, tt, :].rearrange("p (h e) -> p h e", e=HD)
                    x1, x2 = v[:, :, 0:16], v[:, :, 16:32]
                    cos, sin = (con(n)[:, 16 * tt:16 * tt + 16].unsqueeze(1).to_broadcast(
                        [P, 12, 16]) for n in ("cos", "sin"))
                    for k, (a, b) in enumerate(((x1, cos), (x2, sin), (x2, cos), (x1, sin))):
                        chain.inc(V.tensor_tensor(rope_t[:, k], a, b, ALU.mult))
                    chain.wait()
                    chain.inc(V.tensor_tensor(x1, rope_t[:, 0], rope_t[:, 1], ALU.subtract))
                    ins = V.tensor_tensor(x2, rope_t[:, 2], rope_t[:, 3], ALU.add)
                    if tt == 0:
                        link(ins)
                ins.then_inc(qk_ready, 1)

            n_copy(0, lambda tt: va[:, tt, :])
            dve.wait_ge(g_act, 3)
            for d in range(2):
                h = slice(2 * d, 2 * d + 2)
                chain.inc(V.scalar_tensor_tensor(
                    out=g2[:, h, :], in0=g2[:, h, :], scalar=64 ** -0.5, in1=qa_t[:], op0=ALU.mult,
                    op1=ALU.mult))
                chain.inc(V.tensor_tensor(g3[:, h, :], g3[:, h, :], ka_t[:], ALU.mult))
                ins = V.tensor_tensor(g4[:, h, :], g4[:, h, :], ka_t[:], ALU.mult)
                if d == 0:
                    chain.inc(ins)
            ins.then_inc(g_dve, 1)
            qk_chunk(0)
            dve.wait_ge(g_pe, 4)
            link(V.tensor_scalar(sc_t[:], ps[:, 4:8, :], 3e38, -3e38, ALU.min, ALU.max))
            for b in range(4):
                v = sc_t[:, b, :].rearrange("p (d h q) -> p d h q", d=2, h=2)
                ins = V.tensor_tensor(v, v, con("causal").rearrange("p (d q) -> p d q", d=2)
                                      .unsqueeze(2).to_broadcast([P, 2, 2, P]), ALU.mult)
                if b < 3:
                    chain.inc(ins)
            ins.then_inc(g_dve, 1)
            qk_reduce(0)
            qk_chunk(1)
            qk_reduce(1)
            dve.wait_ge(g_pe, 5)
            V.tensor_copy(kst[:].rearrange("p a m k -> p a (m k)"), ps[:, 4:6, :]).then_inc(g_dve, 1)
            qk_chunk(2)
            qk_reduce(2)
            qk_mean(0)

            def states(d):
                dve.wait_ge(g_pe, 6 + d)
                for n in range(3):
                    c = n if d == 0 else 3 - n
                    for half in range(2):
                        at, m = inc_at(d, c, half), 2 * d + half
                        for hd in range(2):
                            rows = slice(64 * hd, 64 * hd + 64)
                            add = at[rows, hd * P:(hd + 1) * P]
                            new = state[rows, d, n, half, :]
                            if n == 0:
                                ins = V.tensor_copy(new, add)
                            else:
                                ins = V.scalar_tensor_tensor(
                                    out=new, in0=state[rows, d, n - 1, half, :],
                                    scalar=small[rows, GDEC + 4 * m + c:GDEC + 4 * m + c + 1],
                                    in1=add, op0=ALU.mult, op1=ALU.add)
                            if (n, half, hd) != (2, 1, 1):
                                chain.inc(ins)
                    if n < 2:
                        chain.wait()
                ins.then_inc(g_dve, 1)

            states(0)
            qk_chunk(3)
            qk_reduce(3)
            states(1)
            qk_normalise(0)
            qk_chunk(4)
            qk_reduce(4)
            dve.wait_ge(g_pe, 8)
            for tt in range(TT):
                ins = V.tensor_copy(
                    o_n[:, tt, :].rearrange("p (b a e) -> p a b e", a=2, b=2),
                    ps[:, 4 + 2 * tt:6 + 2 * tt, 0:T].rearrange("p a (b e) -> p a b e", b=2))
                if tt == 0:
                    chain.inc(ins)
            ins.then_inc(g_dve, 1)
            dve.wait_ge(g_act, 4)
            link(V.tensor_reduce(st(GSS, 8), g3[:].rearrange("p a (b e) -> p (a b) e", e=HD),
                                 AX.X, ALU.add))
            V.tensor_scalar(st(GRT, 8), st(GSS, 8), 1.0 / HD, EPS, ALU.mult, ALU.add)\
                .then_inc(g_dve, 1)
            qk_chunk(5)
            qk_reduce(5)
            qk_mean(1)
            dve.wait_ge(g_act, 5)
            link(V.reciprocal(st(GSS, 8), st(GRT, 8)))
            o_v = o_n[:].rearrange("p a (h e) -> p (a h) e", e=HD)
            link(V.tensor_tensor(o_v, o_v, st(GSS, 8).unsqueeze(2).to_broadcast([P, 8, HD]),
                                 ALU.mult))
            V.tensor_tensor(o_n[:], o_n[:], sra[:], ALU.mult).then_inc(g_dve, 1)
            n_copy(8, lambda tt: vn[:, tt, 0:NCH])
            qk_normalise(1)
            n_copy(9, lambda tt: vn[:, tt, NCH:2 * NCH])
            for h in range(HEADS2):
                dve.wait_ge(qk_turned, HEADS2 + h + 1)
                V.tensor_copy(k_t2[:, h, :], tr_slot((HEADS2 + h) % 8)).then_inc(k_copied, 1)
            n_copy(10, lambda tt: vn[:, tt, 2 * NCH:3 * NCH])

            for kb in range(4):
                dve.wait_ge(x_hi, 80 + kb + 1)
                V.scalar_tensor_tensor(out=xl[:, kb, :], in0=tr_slot(kb), scalar=col("g_gla", kb),
                                       in1=xh[:, kb, :].bitcast(F32), op0=ALU.mult,
                                       op1=ALU.subtract).then_inc(x_lo, 1)

            def head_out2(h):
                dve.wait_ge(x_hi, 80 + 4 + h + 1)
                V.tensor_tensor(xl[:, 4 + h, :], ps[:, 7, 0:T], xh[:, 4 + h, :].bitcast(F32),
                                ALU.subtract).then_inc(x_lo, 1)

            dve.wait_ge(got_dil, 16)
            attend(HEADS1, HEADS2, at2, lambda h: dil_sb[:, 0], dil_sb[:, 1], head_out2)
            for c in range(4):
                dve.wait_ge(unit_used, after("out2", 8 * c + 8))
                for tt in range(TT):
                    v = hx[:, tt, c * NCH:(c + 1) * NCH]
                    ins = V.tensor_tensor(v, ps[:, 2 * (c % 2) + tt, :], v, ALU.add)
                    if c == 3:
                        ins.then_inc(h_new, 1)
                if c < 3:
                    ins.then_inc(free_d, 1)
            dve.wait_ge(h_new, 8)
            norm(4, "g_n2")
            for b in range(KB):
                dve.wait_ge(unit_used, after("query", 2 * b + 2))
                V.tensor_copy(qry_t[:, b, :], t_bank(b % 4)).then_inc(free_d, 1)
            for tt in range(TT):
                lists = {16 * tt + r: ps[:, 4 + r // 4, (r % 4) * P:(r % 4 + 1) * P]
                         for r in range(16)}
                dve.wait_ge(key_scores, tt + 1)
                for r in lists:
                    chain.inc(V.max(top[:, r, 0:8], lists[r]))
                chain.wait()
                for r in lists:
                    chain.inc(V.max_index(top_u[:, r, 0:8], top[:, r, 0:8], lists[r]))
                    V.match_replace(sc_rest[:, r, :], top[:, r, 0:8], lists[r], -3e38)\
                        .then_inc(lists_read, 1)
                dve.wait_ge(lists_read, 16 * (tt + 1))
                for r in lists:
                    chain.inc(V.max(top[:, r, 8:16], sc_rest[:, r, :]))
                chain.wait()
                for r in lists:
                    chain.inc(V.max_index(top_u[:, r, 8:16], top[:, r, 8:16], sc_rest[:, r, :]))
            chain.wait()
            pairs = top[:].rearrange("p (n c) k -> p n c k", c=2)
            cand_v = cand[:].rearrange("p n (a b) -> p n a b", b=16)
            link(V.tensor_tensor(cand_v, pairs[:, :, 0, :].unsqueeze(3).to_broadcast([P, 16, 16, 16]),
                                 pairs[:, :, 1, :].unsqueeze(2).to_broadcast([P, 16, 16, 16]),
                                 ALU.add))
            link(V.tensor_copy(top_i[:], top_u[:]))
            for r in range(16):
                chain.inc(V.max(best[:, r, 0:8], cand[:, r, :]))
            chain.wait()
            for r in range(16):
                chain.inc(V.max_index(pos[:, r, 0:8], best[:, r, 0:8], cand[:, r, :]))
                chain.inc(V.match_replace(cand_rest[:, r, :], best[:, r, 0:8], cand[:, r, :],
                                          -3e38))
            chain.wait()
            for r in range(16):
                chain.inc(V.max(best[:, r, 8:16], cand_rest[:, r, :]))
            chain.wait()
            for r in range(16):
                chain.inc(V.max_index(pos[:, r, 8:16], best[:, r, 8:16], cand_rest[:, r, :]))
            V.tensor_tensor(route[:, 2, :].rearrange("p (n k) -> p n k", k=16), best[:],
                            best[:, :, 0:1].to_broadcast([P, 16, 16]), ALU.subtract)\
                .then_inc(route_m, 1)
            chain.wait()
            chain.inc(V.tensor_scalar(pos_a[:], pos[:], 4, None, ALU.logical_shift_right))
            link(V.tensor_scalar(pos_b[:], pos[:], 15, None, ALU.bitwise_and))
            chain.inc(V.tensor_copy(pos_f[:, 0, :], pos_a[:].rearrange("p a b -> p (a b)")))
            link(V.tensor_copy(pos_f[:, 1, :], pos_b[:].rearrange("p a b -> p (a b)")))
            keys_i = top_i[:].rearrange("p (n c) k -> p n c k", c=2)
            for c in range(2):
                link(V.tensor_tensor(pick[:], pos_f[:, c, :].unsqueeze(2).to_broadcast([P, 256, 16]),
                                     iota[:, 0:16].unsqueeze(1).to_broadcast([P, 256, 16]),
                                     ALU.is_equal))
                pv = pick[:].rearrange("p (n k) a -> p n k a", k=16)
                link(V.tensor_tensor(pv, pv, keys_i[:, :, c, :].unsqueeze(2).to_broadcast(
                    [P, 16, 16, 16]), ALU.mult))
                link(V.tensor_reduce(route[:, c, :], pick[:], AX.X, ALU.add))
            dve.wait_ge(route_e, 1)
            gates_v = route[:, 2, :].rearrange("p (n k) -> p n k", k=16)
            link(V.tensor_reduce(st(RSUM, 16), gates_v, AX.X, ALU.add))
            link(V.reciprocal(st(RSUM, 16), st(RSUM, 16)))
            V.tensor_tensor(gates_v, gates_v, st(RSUM, 16).unsqueeze(2).to_broadcast([P, 16, 16]),
                            ALU.mult).then_inc(route_ready, 1)
            dve.wait_ge(route_turned, 1)
            for k, to in enumerate((i_t, j_t, gate_t)):
                ins = V.tensor_copy(to[:], ps[:, 4 + k, 0:T])
            ins.then_inc(routed, 1)
            dve.wait_ge(routed, 1)

            def one_hots(g, i, n, first=False):
                s = n % HOTS
                if not first:
                    dve.wait_ge(gmat_done, i * 16 + (g * T + n - (HOTS - 1)))
                at_ = bass.ds(i * 16 + n, 1) if not isinstance(i, int) else \
                    slice(i * 16 + n, i * 16 + n + 1)
                V.tensor_scalar(hot_i[:, s, :], iota, i_t[:, at_], gate_t[:, at_], ALU.is_equal,
                                ALU.mult)
                V.tensor_scalar(hot_j[:, s, :], iota[:, g * 64:g * 64 + 64], j_t[:, at_], None,
                                ALU.is_equal).then_inc(hot_done, 1)

            def gate(g, i, b):
                dve.wait_ge(gmat_done, i * 16 + (g * T + 8 * b + 8))
                first = i * 16 + 8 * b
                tokens = bass.ds(first, 8) if not isinstance(i, int) else slice(first, first + 8)
                v = gm[:, g * 64:g * 64 + 64, tokens].rearrange("p j t -> p t j")
                V.tensor_tensor(v, ps[:, 4 + b, :].rearrange("p (t j) -> p t j", j=64), v,
                                ALU.mult).then_inc(gated_done, 1)

            def sixteen(g, i, first=False):
                for n in range(16):
                    if g == 1 and n % 4 == 0:
                        hidden_lo(i * 4, n // 4)
                    one_hots(g, i, n, first and n < HOTS)
                    if n == 11:
                        gate(g, i, 0)
                    if n == 3 and not first:
                        gate(g, i - 1, 1)

            def hidden_lo(p, k):
                dve.wait_ge(hh_done, p + (k + 1))
                j = (p + k) if isinstance(p, int) else None
                h = gm[:, j, :] if j is not None else \
                    gm[:, bass.ds(p + k, 1), :].rearrange("p a t -> p (a t)")
                V.tensor_tensor(hg_l[:, k, :], h, hg_h[:, k, :].bitcast(F32), ALU.subtract)\
                    .then_inc(hl_done, 1)

            for n in range(HOTS):
                one_hots(0, 0, n, True)
            dve.wait_ge(free_a, 71 + 64)
            for n in range(HOTS, 16):
                one_hots(0, 0, n)
                if n == 11:
                    gate(0, 0, 0)
            with dve.Fori(1, 16) as i:
                sixteen(0, i)
            gate(0, 15, 1)
            dve.wait_ge(free_a, 71 + 128)
            for n in range(16):
                if n % 4 == 0:
                    hidden_lo(0, n // 4)
                one_hots(1, 0, n)
                if n == 11:
                    gate(1, 0, 0)
            with dve.Fori(1, 16) as i:
                sixteen(1, i)
            gate(1, 15, 1)
            with dve.Fori(16, 32) as i:
                for k in range(4):
                    hidden_lo(i * 4, k)

            def hidden_lo_again(i, k):
                dve.wait_ge(hh_done, i * 4 + (k + 1))
                V.tensor_tensor(hg_l[:, k, :], gm[:, bass.ds(i * 4 + (k - NKEY), 1), :].rearrange(
                    "p a t -> p (a t)"), hg_h[:, k, :].bitcast(F32), ALU.subtract)\
                    .then_inc(hl_done, 1)

            def add_residual(b):
                tt, c = out_part(b)
                v = hx_end[:, tt, c * NCH:(c + 1) * NCH]
                V.tensor_tensor(v, ps[:, b, :], v, ALU.add).then_inc(fin_done, 1)

            with dve.Fori(32, 34) as i:
                for k in range(4):
                    hidden_lo_again(i, k)
            dve.wait_ge(got_h, 16)
            dve.wait_ge(unit_used, after("peer_up", 128))
            for b in range(4):
                add_residual(b)
            with dve.Fori(34, 64) as i:
                for k in range(4):
                    hidden_lo_again(i, k)
            dve.wait_ge(unit_used, PIECES)
            for b in range(4, 8):
                add_residual(b)

        @block.tensor
        def _(pe):
            M = nc.tensor

            def exact(out_ap, a, b, n, start, stop, group=True):
                M.matmul(out_ap, a[0], b[0], start=start, stop=False)
                M.matmul(out_ap, a[0], b[1], start=False, stop=False)
                return M.matmul(out_ap, a[1], b[0], start=False, stop=stop)

            def ready(i, k, half):
                pe.wait_ge(lo_done[k], i * 2 + (half + 1))

            def t_block(i, k0, bank, between=None):
                for half in range(2):
                    k = k0 + half
                    for j in range(8):
                        if j % 4 == 0:
                            ready(i, k, j // 4)
                        kb = 8 * half + j
                        w = [m[:, s, j * P:(j + 1) * P] for m, s in ((hi, k), (lo, k % 2))]
                        ins = exact(t_bank(bank), w, (xh[:, kb, :], xl[:, kb, :]), T,
                                    kb == 0, kb == KB - 1)
                        if j == 3:
                            ins.then_inc(half_used, 1)
                        if j == 7:
                            ins.then_inc(unit_used, 1)
                        if between and j % 4 == 3:
                            between(2 * half + j // 4)

            def n_piece(i, k, pair, kb0, first, last, a=None):
                ah, al = a or (xh, xl)
                for j in range(2):
                    ready(i, k, j)
                    for tt in range(TT):
                        act_ = [m[:, kb0 + j, tt * P:(tt + 1) * P] for m in (ah, al)]
                        w = [m[:, s, j * NCH:(j + 1) * NCH] for m, s in ((hi, k), (lo, k % 2))]
                        ins = exact(ps[:, 2 * pair + tt, :], act_, w, NCH, first and j == 0,
                                    last and j == 1)
                    ins.then_inc((half_used, unit_used)[j], 1)

            def n_chunk(i, pair):
                for q in range(8):
                    n_piece(i + q // 4, q % 4, pair, 2 * q, q == 0, q == 7)

            def turn(n):
                pe.wait_ge(xn_done, 2 * n + 2)
                b = [0, 2, 3, 4, 6][n]
                for kb in range(KB):
                    if kb >= 4:
                        pe.wait_ge(x_lo, 16 * b + kb - 3)
                    for tt in range(TT):
                        ins = M.transpose(tr_slot(kb % 8)[:, tt * P:(tt + 1) * P],
                                          xn[:, tt, kb * P:(kb + 1) * P], ident)
                    ins.then_inc(tr_done, 1)

            def plain(out_ap, a, b, start, stop, **kw):
                return M.matmul(out_ap, a, b, start=start, stop=stop, **kw)

            pe.wait_ge(got_const, 32)
            turn(0)
            pe.wait_ge(x_lo, 16)

            def gates(g):
                z, which = g // 2, g % 2
                if g == 0:
                    pe.wait_ge(got_wg, 32)
                    pe.wait_ge(conv_done, 8)
                else:
                    pe.wait_ge(tanh_done, 8 * g)
                for n in range(8):
                    ins = plain(ps[:, 4 + n // 2, (n % 2) * T:(n % 2) * T + T],
                                wg[:, 16 * which + 8 * z + n, :], xc[:, n, :], True, True)
                ins.then_inc(gates_done, 1)

            for b in range(24):
                if b >= 4:
                    pe.wait_ge(free_d, b - 3)
                t_block(b // 2, 2 * (b % 2), b % 4)
                if b in (11, 15, 19, 23):
                    gates((b - 11) // 4)
            for c in range(2):
                pe.wait_ge(free_d, 22 + 2 * c)
                n_chunk(12 + 2 * c, c)
            for b in range(8):
                if b < 4:
                    pe.wait_ge(free_d, 25 + b // 2)
                else:
                    pe.wait_ge(free_a, b - 3)
                t_block(16 + b // 2, 2 * (b % 2), b % 4)

            def sums(branch):
                pe.wait_ge(mo_sq, branch + 1)
                if branch == 0:
                    pe.wait_ge(tanh_done, 32)
                sq = (th_i, th_a)[branch][:, 1]
                for n in range(8):
                    ins = plain(ps[:, 4 + branch, 0:T], ones, sq[:, n, :], n == 0, n == 7)
                return ins

            def attend(n0, heads, slots, q_of, k_of, v_of, exp_sem):
                _, p_sb_, pt = slots

                def scores(h):
                    if h >= 2:
                        pe.wait_ge(at_b, n0 + h - 1)
                    for qt in range(TT):
                        ins = plain(ps[:, 4 + h % 2, qt * T:(qt + 1) * T],
                                    q_of(h)[:, qt * P:(qt + 1) * P], k_of(h), True, True)
                    ins.then_inc(at_s, 1)

                def turned(h):
                    pe.wait_ge(at_p, n0 + h + 1)
                    if h:
                        pe.wait_ge(at_c, n0 + h)
                    for kt in range(TT):
                        for qt in range(TT):
                            ins = M.transpose(
                                ps[:, 6, kt * T + qt * P:kt * T + (qt + 1) * P],
                                p_sb_[:, h % 2, qt, kt * P:(kt + 1) * P], ident)
                    ins.then_inc(at_t, 1)

                def heads_out(h):
                    pe.wait_ge(at_c, n0 + h + 1)
                    if h:
                        exp_sem(h)
                    for kt in range(TT):
                        ins = plain(ps[:, 7, 0:T], v_of(h, kt), pt[:, h % 2, kt, :], kt == 0,
                                    kt == TT - 1)
                    ins.then_inc(at_o, 1)

                scores(0)
                scores(1)
                for h in range(heads):
                    turned(h)
                    if h + 2 < heads:
                        scores(h + 2)
                    heads_out(h)

            pe.wait_ge(tanh_done, 32)
            attend(0, HEADS1, at1, lambda h: q_t[:, h, :], lambda h: k_t[:, h, :],
                   lambda h, kt: v_n[:, kt, h * P:(h + 1) * P],
                   lambda h: pe.wait_ge(at_f, h))
            pe.wait_ge(at_b, HEADS1)
            sums(0).then_inc(mo_sum, 1)
            sums(1).then_inc(mo_sum, 1)

            def n_stage(name, free):
                r0 = ROUND0[name]
                for c in range(4):
                    free(c)
                    n_chunk(r0 + 2 * c, c % 2)

            def both(d0, a0):
                def free(c):
                    if c >= 2:
                        pe.wait_ge(free_d, d0 + c - 1)
                        pe.wait_ge(free_a, a0 + c - 1)
                return free

            pe.wait_ge(x_lo, 32)
            pe.wait_ge(free_a, 8)
            pe.wait_ge(mo_ms, 2)
            n_stage("out1", both(26, 8))
            turn(1)
            pe.wait_ge(x_lo, 48)
            pe.wait_ge(free_a, 12)
            r0 = ROUND0["ffn"]
            with pe.Fori(0, FB // 2) as i:
                for s in range(2):
                    pe.wait_ge(free_a, i * 2 + (11 + s))
                    t_block(i * 2 + (r0 + s), 0, 2 * s)
                    pe.wait_ge(free_d, i * 2 + (29 + s))
                    t_block(i * 2 + (r0 + s), 2, 2 * s + 1)
            pe.wait_ge(free_d, 74)
            pe.wait_ge(free_a, 56)
            r0 = ROUND0["down"]
            with pe.Fori(0, 2) as i:
                for c in range(2):
                    pe.wait_ge(free_d, i * 2 + (73 + c))
                    pe.wait_ge(free_a, i * 2 + (55 + c))
                    for q in range(22):
                        u = 22 * c + q
                        n_piece(i * 11 + (r0 + u // 4), u % 4, c, 2 * q, q == 0, q == 21,
                                (hid_h, hid_l))
            turn(2)
            pe.wait_ge(x_lo, 64)
            pe.wait_ge(got_ple, 32)
            r0 = ROUND0["gate"]
            for c in range(4):
                if c >= 2:
                    pe.wait_ge(free_a, 60 + c - 1)
                    pe.wait_ge(ple_free, c - 1)
                else:
                    pe.wait_ge(free_d, 78)
                    pe.wait_ge(free_a, 60)
                for tt in range(TT):
                    for j in range(2):
                        ins = plain(ps[:, 4 + 2 * (c % 2) + tt, :], p_sb[:, j, tt * P:(tt + 1) * P],
                                    w_pr[:, j, c * NCH:(c + 1) * NCH], j == 0, j == 1)
                ins.then_inc(ple_done, 1)
                n_chunk(r0 + 2 * c, c % 2)
            turn(3)

            pe.wait_ge(x_lo, 80)
            pe.wait_ge(g_dve, 1)
            for tt in range(TT):
                for kb in range(KB):
                    ins = exact(ps[:, 4, 32 * tt:32 * tt + 32],
                                [m[:, kb, tt * P:(tt + 1) * P] for m in (xh, xl)],
                                [m[:, kb, :] for m in (wgd_h, wgd_l)], 32, kb == 0, kb == KB - 1)
            ins.then_inc(g_pe, 1)
            r0 = ROUND0["in2"]
            pe.wait_ge(free_a, 64)
            t_block(r0, 0, 0)
            t_block(r0, 2, 1)
            pe.wait_ge(g_dve, 2)
            for tt in range(TT):
                ins = plain(ps[0:32, 5, tt * P:(tt + 1) * P], gd_n[:, tt, :], ident, True, True)
            ins.then_inc(g_pe, 1)
            t_block(r0 + 1, 0, 2)
            t_block(r0 + 1, 2, 3)
            pe.wait_ge(g_dve, 3)
            for m in range(4):
                ins = plain(tr_slot(4 + m), up[:, m * P:(m + 1) * P], gd_t[:], True, True)
            ins.then_inc(g_pe, 1)

            def scores_in_chunks():
                pe.wait_ge(g_dve, 5)
                for d in range(2):
                    for tt in range(TT):
                        for h in range(4):
                            rows, m = slice(64 * (h % 2), 64 * (h % 2) + 64), 2 * d + h // 2
                            at_ = (2 * d + h // 2) * P
                            ins = plain(ps[:, 4 + 2 * tt + h % 2, at_:at_ + P],
                                        g3[rows, m, tt * P:(tt + 1) * P],
                                        g2[rows, m, tt * P:(tt + 1) * P], True, True)
                ins.then_inc(g_pe, 1)

            def turn_key_states():
                pe.wait_ge(g_dve, 6)
                for tt in range(TT):
                    for m in range(4):
                        ins = M.transpose(ps[:, 4 + tt, m * P:(m + 1) * P],
                                          g4[:, m, tt * P:(tt + 1) * P], ident)
                ins.then_inc(g_pe, 1)

            def increments(d):
                pe.wait_ge(g_dve, 7 + d)
                for n in range(3):
                    c = n if d == 0 else 3 - n
                    rows = slice(64 * (c % 2), 64 * (c % 2) + 64)
                    for half in range(2):
                        ins = plain(inc_at(d, c, half), kst[rows, c // 2, 2 * d + half, :],
                                    va[rows, c // 2, half * T:(half + 1) * T], True, True)
                ins.then_inc(g_pe, 1)

            def gla_out():
                pe.wait_ge(g_dve, 9)
                for tt in range(TT):
                    for h in range(4):
                        bank, at_ = 4 + 2 * tt + h % 2, (h // 2) * P
                        rows = slice(64 * (h % 2), 64 * (h % 2) + 64)
                        for d in range(2):
                            o = (2 * d + h // 2) * P
                            plain(ps[:, bank, at_:at_ + P], sc_t[:, 2 * tt + h % 2, o:o + P],
                                  va[:, tt, h * P:(h + 1) * P], d == 0, False,
                                  skip_group_check=True)
                        for c in (2 * tt, 2 * tt + 1):
                            for d in range(2):
                                before = c - 1 if d == 0 else 2 - c
                                if before < 0:
                                    continue
                                half = slice(64 * (c % 2), 64 * (c % 2) + 64)
                                ins = plain(ps[half, bank, at_:at_ + P],
                                            g2[rows, 2 * d + h // 2, 64 * c:64 * c + 64],
                                            state[rows, d, before, h // 2, :], False, True,
                                            skip_group_check=True)
                ins.then_inc(g_pe, 1)

            def turn_qk(which):
                pe.wait_ge(qk_ready, which + 1)
                for h in range(HEADS2):
                    n = HEADS2 * which + h
                    if n >= 4:
                        if n - 4 < HEADS2:
                            pe.wait_ge(q_copied, n - 3)
                        else:
                            pe.wait_ge(k_copied, n - 3 - HEADS2)
                    for tt in range(TT):
                        ins = M.transpose(tr_slot(n % 8)[:, tt * P:(tt + 1) * P],
                                          qk_n[which][:, tt, h * P:(h + 1) * P], ident)
                    ins.then_inc(qk_turned, 1)

            waits = [(80, 0), (82, 0), (83, 0), (0, 65), (84, 66), (85, 67), (86, 68), (87, 69),
                     (88, 70), (89, 71), (90, 0)]
            then = {1: scores_in_chunks, 3: turn_key_states, 4: lambda: increments(0),
                    5: lambda: increments(1), 6: gla_out}
            for n in range(11):
                for s_, v_ in zip((free_d, free_a), waits[n]):
                    if v_:
                        pe.wait_ge(s_, v_)
                n_chunk(r0 + 2 + 2 * n, n % 2)
                if n in then:
                    then[n]()
                if n == 7:
                    pe.wait_ge(g_dve, 10)
                    turn_qk(0)
                if n == 9:
                    turn_qk(1)
            pe.wait_ge(g_dve, 12)
            pe.wait_ge(k_copied, HEADS2)
            for kb in range(4):
                for tt in range(TT):
                    ins = M.transpose(tr_slot(kb)[:, tt * P:(tt + 1) * P],
                                      o_n[:, tt, kb * P:(kb + 1) * P], ident)
                ins.then_inc(g_pe, 1)
            pe.wait_ge(x_lo, 84)
            pe.wait_ge(free_d, 92)
            attend(HEADS1, HEADS2, at2, lambda h: q_t2[:, h, :], lambda h: k_t2[:, h, :],
                   lambda h, kt: vn[:, kt, h * P:(h + 1) * P],
                   lambda h: pe.wait_ge(x_lo, 84 + h))
            pe.wait_ge(x_lo, 96)
            r0 = ROUND0["out2"]
            for c in range(4):
                if c >= 2:
                    pe.wait_ge(free_d, 92 + c - 1)
                n_chunk(r0 + 2 * c, c % 2)
            turn(4)
            pe.wait_ge(x_lo, 112)
            for b in range(KB):
                if b >= 4:
                    pe.wait_ge(free_d, 95 + b - 3)
                t_block(ROUND0["query"] + b // 2, 2 * (b % 2), b % 4)
            def scores_of_keys(tt):
                for r in range(16):
                    ins = plain(ps[:, 4 + r // 4, (r % 4) * P:(r % 4 + 1) * P],
                                qry_t[:, r, tt * P:(tt + 1) * P], keys_t[:, r, :], True, True)
                ins.then_inc(key_scores, 1)

            pe.wait_ge(free_d, 111)
            pe.wait_ge(got_keys, 16)
            scores_of_keys(0)
            r0 = ROUND0["peer_down"]

            def down_blocks(i, between=None):
                for j in range(4):
                    pe.wait_ge(free_a, i * 4 + (71 + j - 3))
                    t_block(i * 2 + (r0 + j // 2), 2 * (j % 2), j,
                            between and (lambda q, j=j: between(i, 4 * j + q)))

            for j in range(4):
                t_block(r0 + j // 2, 2 * (j % 2), j)
            with pe.Fori(1, 3) as i:
                down_blocks(i)
            pe.wait_ge(lists_read, 16)
            scores_of_keys(1)
            with pe.Fori(3, 8) as i:
                down_blocks(i)
            pe.wait_ge(route_ready, 1)
            for k in range(3):
                for tt in range(TT):
                    ins = M.transpose(ps[:, 4 + k, tt * P:(tt + 1) * P],
                                      route[:, k, tt * P:(tt + 1) * P], ident)
            ins.then_inc(route_turned, 1)
            with pe.Fori(8, 16) as i:
                down_blocks(i)

            def gate_products(g, i, n, first=False):
                pe.wait_ge(hot_done, i * 16 + (g * T + n + 1))
                if n % 8 == 0 and not first:
                    pe.wait_ge(gated_done, i * 2 + (32 * g + n // 8 - 1))
                plain(ps[:, 4 + n // 8, (n % 8) * 64:(n % 8 + 1) * 64], hot_i[:, n % HOTS, :],
                      hot_j[:, n % HOTS, :], True, True).then_inc(gmat_done, 1)

            pe.wait_ge(routed, 1)
            down_blocks(16, lambda i, n: gate_products(0, 0, n, True))
            with pe.Fori(17, 32) as i:
                down_blocks(i, lambda i, n: gate_products(0, i - 16, n))

            def up_piece(i, k, half, first=False, last=False, between=None):
                pe.wait_ge(hl_done, i * 4 + (k + 1))
                for n in range(2):
                    ready(i + r0, k, n)
                    for tt in range(TT):
                        ins = exact(ps[:, 4 * half + 2 * tt + n, :],
                                    [m[:, k, tt * P:(tt + 1) * P] for m in (hg_h, hg_l)],
                                    [m[:, q, n * NCH:(n + 1) * NCH]
                                     for m, q in ((hi, k), (lo, k % 2))], NCH, first, last)
                        if tt == 1:
                            ins.then_inc((half_used, unit_used)[n], 1)
                        if between:
                            between(2 * n + tt)

            r0 = ROUND0["peer_up"]
            pe.wait_ge(free_a, 71 + 128)
            for k in range(4):
                up_piece(0, k, 0, first=k == 0,
                         between=lambda q, k=k: gate_products(1, 0, 4 * k + q))
            with pe.Fori(1, 16) as i:
                for k in range(4):
                    up_piece(i, k, 0, between=lambda q, k=k: gate_products(1, i, 4 * k + q))
            with pe.Fori(16, 31) as i:
                for k in range(4):
                    up_piece(i, k, 0)
            for k in range(4):
                up_piece(31, k, 0, last=k == 3)
            for k in range(4):
                up_piece(32, k, 1, first=k == 0)
            with pe.Fori(33, 63) as i:
                for k in range(4):
                    up_piece(i, k, 1)
            for k in range(4):
                up_piece(63, k, 1, last=k == 3)


def pieces_t(w, blocks):
    w = w.reshape(2, 8, P, -1, P)[:, :, :, blocks]
    return w.transpose(3, 0, 2, 1, 4).reshape(-1, P, PIECE)


def pieces_n(w, first, chunks):
    w = w[:, first:first + chunks * NCH].reshape(-1, 2, P, chunks, NCH)
    return w.transpose(3, 0, 2, 1, 4).reshape(-1, P, PIECE)


def lay_out(x, p, g_mix_pre, w_in, rpb, conv_w, conv_b, w_rg_a, b_rg_a, w_rg_i, b_rg_i, lam,
            g_attn_out, g_rec_out, w_out, g_mix_post, g_ffn_pre, w_ffn_gate, w_ffn_up, w_ffn_down,
            g_ffn_post, g_ple_pre, w_ple_gate, w_ple_proj, g_ple_post, norm1_g_2, w_in_2,
            gla_up_f_2, gla_bias_f_2, gla_up_b_2, gla_bias_b_2, gla_out_g_2, q_norm_g_2,
            k_norm_g_2, w_out_2, norm2_g_2, peer_w_query_2, peer_sub_keys_2, peer_down_2,
            peer_up_2):
    c, band, dil = shape_constants()
    win, win2 = w_in[0], w_in_2[0]
    gate_up = np.stack([pieces_t(w_ffn_gate[0], np.arange(FB)).reshape(FB, 2, P, PIECE),
                        pieces_t(w_ffn_up[0], np.arange(FB)).reshape(FB, 2, P, PIECE)], 1)
    rest = np.concatenate([win2[:, 512:1024], win2[:, 1056:]], 1)
    down = peer_down_2[0].reshape(P, NKEY, 2, 8, P).transpose(1, 2, 4, 3, 0)
    up = peer_up_2[0].reshape(P, NKEY, 2, PIECE).transpose(2, 1, 0, 3)
    stream = np.concatenate([
        pieces_t(win, np.r_[24:32, 0:16]), pieces_n(win, 2048, 2), pieces_t(win, np.arange(32, 40)),
        pieces_n(w_out[0], 0, 4), gate_up.reshape(-1, P, PIECE), pieces_n(w_ffn_down[0], 0, 4),
        pieces_n(w_ple_gate[0], 0, 4), pieces_t(win2[:, 0:512], np.arange(4)),
        pieces_n(rest, 0, 11), pieces_n(w_out_2[0], 0, 4),
        pieces_t(peer_w_query_2[0], np.arange(KB)), down.reshape(-1, P, PIECE),
        up.reshape(-1, P, PIECE)])
    assert stream.shape[0] == PIECES

    def columns(*vectors):
        return np.concatenate([v.reshape(-1, P) for v in vectors]).T

    cols = columns(g_mix_pre, g_ffn_pre, g_ple_pre, norm1_g_2, norm2_g_2, g_attn_out, g_rec_out,
                   gla_out_g_2, conv_w, conv_b, b_rg_a, b_rg_i, lam, gla_bias_f_2, gla_bias_b_2)
    col_, row = np.arange(64), np.arange(4)
    gap = col_[None, :] - col_[:, None] + 15
    wide = rpb[0][:, (row[None, :] - row[:, None] + 7)[:, :, None, None],
                  np.clip(gap, 0, 30)[None, None]]
    wide = np.where((gap >= 0) & (gap <= 30), wide, np.zeros((), rpb.dtype))
    wide = wide.transpose(1, 3, 0, 2, 4).reshape(TT, P, HEADS1, T).transpose(1, 2, 0, 3)
    up_fb = np.zeros((32, 512), np.float32)
    up_fb[0:16, 0:256] = gla_up_f_2[0]
    up_fb[16:32, 256:512] = gla_up_b_2[0]
    gains = np.stack([np.broadcast_to(g[0], (P, D)) for g in (g_mix_post, g_ffn_post, g_ple_post)])
    return {
        "stream": stream,
        "cols": cols,
        "cons": c,
        "band": band,
        "dil": dil,
        "x": x[0],
        "rpb": wide,
        "w_gates": np.concatenate([w_rg_a[0].reshape(16, P, P), w_rg_i[0].reshape(16, P, P)])
        .transpose(1, 0, 2),
        "gains": gains,
        "p_t": p[0, 0].T.reshape(2, P, T).transpose(1, 0, 2),
        "w_proj": w_ple_proj[0].reshape(2, P, D).transpose(1, 0, 2),
        "w_gd": win2[:, 1024:1056].reshape(KB, P, 32).transpose(1, 0, 2),
        "up_fb": up_fb,
        "qk_gain": np.broadcast_to(np.stack([q_norm_g_2[0], k_norm_g_2[0]]), (P, 2, HD)),
        "sub_keys": peer_sub_keys_2[0].transpose(3, 0, 1, 2).reshape(P, KB, NKEY),
    }


def kernel(**inputs):
    import concourse.bacc as bacc
    from concourse.bass_utils import run_bass_kernel_spmd

    nc = bacc.Bacc("TRN2", target_bir_lowering=False, num_devices=1)
    laid = lay_out(**{k: np.asarray(v) for k, v in inputs.items()})
    arrays, args = {}, {}
    for name, a in laid.items():
        a = np.ascontiguousarray(a)
        arrays[f"in_{name}"] = a
        args[name] = nc.dram_tensor(f"in_{name}", a.shape, mybir.dt.from_np(a.dtype),
                                    kind="ExternalInput").ap()
    spill = nc.dram_tensor("spill", [P, TT, D], F32).ap()
    out = nc.dram_tensor("out", [T, D], F32, kind="ExternalOutput").ap()
    build(nc, spill=spill, out=out, **args)
    r = run_bass_kernel_spmd(nc, [arrays], core_ids=[0])
    return r.results[0]["out"].reshape(1, T, D)
```

```python
import numpy as np
import concourse.bass as bass
from concourse import mybir
from contextlib import ExitStack

F32 = mybir.dt.float32
F32R = mybir.dt.float32r
U32 = mybir.dt.uint32
BF16 = mybir.dt.bfloat16
ALU = mybir.AluOpType
ACT = mybir.ActivationFunctionType
AX = mybir.AxisListType

P = 128
T = 256
TT = T // P
D = 2048
KB = D // P
DFF = 5632
FB = DFF // P
EPS = 1e-6
NCH = 512
HD = 128
SCALE = HD ** -0.5
HEADS1 = 8
HEADS2 = 12
GLA_W = 512
EXPERTS = 16384
NKEY = 128
PIECE = 1024

STAGES = [("in1", 80), ("out1", 32), ("ffn", 176), ("down", 88), ("gate", 32), ("in2", 96),
          ("out2", 32), ("query", 32), ("peer_down", 256), ("peer_up", 256)]
ROUND0, _n = {}, 0
for _name, _pieces in STAGES:
    ROUND0[_name] = _n // 4
    _n += _pieces
PIECES = _n
ROUNDS = PIECES // 4


def after(name, pieces):
    return 4 * ROUND0[name] + pieces


COLS, _n = {}, 0
for _name, _w in [("g_mix", 16), ("g_ffn", 16), ("g_ple", 16), ("g_n1", 16), ("g_n2", 16),
                  ("g_mo", 16), ("g_gla", 4), ("conv_w", 32), ("conv_b", 8), ("b_a", 16),
                  ("b_i", 16), ("lam", 16), ("gla_b", 4)]:
    COLS[_name] = (_n, _w)
    _n += _w
NCOLS = _n
CONS, _n = {}, 0
for _name, _w in [("ident", 128), ("iota", 128), ("ones", 128), ("cos", 32), ("sin", 32),
                  ("scan", 256), ("causal", 256)]:
    CONS[_name] = (_n, _w)
    _n += _w
NCONS = _n


def shape_constants():
    c = np.zeros((P, NCONS), np.float32)
    lane = np.arange(P)

    def put(name, a):
        o, w = CONS[name]
        c[:, o:o + w] = np.asarray(a, np.float32).reshape(P, w)

    put("ident", np.eye(P))
    put("ones", np.ones((P, P)))
    put("iota", np.broadcast_to(lane, (P, P)))
    half = 16
    inv = np.float32(500000.0) ** (-np.arange(half, dtype=np.float32) / np.float32(half))
    ang = (np.arange(T, dtype=np.float32)[:, None] * inv[None, :]).astype(np.float32)
    put("cos", np.cos(ang).reshape(TT, P, half).transpose(1, 0, 2))
    put("sin", np.sin(ang).reshape(TT, P, half).transpose(1, 0, 2))
    put("scan", np.broadcast_to(np.arange(T) % 64 != 0, (P, T)))
    same = lane[:, None] // 64 == lane[None, :] // 64
    key, query = lane[:, None], lane[None, :]
    put("causal", np.stack([same & (key <= query), same & (key > query)], 1))
    col = np.arange(64)
    start = np.clip(col - 8, 0, 48)
    near = (col[None] >= start[:, None]) & (col[None] < start[:, None] + 16)
    band = np.where(near, 0.0, -1e9)[lane % 64].astype(np.float32)
    q = np.arange(T)
    gap = np.abs(q[:, None] - q[None, :])
    times = (gap <= 64).astype(np.float32) + (gap % 4 == 0) + (gap % 16 == 0)
    times = times.reshape(TT, P, T).transpose(1, 0, 2).astype(np.float32)
    dil = np.stack([np.where(times == 0, -1e30, 0.0), times], 1).astype(np.float32)
    return c, band, dil


def build(nc, stream, cols, cons, band, dil, x, rpb, w_gates, gains, p_t, w_proj, w_gd, up_fb,
          qk_gain, sub_keys, spill, out):
    ctx = ExitStack()
    with ctx:
        def sem(name):
            return ctx.enter_context(nc.semaphore(name))

        base = -(-nc.sbuf_base // 32) * 32
        ctx.enter_context(nc.sbuf_tensor("whole", [P, (nc.sbuf_top - nc.sbuf_base - 32) // 4], F32))

        def place(name, shape, at, dt=F32):
            return nc.alloc_sbuf_tensor_at(name, shape, dt, offset=base + at)

        cons_sb = place("cons_sb", [P, NCONS], 0)
        cols_sb = place("cols_sb", [P, NCOLS], NCONS * 4)
        X_AT = 8032
        STATS = 320
        small = place("small", [P, STATS], X_AT - 4 * STATS)
        assert (NCONS + NCOLS + STATS) * 4 <= X_AT
        hot_at = 256 * 4
        i_t, j_t = (place(n, [P, T], hot_at + 1024 * k) for k, n in enumerate(("i_t", "j_t")))
        gate_t = place("gate_t", [P, T, 3], hot_at + 2048, BF16)
        HOTS = 4
        hot_i = place("hot_i", [P, HOTS, P], hot_at + 3584, BF16)
        hot_j = place("hot_j", [P, HOTS, 3, 64], hot_at + 3584 + 256 * HOTS, BF16)
        assert hot_at + 3584 + 640 * HOTS <= X_AT
        RING_AT = X_AT + 32768
        W_AT = RING_AT + 40960
        assert base + W_AT + 131072 <= nc.sbuf_usable_end, (base, nc.sbuf_usable_end)
        xh = place("xh", [P, KB, T], X_AT, F32R)
        xl = place("xl", [P, KB, T], X_AT + 16384, F32R)
        raw = place("raw", [P, 4, PIECE], RING_AT)
        hi = place("hi", [P, 4, PIECE], RING_AT + 16384, F32R)
        lo = place("lo", [P, 2, PIECE], RING_AT + 32768, F32R)
        hx = place("hx", [P, TT, D], W_AT)
        xn = place("xn", [P, TT, D], W_AT + 16384)
        Z_AT = W_AT + 40960

        def con(name, *dims):
            o, w = CONS[name]
            return cons_sb[:, o:o + w]

        def col(name, i, n=1):
            o, _ = COLS[name]
            return cols_sb[:, o + i:o + i + n]

        ident, ones, iota = con("ident"), con("ones"), con("iota")

        def st(i, n=1):
            return small[:, i:i + n]

        ps = ctx.enter_context(nc.psum_tensor("ps", [P, 8, 512], F32))

        loaded = [sem(f"loaded{k}") for k in range(4)]
        hi_done, unit_used, half_used = sem("hi_done"), sem("unit_used"), sem("half_used")
        lo_done = [sem(f"lo_done{k}") for k in range(4)]
        free_d, free_a = sem("free_d"), sem("free_a")
        x_hi, x_lo = sem("x_hi"), sem("x_lo")
        dch, ach = sem("dve_chain"), sem("act_chain")
        got_const, got_x, got_wg, got_bias, got_gain = (sem(n) for n in (
            "got_const", "got_x", "got_gate_weights", "got_bias", "got_gain"))
        got_ple, got_in2 = sem("got_ple"), sem("got_in2")
        spilled, got_h = sem("spilled"), sem("got_h")
        h_new, ss_done, ms_done, rms_done, xn_done, tr_done = (sem(n) for n in (
            "h_new", "ss_done", "ms_done", "rms_done", "xn_done", "tr_done"))
        conv_done, gates_done, tanh_done, decay_done, z_done, sqrt_done = (
            sem(n) for n in ("conv_done", "gates_done", "tanh_done", "decay_done", "z_done",
                             "sqrt_done"))
        soft_e, soft_c = sem("soft_e"), sem("soft_c")
        at_s, at_b, at_m, at_e, at_p, at_t, at_c, at_o, at_f = (sem(n) for n in (
            "scores_done", "bias_added", "max_done", "exp_done", "probs_ready", "probs_turned",
            "probs_copied", "heads_done", "heads_copied"))
        mo_sq, mo_sum, mo_ms, mo_rt, mo_ready = (sem(n) for n in (
            "mo_sq", "mo_sum", "mo_ms", "mo_rt", "mo_ready"))
        act_post, prod_done = sem("act_post"), sem("prod_done")
        ple_done, ple_free, pz_squared = sem("ple_done"), sem("ple_free"), sem("pz_squared")
        hid_hi = sem("hid_hi")
        out_stored = sem("out_stored")
        g_pe, g_dve, g_act = sem("gla_pe"), sem("gla_dve"), sem("gla_act")
        qk_reduced, qk_ms, qk_rt, qk_ready, qk_turned, q_copied, k_copied = (
            sem(n) for n in ("qk_reduced", "qk_ms", "qk_rt", "qk_ready",
                             "qk_turned", "q_copied", "k_copied"))
        got_dil, got_keys = sem("got_dil"), sem("got_keys")
        lists_read = sem("lists_read")
        key_scores, route_m, route_e, route_ready, route_turned, routed = (
            sem(n) for n in ("key_scores", "route_m", "route_e", "route_ready", "route_turned",
                             "routed"))
        hot_done, gmat_done = sem("hot_done"), sem("gmat_done")
        gate_split = sem("gate_split")
        gated_done, hh_done, hl_done = sem("gated_done"), sem("hh_done"), sem("hl_done")
        fin_done = sem("fin_done")

        block = ctx.enter_context(nc.Block())

        XRW = 260
        xr = place("xr", [P, 8, XRW], Z_AT)
        t_z0 = place("t_z0", [P, 8, T], Z_AT)
        xc = place("xc", [P, 8, T], Z_AT + 8320)
        q_t = place("q_t", [P, 8, T], Z_AT + 8320 + 8192)
        k_t = place("k_t", [P, 8, T], Z_AT + 8320 + 2 * 8192)
        v_n = place("v_n", [P, TT, 1024], Z_AT + 8320 + 3 * 8192)
        yg = place("yg", [P, 8, T], Z_AT + 8320 + 4 * 8192)
        th_a = place("th_a", [P, 2, 8, T], Z_AT + 8320 + 5 * 8192)
        th_i = place("th_i", [P, 2, 8, T], Z_AT + 8320 + 7 * 8192)
        band_sb = place("band_sb", [P, 64], Z_AT + 8320 + 9 * 8192)
        mo_r = place("mo_r", [P, 2, T], Z_AT + 8320 + 9 * 8192 + 256)
        wg = place("wg", [P, 32, P], W_AT + 16384)
        bias = place("bias", [P, HEADS1, TT, T], W_AT + 16384)
        t_z1 = place("t_z1", [P, 8, T], W_AT + 32768)
        attn_t = place("attn_t", [P, 8, T], W_AT + 32768)
        A1 = Z_AT + 8320 + 5 * 8192
        at1 = [place(f"at1_{i}", [P, 2, TT, T], A1 + 4096 * i) for i in range(3)]
        sq_sum, sq_one = (place(n, [P, T], A1 + 14336 + 1024 * k)
                          for k, n in enumerate(("sq_sum", "sq_one")))
        y = place("y", [P, TT, D], W_AT + 16384)
        gbc = place("gbc", [P, D], W_AT + 32768)
        sil = place("sil", [P, 2, T], W_AT + 16384)
        prod = place("prod", [P, 2, T], W_AT + 16384 + 2048)
        hid_h = place("hid_h", [P, FB, T], Z_AT, F32R)
        hid_l = place("hid_l", [P, FB, T], Z_AT + FB * T * 4, F32R)
        w_pr = place("w_pr", [P, 2, D], Z_AT)
        p_sb = place("p_sb", [P, 2, T], Z_AT + 16384)
        sig = place("sig", [P, 2, TT, NCH], Z_AT + 18432)
        pz = place("pz", [P, TT, NCH], Z_AT + 26624)
        SS, MS, RT, RI = 0, 2, 4, 6
        SSP = 8
        NM, SM, SI = 16, 24, 32
        LAMW = 40
        CSP = 104
        SSQ = 136
        SRT = 184
        GDEC = 232
        GSS = 248
        GRT = 256
        BA2 = 264
        WARM = 312

        qn, kn, vn = (place(n, [P, TT, HEADS2 * HD], Z_AT + 12288 * k)
                      for k, n in enumerate(("qn", "kn", "vn")))
        qk_n = (qn, kn)
        GZ = Z_AT + 36864
        qa_t = place("qa_t", [P, 2, T], GZ)
        ka_t = place("ka_t", [P, 2, T], GZ + 2048)
        va = place("va", [P, TT, GLA_W], GZ + 4096)
        sra = place("sra", [P, TT, GLA_W], GZ + 8192)
        g1, g2, g3, g4 = (place(f"g{k + 1}", [P, 4, T], GZ + 12288 + 4096 * k) for k in range(4))
        kst = place("kst", [P, TT, 4, P], GZ + 12288)
        sc_t = place("sc_t", [P, 4, 512], GZ + 28672)
        state = place("state", [P, 2, 3, 2, P], GZ + 36864)
        o_n = place("o_n", [P, TT, GLA_W], GZ + 43008)
        sqt = place("sqt", [P, TT, NCH], GZ + 47104)
        rope_t = place("rope_t", [P, 4, 12, 16], GZ + 47104)
        qkg = place("qkg", [P, 2, HD], GZ + 51200)
        wgd = place("wgd", [P, KB, 32], GZ + 28672)
        wgd_h = place("wgd_h", [P, KB, 32], GZ + 28672 + 2048, F32R)
        wgd_l = place("wgd_l", [P, KB, 32], GZ + 28672 + 4096, F32R)
        gd_t = place("gd_t", [32, T], GZ + 28672 + 6400)
        up = place("up", [32, 512], GZ + 28672 + 7424)
        q_t2 = place("q_t2", [P, HEADS2, T], W_AT + 16384)
        k_t2 = place("k_t2", [P, HEADS2, T], W_AT + 28672)
        dil_sb = place("dil_sb", [P, 2, TT, T], GZ + 12288)
        at2 = [place(f"at2_{i}", [P, 2, TT, T], GZ + 16384 + 4096 * i) for i in range(3)]
        W2_AT = W_AT + 65536
        qry_t = place("qry_t", [P, KB, T], W2_AT)
        keys_t = place("keys_t", [P, KB, NKEY], W2_AT + 16384)
        sc_rest = place("sc_rest", [P, 32, NKEY], W2_AT + 24576)
        cand = place("cand", [P, 16, 256], W2_AT)
        cand_rest = place("cand_rest", [P, 16, 256], W2_AT + 24576)
        pick = place("pick", [P, 256, 16], W2_AT + 24576)
        R_AT = W2_AT + 40960
        top = place("top", [P, 32, 16], R_AT)
        top_u = place("top_u", [P, 32, 16], R_AT + 2048, U32)
        top_i = place("top_i", [P, 32, 16], R_AT + 4096)
        best = place("best", [P, 16, 16], R_AT + 6144)
        pos = place("pos", [P, 16, 16], R_AT + 7168, U32)
        pos_a = place("pos_a", [P, 16, 16], R_AT + 8192, U32)
        pos_b = place("pos_b", [P, 16, 16], R_AT + 9216, U32)
        pos_f = place("pos_f", [P, 2, 256], R_AT + 10240)
        route = place("route", [P, 3, 256], R_AT + 12288)
        gate_rest = place("gate_rest", [P, T], R_AT + 10240)
        RSUM = 296
        gm = place("gm", [P, NKEY, T], W_AT)
        hg_h = place("hg_h", [P, 4, T], X_AT, F32R)
        hg_l = place("hg_l", [P, 4, T], X_AT + 4096, F32R)
        hx_end = place("hx_end", [P, TT, D], X_AT + 8192)

        class Chain:

            def __init__(self, eng, s):
                self.eng, self.s, self.n, self.reg, self.per, self.k = eng, s, 0, None, 0, 0

            def value(self):
                return self.n if self.reg is None else self.reg * self.per + (self.n + self.k)

            def inc(self, ins):
                if self.reg is None:
                    self.n += 1
                else:
                    self.k += 1
                ins.then_inc(self.s, 1)

            def wait(self):
                self.eng.wait_ge(self.s, self.value())

            def link(self, ins):
                self.inc(ins)
                self.wait()

            def enter(self, reg, per):
                self.reg, self.per, self.k = reg, per, 0

            def leave(self, times):
                assert self.k == self.per, (self.k, self.per)
                self.n += self.per * times
                self.reg = None

        SUM_BANK = (7, 5)

        def t_bank(b):
            return ps[:, b, 0:T]

        def inc_at(d, c, half):
            nth = 1 if (d, c) in ((0, 2), (1, 1)) else 0
            return ps[:, 4 + c % 2 + 2 * nth, half * T:(half + 1) * T]

        def out_part(b):
            return b // 2 % 2, 2 * (b // 4) + b % 2

        def tr_slot(s):
            return ps[:, 4 + s % 4, (s // 4) * T:(s // 4) * T + T]

        @block.sync
        def _(sp):
            for tt in range(TT):
                sp.dma_start(hx[:, tt, :], x[tt * P:(tt + 1) * P, :]).then_inc(got_x, 16)
            for k in range(4):
                sp.dma_start(raw[:, k, :], stream[k]).then_inc(loaded[k], 16)
            with sp.Fori(1, ROUNDS) as i:
                for k in range(4):
                    sp.wait_ge(lo_done[k], i * 2)
                    sp.dma_start(raw[:, k, :], stream[bass.ds(i * 4 + k, 1)].rearrange(
                        "a p n -> p (a n)")).then_inc(loaded[k], 16)
            for b in range(8):
                sp.wait_ge(fin_done, b + 1)
                tt, c = out_part(b)
                sp.dma_start(out[tt * P:(tt + 1) * P, c * NCH:(c + 1) * NCH],
                             hx_end[:, tt, c * NCH:(c + 1) * NCH]).then_inc(out_stored, 16)
            sp.wait_ge(out_stored, 16 * 8)

        @block.gpsimd
        def _(pool):
            def take_lo(i, k, first):
                pool.wait_ge(hi_done, i * 4 + (k + 1))
                for half, used in enumerate((half_used, unit_used)):
                    if not (first and k < 2):
                        pool.wait_ge(used, i * 4 + (k - 1))
                    n = slice(half * NCH, (half + 1) * NCH)
                    nc.gpsimd.tensor_tensor(lo[:, k % 2, n], raw[:, k, n],
                                            hi[:, k, n].bitcast(F32), ALU.subtract)\
                        .then_inc(lo_done[k], 1)

            for k in range(4):
                take_lo(0, k, True)
            with pool.Fori(1, ROUNDS) as i:
                for k in range(4):
                    take_lo(i, k, False)

        @block.scalar
        def _(act):
            chain = Chain(act, ach)
            act.dma_start(cons_sb[:], cons).then_inc(got_const, 16)
            act.dma_start(cols_sb[:], cols).then_inc(got_const, 16)

            ahead = set()

            def take_hi(i, k, first=False):
                if isinstance(i, int) and (i, k) in ahead:
                    return
                act.wait_ge(loaded[k], i * 16 + 16)
                if not first:
                    act.wait_ge(unit_used, i * 4 + (k - 3))
                nc.scalar.activation(hi[:, k, :], raw[:, k, :], ACT.Copy).then_inc(hi_done, 1)

            def take_ahead(i, *ks):
                for k in ks:
                    take_hi(i, k)
                    ahead.add((i, k))

            def norm(n, gain, following=None):
                if n:
                    take_ahead(ROUND0[following], 0, 1)
                for tt in range(TT):
                    if n == 0:
                        if tt == 0:
                            act.wait_ge(got_x, 16 * TT)
                    else:
                        act.wait_ge(h_new, 2 * (n - 1) + tt + 1)
                    nc.scalar.activation(xn[:, tt, :], hx[:, tt, :], ACT.Square,
                                         accum_out=st(SS + tt)).then_inc(ss_done, 1)
                act.wait_ge(ms_done, n + 1)
                nc.scalar.activation(st(RT, 2), st(MS, 2), ACT.Sqrt).then_inc(rms_done, 1)
                if n:
                    take_ahead(ROUND0[following], 2, 3)
                else:
                    take_hi(0, 0, True)
                    take_hi(0, 1, True)
                for kb in range(KB):
                    act.wait_ge(tr_done, 16 * n + kb + 1)
                    nc.scalar.activation(xh[:, kb, :], tr_slot(kb % 8), ACT.Copy,
                                         scale=col(gain, kb)).then_inc(x_hi, 1)

            act.wait_ge(got_const, 32)
            lam = col("lam", 0, 16)
            chain.link(nc.scalar.activation(st(LAMW, 16), lam, ACT.Abs))
            nc.scalar.activation(st(LAMW, 16), st(LAMW, 16), ACT.Exp, scale=-1.0).then_inc(soft_e, 1)
            norm(0, "g_mix")
            take_hi(0, 2, True)
            take_hi(0, 3, True)
            act.wait_ge(tr_done, 16)
            act.dma_start(wg[:], w_gates).then_inc(got_wg, 16)
            act.dma_start(band_sb[:], band).then_inc(got_wg, 16)

            def tanh_group(g, n):
                z, which = g // 2, g % 2
                if n == 0:
                    act.wait_ge(gates_done, g + 1)
                    if g == 0:
                        act.wait_ge(soft_c, 1)
                to = (th_a, th_i)[which][:, z, n, :]
                nc.scalar.activation(to, ps[:, 4 + n // 2, (n % 2) * T:(n % 2) * T + T], ACT.Tanh,
                                     scale=0.5, bias=st(BA2 + 16 * which + 8 * z + n))\
                    .then_inc(tanh_done, 1)

            def decay(z, n):
                c, t = 8 * z + n, (t_z0, t_z1)[z]
                if n == 0:
                    act.wait_ge(tanh_done, 16 * z + 8)
                    act.wait_ge(conv_done, 8)
                nc.scalar.activation(t[:, n, :], th_a[:, z, n, :], ACT.Tanh, scale=st(CSP + c),
                                     bias=st(CSP + c)).then_inc(ach, 1)
                chain.n += 1
                chain.wait()
                nc.scalar.activation(th_a[:, z, n, :], th_a[:, z, n, :], ACT.Exp,
                                     scale=st(CSP + 16 + c), bias=st(CSP + 16 + c))\
                    .then_inc(decay_done, 1)

            def root(z):
                t = (t_z0, t_z1)[z]
                act.wait_ge(z_done, z + 1)
                nc.scalar.activation(t[:], t[:], ACT.Sqrt).then_inc(sqrt_done, 1)

            def gelu(b):
                act.wait_ge(unit_used, after("in1", 18 + 2 * b))
                nc.scalar.activation(yg[:, b, :], t_bank(b % 4), ACT.Gelu_apprx_tanh)\
                    .then_inc(free_a, 1)

            def bias_load():
                act.wait_ge(gates_done, 4)
                act.dma_start(bias[:], rpb).then_inc(got_bias, 16)

            def attend(n0, heads, slots, times):
                s_sb, p_sb_, pt = slots

                def exps(h):
                    n = n0 + h
                    act.wait_ge(at_m, n + 1)
                    for qt in range(TT):
                        if times is None:
                            ins = nc.scalar.activation(
                                p_sb_[:, h % 2, qt, :], s_sb[:, h % 2, qt, :], ACT.Exp,
                                bias=st(NM + 2 * (h % 4) + qt),
                                accum_out=st(SM + 2 * (h % 4) + qt))
                        else:
                            ins = nc.scalar.activation(
                                p_sb_[:, h % 2, qt, :], s_sb[:, h % 2, qt, :], ACT.Exp,
                                bias=st(NM + 2 * (h % 4) + qt))
                    ins.then_inc(at_e, 1)

                def copy_turned(h):
                    n = n0 + h
                    act.wait_ge(at_t, n + 1)
                    if h >= 2:
                        act.wait_ge(at_o, n - 1)
                    nc.scalar.activation(pt[:, h % 2, :, :],
                                         ps[:, 6, :].rearrange("p (a b) -> p a b", a=2),
                                         ACT.Copy).then_inc(at_c, 1)
                    if times is not None:
                        act.wait_ge(at_o, n + 1)
                        nc.scalar.activation(xh[:, 4 + h, :], ps[:, 7, 0:T], ACT.Copy)\
                            .then_inc(x_hi, 1)

                return exps, copy_turned

            def mo_root(branch):
                act.wait_ge(mo_ms, branch + 1)
                nc.scalar.activation(mo_r[:, branch, :], mo_r[:, branch, :], ACT.Sqrt)\
                    .then_inc(mo_rt, 1)

            def mo_split(branch):
                act.wait_ge(mo_ready, 1 + branch)
                src, kb0 = ((xc, 8), (attn_t, 0))[branch]
                for n in range(8):
                    nc.scalar.activation(xh[:, kb0 + n, :], src[:, n, :], ACT.Copy,
                                         scale=col("g_mo", kb0 + n)).then_inc(x_hi, 1)

            exps, copy_turned = attend(0, HEADS1, at1, None)
            tasks = {}

            def task(u, *what):
                tasks.setdefault(u, []).append(what)

            for g, u0 in enumerate((23, 27, 31, 35)):
                for n in range(8):
                    task(u0 + n // 2, tanh_group, g, n)
            for z, u0 in enumerate((27, 35)):
                for n in range(8):
                    task(u0 + n, decay, z, n)
            for b in range(8):
                task(2 * b + 21, gelu, b)
            task(36, bias_load)
            task(43, root, 0)
            task(46, root, 1)
            task(54, mo_root, 0)
            for h in range(HEADS1 - 2):
                task(57 + 4 * h, exps, h)
                task(59 + 4 * h, copy_turned, h)
            for u in range(4, 80):
                take_hi(u // 4, u % 4)
                for f, *a in tasks.get(u, []):
                    f(*a)
            r0 = ROUND0["out1"]
            exps(HEADS1 - 2)
            copy_turned(HEADS1 - 2)
            take_ahead(r0, 0)
            exps(HEADS1 - 1)
            take_ahead(r0, 1)
            copy_turned(HEADS1 - 1)
            act.wait_ge(unit_used, after("in1", 80))
            mo_split(0)
            mo_root(1)
            take_ahead(r0, 2, 3)
            mo_split(1)
            act.wait_ge(x_lo, 32)
            act.dma_start(gbc[:], gains[0]).then_inc(got_gain, 16)

            def post_squares(name):
                per = 22 if name == "down" else 8
                a0 = {"out1": 8, "down": 56}[name]

                def squares(where):
                    pair = where % 2
                    act.wait_ge(unit_used, after(name, per * (where + 1)))
                    if where >= 2:
                        act.wait_ge(free_a, a0 + where - 1)
                    for tt in range(TT):
                        ins = nc.scalar.activation(ps[:, 4 + 2 * pair + tt, :],
                                                   ps[:, 2 * pair + tt, :],
                                                   ACT.Square, accum_out=st(SSP + 4 * tt + where))
                    ins.then_inc(free_a, 1)
                return squares

            squares = post_squares("out1")
            r0 = ROUND0["out1"]
            for c in range(4):
                for k in range(4):
                    take_hi(r0 + 2 * c, k)
                if c:
                    squares(c - 1)
                for k in range(4):
                    take_hi(r0 + 2 * c + 1, k)
            squares(3)

            def post_root(n):
                act.wait_ge(act_post, 2 * n + 1)
                nc.scalar.activation(st(RT, 2), st(MS, 2), ACT.Sqrt).then_inc(act_post, 1)

            post_root(0)
            norm(1, "g_ffn", "ffn")

            r0 = ROUND0["ffn"]

            def silu(f, s):
                act.wait_ge(unit_used, f * 4 + after("ffn", 2))
                act.wait_ge(prod_done, f - 1) if not isinstance(f, int) or f >= 2 else None
                nc.scalar.activation(sil[:, s, :], t_bank(2 * s), ACT.Silu).then_inc(free_a, 1)

            def ffn_pair(f0, r, first=False, last=False):
                for k in range(4):
                    take_hi(r, k)
                if not first:
                    silu(f0 - 1, 1)
                for k in range(4):
                    take_hi(r + 1, k)
                silu(f0, 0)
                if last:
                    silu(f0 + 1, 1)

            ffn_pair(0, r0, first=True)
            with act.Fori(1, FB // 2 - 1) as i:
                ffn_pair(i * 2, i * 2 + r0)
            ffn_pair(FB - 2, r0 + FB - 2, last=True)
            act.dma_start(gbc[:], gains[1]).then_inc(got_gain, 16)
            nc.scalar.activation(st(WARM), ones[:, 0:1], ACT.Sqrt)
            squares = post_squares("down")
            r0 = ROUND0["down"]
            for c in range(4):
                with act.Fori(0, 5) as i:
                    for k in range(4):
                        q = 22 * c + k
                        take_hi(i + (r0 + q // 4), q % 4)
                for u in range(22 * c + 20, 22 * c + 22):
                    take_hi(r0 + u // 4, u % 4)
                if c:
                    squares(c - 1)
            squares(3)
            act.dma_start(w_pr[:], w_proj).then_inc(got_ple, 16)
            act.dma_start(p_sb[:], p_t).then_inc(got_ple, 16)
            act.dma_start(wgd[:], w_gd).then_inc(got_in2, 16)
            act.dma_start(up[:], up_fb).then_inc(got_in2, 16)
            act.dma_start(qkg[:], qk_gain).then_inc(got_in2, 16)
            post_root(1)
            norm(2, "g_ple", "gate")
            act.wait_ge(h_new, 4)
            act.dma_start(gbc[:], gains[2]).then_inc(got_gain, 16)
            r0 = ROUND0["gate"]

            def sigmoids(c):
                act.wait_ge(unit_used, after("gate", 8 * c + 8))
                if c >= 2:
                    act.wait_ge(ple_free, c - 1)
                    act.wait_ge(pz_squared, c - 1)
                for tt in range(TT):
                    ins = nc.scalar.activation(sig[:, c % 2, tt, :], ps[:, 2 * (c % 2) + tt, :],
                                               ACT.Sigmoid)
                ins.then_inc(free_a, 1)

            def gated_squares(c):
                act.wait_ge(ple_free, c + 1)
                for tt in range(TT):
                    ins = nc.scalar.activation(sig[:, c % 2, tt, :], pz[:, tt, :], ACT.Square,
                                               accum_out=st(SSP + 4 * tt + c))
                ins.then_inc(pz_squared, 1)

            for c in range(4):
                for k in range(4):
                    take_hi(r0 + 2 * c, k)
                if c:
                    sigmoids(c - 1)
                for k in range(4):
                    take_hi(r0 + 2 * c + 1, k)
                if c:
                    gated_squares(c - 1)
            sigmoids(3)
            gated_squares(3)
            post_root(2)
            norm(3, "g_n1", "in2")

            def log_sigmoid_parts():
                act.wait_ge(g_pe, 2)
                for m in range(4):
                    ins = nc.scalar.activation(g1[:, m, :], tr_slot(4 + m), ACT.Abs,
                                               bias=col("gla_b", m))
                chain.link(ins)
                chain.link(nc.scalar.activation(g1[:], g1[:], ACT.Exp, scale=-1.0))
                nc.scalar.activation(g1[:], g1[:], ACT.Ln, bias=1.0).then_inc(g_act, 1)

            def last_of(d):
                v = g1[:, 2 * d:2 * d + 2, :].rearrange("p m (c t) -> p m c t", t=64)
                return v[:, :, :, 63 if d == 0 else 0]

            def decays():
                act.wait_ge(g_dve, 3)
                nc.scalar.activation(g2[:], g1[:], ACT.Exp, scale=1.0 / 16)
                nc.scalar.activation(g3[:], g1[:], ACT.Exp, scale=-1.0 / 16)
                for d in range(2):
                    nc.scalar.activation(st(GDEC + 8 * d, 8).rearrange("p (m c) -> p m c", c=4),
                                         last_of(d), ACT.Exp, scale=1.0 / 16)
                nc.scalar.activation(g4[:], g4[:], ACT.Exp, scale=1.0 / 16).then_inc(g_act, 1)

            def silu_r():
                act.wait_ge(unit_used, after("in2", 24))
                for tt in range(TT):
                    ins = nc.scalar.activation(sra[:, tt, :], ps[:, 2 + tt, :], ACT.Silu)
                ins.then_inc(free_a, 1)

            def qk_squares(c):
                act.wait_ge(unit_used, after("in2", 32 + 8 * c))
                if c:
                    act.wait_ge(qk_reduced, c)
                if c == 4:
                    act.wait_ge(qk_ready, 1)
                for tt in range(TT):
                    ins = nc.scalar.activation(sqt[:, tt, :], ps[:, 2 * (c % 2) + tt, :],
                                               ACT.Square)
                ins.then_inc(free_a, 1)

            def qk_root(which):
                act.wait_ge(qk_ms, which + 1)
                nc.scalar.activation(st(SRT, 24), st(SRT, 24), ACT.Sqrt).then_inc(qk_rt, 1)

            def o_squares():
                act.wait_ge(g_dve, 9)
                nc.scalar.activation(g3[:], o_n[:].rearrange("p a (b c) -> p (a b) c", c=T),
                                     ACT.Square).then_inc(g_act, 1)

            def o_root():
                act.wait_ge(g_dve, 10)
                nc.scalar.activation(st(GRT, 8), st(GRT, 8), ACT.Sqrt).then_inc(g_act, 1)

            def q_copy(h):
                act.wait_ge(qk_turned, h + 1)
                nc.scalar.activation(q_t2[:, h, :], tr_slot(h % 8), ACT.Copy).then_inc(q_copied, 1)

            act.wait_ge(got_in2, 48)
            nc.scalar.activation(wgd_h[:], wgd[:], ACT.Copy).then_inc(g_act, 1)
            tasks = {11: [(log_sigmoid_parts,)], 15: [(decays,)], 27: [(silu_r,)],
                     61: [(qk_root, 0)], 69: [(o_squares,)], 72: [(o_root,)], 83: [(qk_root, 1)]}
            for c in range(6):
                tasks[35 + 8 * c] = [(qk_squares, c)]
            for h in range(HEADS2):
                tasks[75].append((q_copy, h))
            for u in range(96):
                take_hi(ROUND0["in2"] + u // 4, u % 4)
                for f, *a in tasks.get(u, []):
                    f(*a)
            act.wait_ge(g_pe, 7)
            act.dma_start(dil_sb[:], dil).then_inc(got_dil, 16)
            for kb in range(4):
                act.wait_ge(g_pe, 8 + kb)
                nc.scalar.activation(xh[:, kb, :], tr_slot(kb), ACT.Copy, scale=col("g_gla", kb))\
                    .then_inc(x_hi, 1)
            exps, copy_turned = attend(HEADS1, HEADS2, at2, dil_sb)
            exps(0)
            for h in range(HEADS2):
                if h + 1 < HEADS2:
                    exps(h + 1)
                copy_turned(h)
                if 1 <= h <= 4:
                    take_ahead(ROUND0["out2"], h - 1)
            act.dma_start(keys_t[:], sub_keys).then_inc(got_keys, 16)
            nc.scalar.activation(st(WARM), ones[:, 0:1], ACT.Sqrt)
            with act.Fori(1, 8) as i:
                for k in range(4):
                    take_hi(i + ROUND0["out2"], k)
            norm(4, "g_n2", "query")
            act.dma_start(spill, hx[:]).then_inc(spilled, 16)
            with act.Fori(1, 8) as i:
                for k in range(4):
                    take_hi(i + ROUND0["query"], k)
            act.wait_ge(spilled, 16)

            def expert_gelu(j, bank):
                act.wait_ge(unit_used, j * 2 + after("peer_down", 2))
                to = gm[:, j, :] if isinstance(j, int) else \
                    gm[:, bass.ds(j, 1), :].rearrange("p a t -> p (a t)")
                nc.scalar.activation(to, t_bank(bank), ACT.Gelu_apprx_tanh).then_inc(free_a, 1)

            r0 = ROUND0["peer_down"]

            def gelu_rounds(j0, r, first=False):
                for half in range(2):
                    for k in range(2):
                        take_hi(r + half, k)
                    if not (first and half == 0):
                        expert_gelu(j0 + (2 * half - 1), (2 * half - 1) % 4)
                    for k in range(2, 4):
                        take_hi(r + half, k)
                    expert_gelu(j0 + 2 * half, 2 * half)

            gelu_rounds(0, r0, True)
            with act.Fori(1, 7) as i:
                gelu_rounds(i * 4, i * 2 + r0)
            act.wait_ge(route_m, 1)
            nc.scalar.activation(route[:, 2, :], route[:, 2, :], ACT.Exp).then_inc(route_e, 1)
            with act.Fori(7, 16) as i:
                gelu_rounds(i * 4, i * 2 + r0)
            act.wait_ge(routed, 1)
            with act.Fori(16, 32) as i:
                gelu_rounds(i * 4, i * 2 + r0)
            expert_gelu(127, 3)
            r0 = ROUND0["peer_up"]
            act.wait_ge(unit_used, after("peer_up", 0))
            act.dma_start(hx_end[:], spill).then_inc(got_h, 16)

            def up_round(i, first=False, half=0):
                for k in range(4):
                    if not first:
                        act.wait_ge(unit_used, i * 4 + after("peer_up", k - 3))
                    j = i * 4 + (k - half * NKEY)
                    h = gm[:, j, :] if isinstance(j, int) else \
                        gm[:, bass.ds(j, 1), :].rearrange("p a t -> p (a t)")
                    nc.scalar.activation(hg_h[:, k, :], h, ACT.Copy).then_inc(hh_done, 1)
                    take_hi(i + r0, k)

            act.wait_ge(gated_done, T // 8)
            up_round(0, True)
            with act.Fori(1, 16) as i:
                up_round(i)
            act.wait_ge(gated_done, T // 4)
            with act.Fori(16, 32) as i:
                up_round(i)
            with act.Fori(32, 64) as i:
                up_round(i, half=1)

        @block.vector
        def _(dve):
            chain = Chain(dve, dch)
            link = chain.link
            V = nc.vector

            def norm(n, gain):
                dve.wait_ge(ss_done, 2 * n + 2)
                V.tensor_scalar(st(MS, 2), st(SS, 2), 1.0 / D, EPS, ALU.mult, ALU.add)\
                    .then_inc(ms_done, 1)
                dve.wait_ge(rms_done, n + 1)
                link(V.reciprocal(st(RI, 2), st(RT, 2)))
                for half in range(2):
                    f = slice(half * D // 2, (half + 1) * D // 2)
                    for tt in range(TT):
                        V.tensor_scalar(xn[:, tt, f], hx[:, tt, f], st(RI + tt), None, ALU.mult)\
                            .then_inc(xn_done, 1)
                for kb in range(KB):
                    dve.wait_ge(x_hi, 16 * BUILD[n] + kb + 1)
                    V.scalar_tensor_tensor(out=xl[:, kb, :], in0=tr_slot(kb % 8),
                                           scalar=col(gain, kb), in1=xh[:, kb, :].bitcast(F32),
                                           op0=ALU.mult, op1=ALU.subtract).then_inc(x_lo, 1)

            BUILD = [0, 2, 3, 4, 6]

            V.memset(xr[:, :, 0:2], 0.0).then_inc(dch, 1)
            V.memset(xr[:, :, 258:260], 0.0).then_inc(dch, 1)
            chain.n += 2
            dve.wait_ge(got_const, 32)
            dve.wait_ge(soft_e, 1)
            e, s, s2, acc = (st(LAMW + 16 * i, 16) for i in range(4))
            link(V.tensor_scalar(s, e, 2.0, None, ALU.add))
            link(V.reciprocal(s, s))
            link(V.tensor_tensor(s, s, e, ALU.mult))
            link(V.tensor_tensor(s2, s, s, ALU.mult))
            link(V.tensor_scalar(acc, s2, 2.0 / 15, 2.0 / 13, ALU.mult, ALU.add))
            for odd in (11, 9, 7, 5, 3, 1):
                link(V.tensor_tensor(acc, acc, s2, ALU.mult))
                link(V.tensor_scalar(acc, acc, 2.0 / odd, None, ALU.add))
            link(V.tensor_tensor(acc, acc, s, ALU.mult))
            link(V.tensor_scalar(s, col("lam", 0, 16), -1.0, 0.0, ALU.mult, ALU.max))
            link(V.tensor_tensor(acc, acc, s, ALU.add))
            V.tensor_scalar(st(CSP, 16), acc, 4.0, None, ALU.mult).then_inc(dch, 1)
            V.tensor_scalar(st(CSP + 16, 16), acc, -4.0, None, ALU.mult).then_inc(dch, 1)
            V.tensor_scalar(st(BA2, 32), col("b_a", 0, 32), 0.5, None, ALU.mult).then_inc(dch, 1)
            chain.n += 3
            chain.wait()
            V.memset(st(LAMW), 0.0).then_inc(soft_c, 1)

            norm(0, "g_mix")

            def block_copy(b, to, scale=None):
                dve.wait_ge(unit_used, after("in1", 2 * b + 2))
                if scale is None:
                    ins = V.tensor_copy(to, t_bank(b % 4))
                else:
                    ins = V.tensor_scalar(to, t_bank(b % 4), scale, None, ALU.mult)
                ins.then_inc(free_d, 1)
                return ins

            for n in range(8):
                block_copy(n, xr[:, n, 2:258])
                dve.wait_ge(free_d, n + 1)
                link(V.tensor_scalar(xc[:, n, :], xr[:, n, 0:T], col("conv_w", n),
                                     col("conv_b", n), ALU.mult, ALU.add))
                for j in range(1, 4):
                    ins = V.scalar_tensor_tensor(out=xc[:, n, :], in0=xr[:, n, j:j + T],
                                                 scalar=col("conv_w", 8 * j + n),
                                                 in1=xc[:, n, :], op0=ALU.mult, op1=ALU.add)
                    if j < 3:
                        link(ins)
                    else:
                        ins.then_inc(conv_done, 1)

            def z_step(z):
                t = (t_z0, t_z1)[z]
                dve.wait_ge(decay_done, 8 * z + 8)
                dve.wait_ge(tanh_done, 16 * z + 16)
                dve.wait_ge(conv_done, 8)
                sq = k_t
                link(V.tensor_tensor(sq[:], th_a[:, z], th_a[:, z], ALU.mult))
                V.scalar_tensor_tensor(out=t[:], in0=sq[:], scalar=1.0, in1=t[:], op0=ALU.add,
                                       op1=ALU.mult).then_inc(z_done, 1)
                link(V.scalar_tensor_tensor(out=th_i[:, z], in0=th_i[:, z], scalar=1.0, in1=xc[:],
                                            op0=ALU.add, op1=ALU.mult))
                dve.wait_ge(z_done, z + 1)

            def v_copy(c):
                dve.wait_ge(unit_used, after("in1", 40 + 8 * c))
                for tt in range(TT):
                    ins = V.tensor_copy(v_n[:, tt, c * NCH:(c + 1) * NCH], ps[:, 2 * c + tt, :])
                ins.then_inc(free_d, 1)

            def qk_copy(m):
                block_copy(24 + m, (q_t, k_t)[m % 2][:, m // 2, :], None if m % 2 else SCALE)

            def scan(z):
                t = (t_z0, t_z1)[z]
                dve.wait_ge(sqrt_done, z + 1)
                link(V.scalar_tensor_tensor(out=t[:], in0=t[:], scalar=0.5, in1=th_i[:, z],
                                            op0=ALU.mult, op1=ALU.mult))
                for n in range(8):
                    if z == 0:
                        a, b, o = th_a[:, z, n, :], t[:, n, :], th_i[:, z, n, :]
                    else:
                        a, b, o = (m[:, n, ::-1] for m in (th_a[:, z], t, th_i[:, z]))
                    chain.inc(V.tensor_tensor_scan(o, a, b, 0.0, ALU.mult, ALU.add))
                chain.wait()

            z_step(0)
            v_copy(0)
            z_step(1)
            dve.wait_ge(got_bias, 16)
            dve.wait_ge(got_wg, 32)
            for h in range(HEADS1):
                chain.inc(V.tensor_tensor(
                    bias[:, h].rearrange("p a (r c) -> p (a r) c", c=64),
                    bias[:, h].rearrange("p a (r c) -> p (a r) c", c=64),
                    band_sb[:].unsqueeze(1).to_broadcast([P, 8, 64]), ALU.add))
            scan(0)
            v_copy(1)
            scan(1)
            qk_copy(0)
            link(V.tensor_tensor(th_i[:, 0], th_i[:, 0], th_i[:, 1], ALU.add))
            dve.wait_ge(free_a, 8)
            link(V.tensor_tensor(xc[:], th_i[:, 0], yg[:], ALU.mult))
            qk_copy(1)
            V.tensor_tensor(th_i[:, 1], xc[:], xc[:], ALU.mult).then_inc(mo_sq, 1)

            def attend(n0, heads, slots, bias_of, times):
                s_sb, p_sb_, pt = slots

                def first(h):
                    n = n0 + h
                    dve.wait_ge(at_s, n + 1)
                    if h >= 2:
                        dve.wait_ge(at_e, n - 1)
                    V.tensor_tensor(s_sb[:, h % 2], ps[:, 4 + h % 2, :].rearrange(
                        "p (a b) -> p a b", a=2), bias_of(h), ALU.add).then_inc(at_b, 1)
                    dve.wait_ge(at_b, n + 1)
                    V.tensor_reduce(st(NM + 2 * (h % 4), 2), s_sb[:, h % 2], AX.X, ALU.max,
                                    negate=True).then_inc(at_m, 1)

                def second(h):
                    n = n0 + h
                    dve.wait_ge(at_e, n + 1)
                    sm, si = SM + 2 * (h % 4), SI + 2 * (h % 4)
                    if times is not None:
                        for qt in range(TT):
                            chain.inc(V.scalar_tensor_tensor(
                                out=p_sb_[:, h % 2, qt], in0=p_sb_[:, h % 2, qt], scalar=1.0,
                                in1=times[:, qt], op0=ALU.mult, op1=ALU.mult,
                                accum_out=st(sm + qt)))
                        chain.wait()
                    link(V.reciprocal(st(si, 2), st(sm, 2)))
                    for qt in range(TT):
                        ins = V.tensor_scalar(p_sb_[:, h % 2, qt], p_sb_[:, h % 2, qt],
                                              st(si + qt), None, ALU.mult)
                        if qt == 0:
                            chain.inc(ins)
                    ins.then_inc(at_p, 1)

                return first, second

            def head_out(h):
                dve.wait_ge(at_o, h + 1)
                V.tensor_copy(attn_t[:, h, :], ps[:, 7, 0:T]).then_inc(at_f, 1)
                dve.wait_ge(at_f, h + 1)
                to = sq_sum if h == 0 else sq_one
                ins = V.tensor_tensor(to[:], attn_t[:, h, :], attn_t[:, h, :], ALU.mult)
                if h:
                    link(ins)
                    ins = V.tensor_tensor(sq_sum[:], sq_sum[:], sq_one[:], ALU.add)
                if h < HEADS1 - 1:
                    link(ins)
                else:
                    ins.then_inc(mo_sq, 1)

            def mo_mean(branch):
                dve.wait_ge(mo_sum, branch + 1)
                V.tensor_scalar(mo_r[:, branch, :], ps[:, SUM_BANK[branch], 0:T], 1.0 / 1024, EPS,
                                ALU.mult, ALU.add).then_inc(mo_ms, 1)

            def mo_scale(branch):
                dve.wait_ge(mo_rt, branch + 1)
                link(V.reciprocal(mo_r[:, branch, :], mo_r[:, branch, :]))
                m = (xc, attn_t)[branch]
                V.tensor_tensor(m[:], m[:], mo_r[:, branch, :].unsqueeze(1).to_broadcast([P, 8, T]),
                                ALU.mult).then_inc(mo_ready, 1)

            def mo_lo(branch, blocks):
                src, kb0 = ((xc, 8), (attn_t, 0))[branch]
                for n in blocks:
                    dve.wait_ge(x_hi, 16 + 8 * branch + n + 1)
                    V.scalar_tensor_tensor(out=xl[:, kb0 + n, :], in0=src[:, n, :],
                                           scalar=col("g_mo", kb0 + n),
                                           in1=xh[:, kb0 + n, :].bitcast(F32), op0=ALU.mult,
                                           op1=ALU.subtract).then_inc(x_lo, 1)

            first, second = attend(0, HEADS1, at1, lambda h: bias[:, h], None)
            chain.wait()
            for h in range(HEADS1):
                if h == 0:
                    qk_copy(2)
                    mo_mean(0)
                elif h < HEADS1 - 1:
                    qk_copy(2 * h + 2)
                first(h)
                if h:
                    head_out(h - 1)
                second(h)
                if h < HEADS1 - 1:
                    qk_copy(2 * h + 3)
                if h == 1:
                    mo_scale(0)
            head_out(HEADS1 - 1)
            mo_lo(0, range(4))
            mo_mean(1)
            mo_lo(0, range(4, 8))
            mo_scale(1)
            mo_lo(1, range(8))
            def post_mean():
                link(V.tensor_reduce(st(SS, 2), st(SSP, 8).rearrange("p (a b) -> p a b", a=2),
                                     AX.X, ALU.add))
                V.tensor_scalar(st(MS, 2), st(SS, 2), 1.0 / D, EPS, ALU.mult, ALU.add)\
                    .then_inc(act_post, 1)

            def post_chunks(name, n):
                dve.wait_ge(got_gain, 16 * (n + 1))
                for c in range(4):
                    dve.wait_ge(free_a, {"out1": 8, "down": 56}[name] + c + 1)
                    if c == 3:
                        post_mean()
                    for tt in range(TT):
                        ins = V.tensor_tensor(y[:, tt, c * NCH:(c + 1) * NCH],
                                              ps[:, 2 * (c % 2) + tt, :],
                                              gbc[:, c * NCH:(c + 1) * NCH], ALU.mult)
                        if tt == 0:
                            chain.inc(ins)
                    ins.then_inc(free_d, 1)
                chain.wait()

            def post(n, frees):
                dve.wait_ge(free_d, frees)
                dve.wait_ge(act_post, 2 * n + 2)
                link(V.reciprocal(st(RI, 2), st(RT, 2)))
                for tt in range(TT):
                    V.scalar_tensor_tensor(out=hx[:, tt], in0=y[:, tt], scalar=st(RI + tt),
                                           in1=hx[:, tt], op0=ALU.mult, op1=ALU.add)\
                        .then_inc(h_new, 1)

            post_chunks("out1", 0)
            post(0, 30)
            norm(1, "g_ffn")

            def hidden(f, s, first=False):
                dve.wait_ge(unit_used, f * 4 + after("ffn", 4))
                dve.wait_ge(free_a, f + 13)
                V.tensor_tensor(prod[:, s, :], t_bank(2 * s + 1), sil[:, s, :], ALU.mult)\
                    .then_inc(prod_done, 1)
                dve.wait_ge(prod_done, f + 1)
                V.tensor_copy(hid_h[:, bass.ds(f, 1), :].rearrange("p a t -> p (a t)")
                              if not isinstance(f, int) else hid_h[:, f, :], prod[:, s, :])\
                    .then_inc(hid_hi, 1)
                dve.wait_ge(hid_hi, f + 1)
                V.tensor_tensor(hid_l[:, bass.ds(f, 1), :].rearrange("p a t -> p (a t)")
                                if not isinstance(f, int) else hid_l[:, f, :], prod[:, s, :],
                                (hid_h[:, bass.ds(f, 1), :].rearrange("p a t -> p (a t)")
                                 if not isinstance(f, int) else hid_h[:, f, :]).bitcast(F32),
                                ALU.subtract).then_inc(free_d, 1)
                dve.wait_ge(free_d, f + 31)

            with dve.Fori(0, FB // 2) as i:
                for s in range(2):
                    hidden(i * 2 + s, s)
            post_chunks("down", 1)
            post(1, 78)
            norm(2, "g_ple")
            dve.wait_ge(got_gain, 48)
            for c in range(4):
                dve.wait_ge(free_a, 60 + c + 1)
                dve.wait_ge(ple_done, c + 1)
                if c:
                    dve.wait_ge(pz_squared, c)
                    chain.wait()
                for tt in range(TT):
                    ins = V.tensor_tensor(pz[:, tt, :], ps[:, 4 + 2 * (c % 2) + tt, :],
                                          sig[:, c % 2, tt, :], ALU.mult)
                    if tt == 0:
                        chain.inc(ins)
                ins.then_inc(ple_free, 1)
                dve.wait_ge(ple_free, c + 1)
                chain.wait()
                for tt in range(TT):
                    chain.inc(V.tensor_tensor(y[:, tt, c * NCH:(c + 1) * NCH], pz[:, tt, :],
                                              gbc[:, c * NCH:(c + 1) * NCH], ALU.mult))
            dve.wait_ge(pz_squared, 4)
            post_mean()
            chain.wait()
            post(2, 78)
            norm(3, "g_n1")

            dve.wait_ge(g_act, 1)
            V.tensor_tensor(wgd_l[:], wgd[:], wgd_h[:].bitcast(F32), ALU.subtract).then_inc(g_dve, 1)
            dve.wait_ge(g_pe, 1)
            V.tensor_copy(gd_t[:], ps[0:32, 4, 0:T]).then_inc(g_dve, 1)

            def t_copy(b, to):
                dve.wait_ge(unit_used, after("in2", 2 * b + 2))
                V.tensor_copy(to, t_bank(b)).then_inc(free_d, 1)

            t_copy(0, qa_t[:, 0, :])
            t_copy(1, qa_t[:, 1, :])
            t_copy(2, ka_t[:, 0, :])
            t_copy(3, ka_t[:, 1, :])
            dve.wait_ge(g_act, 2)
            for m in range(4):
                chain.inc(V.tensor_scalar(g2[:, m, :], tr_slot(4 + m), col("gla_b", m), 0.0,
                                          ALU.add, ALU.min))
            chain.wait()
            link(V.tensor_tensor(g2[:], g2[:], g1[:], ALU.subtract))
            for m in range(4):
                if m < 2:
                    o, a = g1[:, m, :], g2[:, m, :]
                else:
                    o, a = g1[:, m, ::-1], g2[:, m, ::-1]
                chain.inc(V.tensor_tensor_scan(o, con("scan"), a, 0.0, ALU.mult, ALU.add))
            chain.wait()
            for d in range(2):
                v = g1[:, 2 * d:2 * d + 2, :].rearrange("p m (c t) -> p (m c) t", t=64)
                at_end = v[:, :, 63:64] if d == 0 else v[:, :, 0:1]
                ins = V.tensor_tensor(
                    g4[:, 2 * d:2 * d + 2, :].rearrange("p m (c t) -> p (m c) t", t=64),
                    at_end.to_broadcast([P, 8, 64]), v, ALU.subtract)
                if d == 0:
                    chain.inc(ins)
            ins.then_inc(g_dve, 1)

            def n_copy(n, to):
                dve.wait_ge(unit_used, after("in2", 16 + 8 * n))
                for tt in range(TT):
                    ins = V.tensor_copy(to(tt), ps[:, 2 * (n % 2) + tt, :])
                ins.then_inc(free_d, 1)

            def qk_chunk(c):
                dve.wait_ge(free_a, 66 + c)
                n_copy(2 + c, lambda tt: qk_n[c // 3][:, tt, (c % 3) * NCH:(c % 3 + 1) * NCH])

            def qk_reduce(c):
                dve.wait_ge(free_a, 66 + c)
                for tt in range(TT):
                    ins = V.tensor_reduce(st(SSQ + 24 * (c // 3) + 12 * tt + 4 * (c % 3), 4),
                                          sqt[:, tt, :].rearrange("p (h e) -> p h e", e=HD),
                                          AX.X, ALU.add)
                    if tt == 0:
                        chain.inc(ins)
                ins.then_inc(qk_reduced, 1)

            def qk_mean(which):
                dve.wait_ge(qk_reduced, 3 * which + 3)
                if which:
                    dve.wait_ge(qk_ready, 1)
                V.tensor_scalar(st(SRT, 24), st(SSQ + 24 * which, 24), 1.0 / HD, EPS, ALU.mult,
                                ALU.add).then_inc(qk_ms, 1)

            def qk_normalise(which):
                dve.wait_ge(qk_rt, which + 1)
                inv = st(SSQ + 24 * which, 24)
                link(V.reciprocal(inv, st(SRT, 24)))
                if which == 0:
                    link(V.tensor_scalar(inv, inv, SCALE, None, ALU.mult))
                full = qk_n[which][:].rearrange("p a (h e) -> p (a h) e", e=HD)
                link(V.tensor_tensor(full, full, inv.unsqueeze(2).to_broadcast([P, 24, HD]),
                                     ALU.mult))
                link(V.tensor_tensor(full, full, qkg[:, which, :].unsqueeze(1).to_broadcast(
                    [P, 24, HD]), ALU.mult))
                for tt in range(TT):
                    v = qk_n[which][:, tt, :].rearrange("p (h e) -> p h e", e=HD)
                    x1, x2 = v[:, :, 0:16], v[:, :, 16:32]
                    cos, sin = (con(n)[:, 16 * tt:16 * tt + 16].unsqueeze(1).to_broadcast(
                        [P, 12, 16]) for n in ("cos", "sin"))
                    for k, (a, b) in enumerate(((x1, cos), (x2, sin), (x2, cos), (x1, sin))):
                        chain.inc(V.tensor_tensor(rope_t[:, k], a, b, ALU.mult))
                    chain.wait()
                    chain.inc(V.tensor_tensor(x1, rope_t[:, 0], rope_t[:, 1], ALU.subtract))
                    ins = V.tensor_tensor(x2, rope_t[:, 2], rope_t[:, 3], ALU.add)
                    if tt == 0:
                        link(ins)
                ins.then_inc(qk_ready, 1)

            n_copy(0, lambda tt: va[:, tt, :])
            dve.wait_ge(g_act, 3)
            for d in range(2):
                h = slice(2 * d, 2 * d + 2)
                chain.inc(V.scalar_tensor_tensor(
                    out=g2[:, h, :], in0=g2[:, h, :], scalar=64 ** -0.5, in1=qa_t[:], op0=ALU.mult,
                    op1=ALU.mult))
                chain.inc(V.tensor_tensor(g3[:, h, :], g3[:, h, :], ka_t[:], ALU.mult))
                ins = V.tensor_tensor(g4[:, h, :], g4[:, h, :], ka_t[:], ALU.mult)
                if d == 0:
                    chain.inc(ins)
            ins.then_inc(g_dve, 1)
            qk_chunk(0)
            dve.wait_ge(g_pe, 3)
            link(V.tensor_scalar(sc_t[:], ps[:, 4:8, :], 3e38, -3e38, ALU.min, ALU.max))
            for b in range(4):
                v = sc_t[:, b, :].rearrange("p (d h q) -> p d h q", d=2, h=2)
                ins = V.tensor_tensor(v, v, con("causal").rearrange("p (d q) -> p d q", d=2)
                                      .unsqueeze(2).to_broadcast([P, 2, 2, P]), ALU.mult)
                if b < 3:
                    chain.inc(ins)
            ins.then_inc(g_dve, 1)
            qk_reduce(0)
            qk_chunk(1)
            qk_reduce(1)
            dve.wait_ge(g_pe, 4)
            V.tensor_copy(kst[:].rearrange("p a m k -> p a (m k)"), ps[:, 4:6, :]).then_inc(g_dve, 1)
            qk_chunk(2)
            qk_reduce(2)
            qk_mean(0)

            def states(d):
                dve.wait_ge(g_pe, 5 + d)
                for n in range(3):
                    c = n if d == 0 else 3 - n
                    for half in range(2):
                        at, m = inc_at(d, c, half), 2 * d + half
                        for hd in range(2):
                            rows = slice(64 * hd, 64 * hd + 64)
                            add = at[rows, hd * P:(hd + 1) * P]
                            new = state[rows, d, n, half, :]
                            if n == 0:
                                ins = V.tensor_copy(new, add)
                            else:
                                ins = V.scalar_tensor_tensor(
                                    out=new, in0=state[rows, d, n - 1, half, :],
                                    scalar=small[rows, GDEC + 4 * m + c:GDEC + 4 * m + c + 1],
                                    in1=add, op0=ALU.mult, op1=ALU.add)
                            if (n, half, hd) != (2, 1, 1):
                                chain.inc(ins)
                    if n < 2:
                        chain.wait()
                ins.then_inc(g_dve, 1)

            states(0)
            qk_chunk(3)
            qk_reduce(3)
            states(1)
            qk_normalise(0)
            qk_chunk(4)
            qk_reduce(4)
            dve.wait_ge(g_pe, 7)
            for tt in range(TT):
                ins = V.tensor_copy(
                    o_n[:, tt, :].rearrange("p (b a e) -> p a b e", a=2, b=2),
                    ps[:, 4 + 2 * tt:6 + 2 * tt, 0:T].rearrange("p a (b e) -> p a b e", b=2))
                if tt == 0:
                    chain.inc(ins)
            ins.then_inc(g_dve, 1)
            dve.wait_ge(g_act, 4)
            link(V.tensor_reduce(st(GSS, 8), g3[:].rearrange("p a (b e) -> p (a b) e", e=HD),
                                 AX.X, ALU.add))
            V.tensor_scalar(st(GRT, 8), st(GSS, 8), 1.0 / HD, EPS, ALU.mult, ALU.add)\
                .then_inc(g_dve, 1)
            qk_chunk(5)
            qk_reduce(5)
            qk_mean(1)
            dve.wait_ge(g_act, 5)
            link(V.reciprocal(st(GSS, 8), st(GRT, 8)))
            o_v = o_n[:].rearrange("p a (h e) -> p (a h) e", e=HD)
            link(V.tensor_tensor(o_v, o_v, st(GSS, 8).unsqueeze(2).to_broadcast([P, 8, HD]),
                                 ALU.mult))
            V.tensor_tensor(o_n[:], o_n[:], sra[:], ALU.mult).then_inc(g_dve, 1)
            n_copy(8, lambda tt: vn[:, tt, 0:NCH])
            qk_normalise(1)
            n_copy(9, lambda tt: vn[:, tt, NCH:2 * NCH])
            for h in range(HEADS2):
                dve.wait_ge(qk_turned, HEADS2 + h + 1)
                V.tensor_copy(k_t2[:, h, :], tr_slot((HEADS2 + h) % 8)).then_inc(k_copied, 1)
            n_copy(10, lambda tt: vn[:, tt, 2 * NCH:3 * NCH])

            for kb in range(4):
                dve.wait_ge(x_hi, 80 + kb + 1)
                V.scalar_tensor_tensor(out=xl[:, kb, :], in0=tr_slot(kb), scalar=col("g_gla", kb),
                                       in1=xh[:, kb, :].bitcast(F32), op0=ALU.mult,
                                       op1=ALU.subtract).then_inc(x_lo, 1)

            def head_out2(h):
                dve.wait_ge(x_hi, 80 + 4 + h + 1)
                V.tensor_tensor(xl[:, 4 + h, :], ps[:, 7, 0:T], xh[:, 4 + h, :].bitcast(F32),
                                ALU.subtract).then_inc(x_lo, 1)

            dve.wait_ge(got_dil, 16)
            first, second = attend(HEADS1, HEADS2, at2, lambda h: dil_sb[:, 0], dil_sb[:, 1])
            first(0)
            for h in range(HEADS2):
                if h + 1 < HEADS2:
                    first(h + 1)
                second(h)
                if h:
                    head_out2(h - 1)
            head_out2(HEADS2 - 1)
            for c in range(4):
                dve.wait_ge(unit_used, after("out2", 8 * c + 8))
                for tt in range(TT):
                    v = hx[:, tt, c * NCH:(c + 1) * NCH]
                    ins = V.tensor_tensor(v, ps[:, 2 * (c % 2) + tt, :], v, ALU.add)
                    if c == 3:
                        ins.then_inc(h_new, 1)
                if c < 3:
                    ins.then_inc(free_d, 1)
            dve.wait_ge(h_new, 8)
            norm(4, "g_n2")
            for b in range(KB):
                dve.wait_ge(unit_used, after("query", 2 * b + 2))
                V.tensor_copy(qry_t[:, b, :], t_bank(b % 4)).then_inc(free_d, 1)
            for tt in range(TT):
                lists = {16 * tt + r: ps[:, 4 + r // 4, (r % 4) * P:(r % 4 + 1) * P]
                         for r in range(16)}
                dve.wait_ge(key_scores, tt + 1)
                for r in lists:
                    chain.inc(V.max(top[:, r, 0:8], lists[r]))
                chain.wait()
                for r in lists:
                    chain.inc(V.max_index(top_u[:, r, 0:8], top[:, r, 0:8], lists[r]))
                    V.match_replace(sc_rest[:, r, :], top[:, r, 0:8], lists[r], -3e38)\
                        .then_inc(lists_read, 1)
                dve.wait_ge(lists_read, 16 * (tt + 1))
                for r in lists:
                    chain.inc(V.max(top[:, r, 8:16], sc_rest[:, r, :]))
                chain.wait()
                for r in lists:
                    chain.inc(V.max_index(top_u[:, r, 8:16], top[:, r, 8:16], sc_rest[:, r, :]))
            chain.wait()
            pairs = top[:].rearrange("p (n c) k -> p n c k", c=2)
            cand_v = cand[:].rearrange("p n (a b) -> p n a b", b=16)
            link(V.tensor_tensor(cand_v, pairs[:, :, 0, :].unsqueeze(3).to_broadcast([P, 16, 16, 16]),
                                 pairs[:, :, 1, :].unsqueeze(2).to_broadcast([P, 16, 16, 16]),
                                 ALU.add))
            link(V.tensor_copy(top_i[:], top_u[:]))
            for r in range(16):
                chain.inc(V.max(best[:, r, 0:8], cand[:, r, :]))
            chain.wait()
            for r in range(16):
                chain.inc(V.max_index(pos[:, r, 0:8], best[:, r, 0:8], cand[:, r, :]))
                chain.inc(V.match_replace(cand_rest[:, r, :], best[:, r, 0:8], cand[:, r, :],
                                          -3e38))
            chain.wait()
            for r in range(16):
                chain.inc(V.max(best[:, r, 8:16], cand_rest[:, r, :]))
            chain.wait()
            for r in range(16):
                chain.inc(V.max_index(pos[:, r, 8:16], best[:, r, 8:16], cand_rest[:, r, :]))
            V.tensor_tensor(route[:, 2, :].rearrange("p (n k) -> p n k", k=16), best[:],
                            best[:, :, 0:1].to_broadcast([P, 16, 16]), ALU.subtract)\
                .then_inc(route_m, 1)
            chain.wait()
            chain.inc(V.tensor_scalar(pos_a[:], pos[:], 4, None, ALU.logical_shift_right))
            link(V.tensor_scalar(pos_b[:], pos[:], 15, None, ALU.bitwise_and))
            chain.inc(V.tensor_copy(pos_f[:, 0, :], pos_a[:].rearrange("p a b -> p (a b)")))
            link(V.tensor_copy(pos_f[:, 1, :], pos_b[:].rearrange("p a b -> p (a b)")))
            keys_i = top_i[:].rearrange("p (n c) k -> p n c k", c=2)
            for c in range(2):
                link(V.tensor_tensor(pick[:], pos_f[:, c, :].unsqueeze(2).to_broadcast([P, 256, 16]),
                                     iota[:, 0:16].unsqueeze(1).to_broadcast([P, 256, 16]),
                                     ALU.is_equal))
                pv = pick[:].rearrange("p (n k) a -> p n k a", k=16)
                link(V.tensor_tensor(pv, pv, keys_i[:, :, c, :].unsqueeze(2).to_broadcast(
                    [P, 16, 16, 16]), ALU.mult))
                link(V.tensor_reduce(route[:, c, :], pick[:], AX.X, ALU.add))
            dve.wait_ge(route_e, 1)
            gates_v = route[:, 2, :].rearrange("p (n k) -> p n k", k=16)
            link(V.tensor_reduce(st(RSUM, 16), gates_v, AX.X, ALU.add))
            link(V.reciprocal(st(RSUM, 16), st(RSUM, 16)))
            V.tensor_tensor(gates_v, gates_v, st(RSUM, 16).unsqueeze(2).to_broadcast([P, 16, 16]),
                            ALU.mult).then_inc(route_ready, 1)
            dve.wait_ge(route_turned, 1)
            V.tensor_copy(i_t[:], ps[:, 4, 0:T])
            V.tensor_copy(j_t[:], ps[:, 5, 0:T])
            V.tensor_copy(gate_t[:, :, 0], ps[:, 6, 0:T]).then_inc(gate_split, 1)
            for part in range(2):
                dve.wait_ge(gate_split, 2 * part + 1)
                V.tensor_tensor(gate_rest[:], gate_rest[:] if part else ps[:, 6, 0:T],
                                gate_t[:, :, part], ALU.subtract).then_inc(gate_split, 1)
                dve.wait_ge(gate_split, 2 * part + 2)
                V.tensor_copy(gate_t[:, :, part + 1], gate_rest[:])\
                    .then_inc(gate_split if part == 0 else routed, 1)
            dve.wait_ge(routed, 1)

            def one_hots(g, i, n, first=False):
                s = n % HOTS
                if not first:
                    dve.wait_ge(gmat_done, i * 16 + (g * T + n - (HOTS - 1)))
                at_ = bass.ds(i * 16 + n, 1) if not isinstance(i, int) else \
                    slice(i * 16 + n, i * 16 + n + 1)
                V.tensor_scalar(hot_i[:, s, :], iota, i_t[:, at_], None, ALU.is_equal)
                V.scalar_tensor_tensor(
                    out=hot_j[:, s],
                    in0=iota[:, g * 64:g * 64 + 64].unsqueeze(1).to_broadcast([P, 3, 64]),
                    scalar=j_t[:, at_],
                    in1=gate_t[:, at_, :].rearrange("p t c -> p (t c)").unsqueeze(2)
                    .to_broadcast([P, 3, 64]), op0=ALU.is_equal, op1=ALU.mult)\
                    .then_inc(hot_done, 1)

            def gate(g, i, b):
                dve.wait_ge(gmat_done, i * 16 + (g * T + 8 * b + 8))
                first = i * 16 + 8 * b
                tokens = bass.ds(first, 8) if not isinstance(i, int) else slice(first, first + 8)
                v = gm[:, g * 64:g * 64 + 64, tokens].rearrange("p j t -> p t j")
                V.tensor_tensor(v, ps[:, 4 + b, :].rearrange("p (t j) -> p t j", j=64), v,
                                ALU.mult).then_inc(gated_done, 1)

            def sixteen(g, i, first=False):
                for n in range(16):
                    if g == 1 and n % 4 == 0:
                        hidden_lo(i * 4, n // 4)
                    one_hots(g, i, n, first and n < HOTS)
                    if n == 11:
                        gate(g, i, 0)
                    if n == 3 and not first:
                        gate(g, i - 1, 1)

            def hidden_lo(p, k):
                dve.wait_ge(hh_done, p + (k + 1))
                j = (p + k) if isinstance(p, int) else None
                h = gm[:, j, :] if j is not None else \
                    gm[:, bass.ds(p + k, 1), :].rearrange("p a t -> p (a t)")
                V.tensor_tensor(hg_l[:, k, :], h, hg_h[:, k, :].bitcast(F32), ALU.subtract)\
                    .then_inc(hl_done, 1)

            for n in range(HOTS):
                one_hots(0, 0, n, True)
            dve.wait_ge(free_a, 71 + 64)
            for n in range(HOTS, 16):
                one_hots(0, 0, n)
                if n == 11:
                    gate(0, 0, 0)
            with dve.Fori(1, 16) as i:
                sixteen(0, i)
            gate(0, 15, 1)
            dve.wait_ge(free_a, 71 + 128)
            for n in range(16):
                if n % 4 == 0:
                    hidden_lo(0, n // 4)
                one_hots(1, 0, n)
                if n == 11:
                    gate(1, 0, 0)
            with dve.Fori(1, 16) as i:
                sixteen(1, i)
            gate(1, 15, 1)
            with dve.Fori(16, 32) as i:
                for k in range(4):
                    hidden_lo(i * 4, k)

            def hidden_lo_again(i, k):
                dve.wait_ge(hh_done, i * 4 + (k + 1))
                V.tensor_tensor(hg_l[:, k, :], gm[:, bass.ds(i * 4 + (k - NKEY), 1), :].rearrange(
                    "p a t -> p (a t)"), hg_h[:, k, :].bitcast(F32), ALU.subtract)\
                    .then_inc(hl_done, 1)

            def add_residual(b):
                tt, c = out_part(b)
                v = hx_end[:, tt, c * NCH:(c + 1) * NCH]
                V.tensor_tensor(v, ps[:, b, :], v, ALU.add).then_inc(fin_done, 1)

            with dve.Fori(32, 34) as i:
                for k in range(4):
                    hidden_lo_again(i, k)
            dve.wait_ge(got_h, 16)
            dve.wait_ge(unit_used, after("peer_up", 128))
            for b in range(4):
                add_residual(b)
            with dve.Fori(34, 64) as i:
                for k in range(4):
                    hidden_lo_again(i, k)
            dve.wait_ge(unit_used, PIECES)
            for b in range(4, 8):
                add_residual(b)

        @block.tensor
        def _(pe):
            M = nc.tensor

            def exact(out_ap, a, b, n, start, stop):
                M.matmul(out_ap, a[0], b[0], start=start, stop=False)
                M.matmul(out_ap, a[0], b[1], start=False, stop=False)
                return M.matmul(out_ap, a[1], b[0], start=False, stop=stop)

            def ready(i, k, half):
                pe.wait_ge(lo_done[k], i * 2 + (half + 1))

            def t_block(i, k0, bank, norm=None):
                for half in range(2):
                    if norm is not None:
                        turn(norm, (range(12), range(12, KB))[half])
                        pe.wait_ge(x_lo, 16 * BUILD[norm] + 8 + 8 * half)
                    k = k0 + half
                    for j in range(8):
                        if j % 4 == 0:
                            ready(i, k, j // 4)
                        kb = 8 * half + j
                        w = [m[:, s, j * P:(j + 1) * P] for m, s in ((hi, k), (lo, k % 2))]
                        ins = exact(t_bank(bank), w, (xh[:, kb, :], xl[:, kb, :]), T,
                                    kb == 0, kb == KB - 1)
                        if j == 3:
                            ins.then_inc(half_used, 1)
                        if j == 7:
                            ins.then_inc(unit_used, 1)

            def n_piece(i, k, pair, kb0, first, last, a=None):
                ah, al = a or (xh, xl)
                for j in range(2):
                    ready(i, k, j)
                    for tt in range(TT):
                        act_ = [m[:, kb0 + j, tt * P:(tt + 1) * P] for m in (ah, al)]
                        w = [m[:, s, j * NCH:(j + 1) * NCH] for m, s in ((hi, k), (lo, k % 2))]
                        ins = exact(ps[:, 2 * pair + tt, :], act_, w, NCH, first and j == 0,
                                    last and j == 1)
                    ins.then_inc((half_used, unit_used)[j], 1)

            def n_chunk(i, pair, norm=None, between=None):
                for q in range(8):
                    if norm is not None and q % 4 == 0:
                        turn(norm, (range(12), range(12, KB))[q // 4])
                        pe.wait_ge(x_lo, 16 * BUILD[norm] + 8 + 2 * q)
                    if between and q == 4:
                        between()
                    n_piece(i + q // 4, q % 4, pair, 2 * q, q == 0, q == 7)

            BUILD = [0, 2, 3, 4, 6]

            def turn(n, kbs):
                for kb in kbs:
                    if kb % 8 == 0:
                        pe.wait_ge(xn_done, 4 * n + 2 + kb // 4)
                    if kb >= 4:
                        pe.wait_ge(x_lo, 16 * BUILD[n] + kb - 3)
                    for tt in range(TT):
                        ins = M.transpose(tr_slot(kb % 8)[:, tt * P:(tt + 1) * P],
                                          xn[:, tt, kb * P:(kb + 1) * P], ident)
                    ins.then_inc(tr_done, 1)

            def plain(out_ap, a, b, start, stop, **kw):
                return M.matmul(out_ap, a, b, start=start, stop=stop, **kw)

            pe.wait_ge(got_const, 32)

            def gates(g):
                z, which = g // 2, g % 2
                if g == 0:
                    pe.wait_ge(got_wg, 32)
                    pe.wait_ge(conv_done, 8)
                else:
                    pe.wait_ge(tanh_done, 8 * g)
                for n in range(8):
                    ins = plain(ps[:, 4 + n // 2, (n % 2) * T:(n % 2) * T + T],
                                wg[:, 16 * which + 8 * z + n, :], xc[:, n, :], True, True)
                ins.then_inc(gates_done, 1)

            for b in range(16):
                if b >= 12:
                    pe.wait_ge(free_a, b - 11)
                elif b >= 4:
                    pe.wait_ge(free_d, b - 3)
                t_block(b // 2, 2 * (b % 2), b % 4, norm=0 if b == 0 else None)
                if b in (9, 11, 13, 15):
                    gates((b - 9) // 2)
            for c in range(2):
                pe.wait_ge(free_a, 6 + 2 * c)
                n_chunk(8 + 2 * c, c)

            def sums(branch):
                pe.wait_ge(mo_sq, branch + 1)
                squares = [sq_sum[:]] if branch else [th_i[:, 1, n, :] for n in range(8)]
                for n, sq in enumerate(squares):
                    ins = plain(ps[:, SUM_BANK[branch], 0:T], ones, sq, n == 0,
                                n == len(squares) - 1)
                ins.then_inc(mo_sum, 1)

            def attend(n0, heads, slots, q_of, k_of, v_of, exp_sem):
                _, p_sb_, pt = slots

                def scores(h):
                    if h >= 2:
                        pe.wait_ge(at_b, n0 + h - 1)
                    for qt in range(TT):
                        ins = plain(ps[:, 4 + h % 2, qt * T:(qt + 1) * T],
                                    q_of(h)[:, qt * P:(qt + 1) * P], k_of(h), True, True)
                    ins.then_inc(at_s, 1)

                def turned(h):
                    pe.wait_ge(at_p, n0 + h + 1)
                    if h:
                        pe.wait_ge(at_c, n0 + h)
                    for kt in range(TT):
                        for qt in range(TT):
                            ins = M.transpose(
                                ps[:, 6, kt * T + qt * P:kt * T + (qt + 1) * P],
                                p_sb_[:, h % 2, qt, kt * P:(kt + 1) * P], ident)
                    ins.then_inc(at_t, 1)

                def heads_out(h):
                    pe.wait_ge(at_c, n0 + h + 1)
                    if h:
                        exp_sem(h)
                    for kt in range(TT):
                        ins = plain(ps[:, 7, 0:T], v_of(h, kt), pt[:, h % 2, kt, :], kt == 0,
                                    kt == TT - 1)
                    ins.then_inc(at_o, 1)

                return scores, turned, heads_out

            pe.wait_ge(tanh_done, 32)
            scores, turned, heads_out = attend(
                0, HEADS1, at1, lambda h: q_t[:, h, :], lambda h: k_t[:, h, :],
                lambda h, kt: v_n[:, kt, h * P:(h + 1) * P], lambda h: pe.wait_ge(at_f, h))
            for m in range(16):
                pe.wait_ge(free_d, 9 + m // 2 if m < 4 else 10 + m - 3)
                t_block(12 + m // 2, 2 * (m % 2), m % 4)
                if m == 2:
                    sums(0)
                if m >= 2 and m % 2 == 0:
                    pe.wait_ge(free_d, 10 + m)
                    scores(m // 2 - 1)
                    if m >= 4:
                        heads_out(m // 2 - 2)
                elif m >= 3:
                    turned((m - 3) // 2)
            pe.wait_ge(free_d, 26)
            scores(HEADS1 - 1)
            heads_out(HEADS1 - 2)
            turned(HEADS1 - 1)
            heads_out(HEADS1 - 1)
            pe.wait_ge(at_b, HEADS1)
            sums(1)

            def n_stage(name, free):
                r0 = ROUND0[name]
                for c in range(4):
                    free(c)
                    n_chunk(r0 + 2 * c, c % 2)

            def both(d0, a0):
                def free(c):
                    if c >= 2:
                        pe.wait_ge(free_d, d0 + c - 1)
                        pe.wait_ge(free_a, a0 + c - 1)
                return free

            pe.wait_ge(x_lo, 32)
            pe.wait_ge(free_a, 8)
            pe.wait_ge(mo_ms, 2)
            n_stage("out1", both(26, 8))
            pe.wait_ge(free_a, 12)
            r0 = ROUND0["ffn"]

            def ffn_blocks(i, first=False):
                for s in range(2):
                    pe.wait_ge(free_a, i * 2 + (11 + s))
                    t_block(i * 2 + (r0 + s), 0, 2 * s, norm=1 if first and s == 0 else None)
                    pe.wait_ge(free_d, i * 2 + (29 + s))
                    t_block(i * 2 + (r0 + s), 2, 2 * s + 1)

            ffn_blocks(0, True)
            with pe.Fori(1, FB // 2) as i:
                ffn_blocks(i)
            pe.wait_ge(free_d, 74)
            pe.wait_ge(free_a, 56)
            r0 = ROUND0["down"]
            with pe.Fori(0, 2) as i:
                for c in range(2):
                    pe.wait_ge(free_d, i * 2 + (73 + c))
                    pe.wait_ge(free_a, i * 2 + (55 + c))
                    for q in range(22):
                        u = 22 * c + q
                        n_piece(i * 11 + (r0 + u // 4), u % 4, c, 2 * q, q == 0, q == 21,
                                (hid_h, hid_l))
            r0 = ROUND0["gate"]

            def embedding(c):
                for tt in range(TT):
                    for j in range(2):
                        ins = plain(ps[:, 4 + 2 * (c % 2) + tt, :], p_sb[:, j, tt * P:(tt + 1) * P],
                                    w_pr[:, j, c * NCH:(c + 1) * NCH], j == 0, j == 1)
                ins.then_inc(ple_done, 1)

            for c in range(4):
                if c == 0:
                    pe.wait_ge(free_d, 78)
                    pe.wait_ge(free_a, 60)
                elif c >= 2:
                    pe.wait_ge(free_a, 60 + c - 1)
                    pe.wait_ge(ple_free, c - 1)
                if c == 0:
                    pe.wait_ge(got_ple, 32)
                n_chunk(r0 + 2 * c, c % 2, norm=2 if c == 0 else None,
                        between=lambda c=c: embedding(c))

            r0 = ROUND0["in2"]
            pe.wait_ge(free_a, 64)
            t_block(r0, 0, 0, norm=3)
            pe.wait_ge(g_dve, 1)
            for kb in range(KB):
                ins = exact(ps[0:32, 4, 0:T], [m[:, kb, :] for m in (wgd_h, wgd_l)],
                            [m[:, kb, :] for m in (xh, xl)], T, kb == 0, kb == KB - 1)
            ins.then_inc(g_pe, 1)
            t_block(r0, 2, 1)
            t_block(r0 + 1, 0, 2)
            t_block(r0 + 1, 2, 3)
            pe.wait_ge(g_dve, 2)
            for m in range(4):
                ins = plain(tr_slot(4 + m), up[:, m * P:(m + 1) * P], gd_t[:], True, True)
            ins.then_inc(g_pe, 1)

            def scores_in_chunks():
                pe.wait_ge(g_dve, 4)
                for d in range(2):
                    for tt in range(TT):
                        for h in range(4):
                            rows, m = slice(64 * (h % 2), 64 * (h % 2) + 64), 2 * d + h // 2
                            at_ = (2 * d + h // 2) * P
                            ins = plain(ps[:, 4 + 2 * tt + h % 2, at_:at_ + P],
                                        g3[rows, m, tt * P:(tt + 1) * P],
                                        g2[rows, m, tt * P:(tt + 1) * P], True, True)
                ins.then_inc(g_pe, 1)

            def turn_key_states():
                pe.wait_ge(g_dve, 5)
                for tt in range(TT):
                    for m in range(4):
                        ins = M.transpose(ps[:, 4 + tt, m * P:(m + 1) * P],
                                          g4[:, m, tt * P:(tt + 1) * P], ident)
                ins.then_inc(g_pe, 1)

            def increments(d):
                pe.wait_ge(g_dve, 6 + d)
                for n in range(3):
                    c = n if d == 0 else 3 - n
                    rows = slice(64 * (c % 2), 64 * (c % 2) + 64)
                    for half in range(2):
                        ins = plain(inc_at(d, c, half), kst[rows, c // 2, 2 * d + half, :],
                                    va[rows, c // 2, half * T:(half + 1) * T], True, True)
                ins.then_inc(g_pe, 1)

            def gla_out():
                pe.wait_ge(g_dve, 8)
                for tt in range(TT):
                    for h in range(4):
                        bank, at_ = 4 + 2 * tt + h % 2, (h // 2) * P
                        rows = slice(64 * (h % 2), 64 * (h % 2) + 64)
                        for d in range(2):
                            o = (2 * d + h // 2) * P
                            plain(ps[:, bank, at_:at_ + P], sc_t[:, 2 * tt + h % 2, o:o + P],
                                  va[:, tt, h * P:(h + 1) * P], d == 0, False,
                                  skip_group_check=True)
                        for c in (2 * tt, 2 * tt + 1):
                            for d in range(2):
                                before = c - 1 if d == 0 else 2 - c
                                if before < 0:
                                    continue
                                half = slice(64 * (c % 2), 64 * (c % 2) + 64)
                                ins = plain(ps[half, bank, at_:at_ + P],
                                            g2[rows, 2 * d + h // 2, 64 * c:64 * c + 64],
                                            state[rows, d, before, h // 2, :], False, True,
                                            skip_group_check=True)
                ins.then_inc(g_pe, 1)

            def turn_qk(which):
                pe.wait_ge(qk_ready, which + 1)
                for h in range(HEADS2):
                    n = HEADS2 * which + h
                    if n >= 4:
                        if n - 4 < HEADS2:
                            pe.wait_ge(q_copied, n - 3)
                        else:
                            pe.wait_ge(k_copied, n - 3 - HEADS2)
                    for tt in range(TT):
                        ins = M.transpose(tr_slot(n % 8)[:, tt * P:(tt + 1) * P],
                                          qk_n[which][:, tt, h * P:(h + 1) * P], ident)
                    ins.then_inc(qk_turned, 1)

            waits = [(80, 0), (82, 0), (83, 0), (0, 65), (84, 66), (85, 67), (86, 68), (87, 69),
                     (88, 70), (89, 71), (90, 0)]
            then = {1: scores_in_chunks, 3: turn_key_states, 4: lambda: increments(0),
                    5: lambda: increments(1), 6: gla_out}
            for n in range(11):
                for s_, v_ in zip((free_d, free_a), waits[n]):
                    if v_:
                        pe.wait_ge(s_, v_)
                n_chunk(r0 + 2 + 2 * n, n % 2)
                if n in then:
                    then[n]()
                if n == 7:
                    pe.wait_ge(g_dve, 9)
                    turn_qk(0)
                if n == 9:
                    turn_qk(1)
            pe.wait_ge(g_dve, 11)
            pe.wait_ge(k_copied, HEADS2)
            for kb in range(4):
                for tt in range(TT):
                    ins = M.transpose(tr_slot(kb)[:, tt * P:(tt + 1) * P],
                                      o_n[:, tt, kb * P:(kb + 1) * P], ident)
                ins.then_inc(g_pe, 1)
            pe.wait_ge(x_lo, 84)
            pe.wait_ge(free_d, 92)
            scores, turned, heads_out = attend(
                HEADS1, HEADS2, at2, lambda h: q_t2[:, h, :], lambda h: k_t2[:, h, :],
                lambda h, kt: vn[:, kt, h * P:(h + 1) * P], lambda h: pe.wait_ge(x_lo, 84 + h))
            scores(0)
            scores(1)
            for h in range(HEADS2):
                turned(h)
                if h + 2 < HEADS2:
                    scores(h + 2)
                heads_out(h)
            pe.wait_ge(x_lo, 96)
            r0 = ROUND0["out2"]
            for c in range(4):
                if c >= 2:
                    pe.wait_ge(free_d, 92 + c - 1)
                n_chunk(r0 + 2 * c, c % 2)
            for b in range(KB):
                if b >= 4:
                    pe.wait_ge(free_d, 95 + b - 3)
                t_block(ROUND0["query"] + b // 2, 2 * (b % 2), b % 4, norm=4 if b == 0 else None)
            def scores_of_keys(tt):
                for r in range(16):
                    ins = plain(ps[:, 4 + r // 4, (r % 4) * P:(r % 4 + 1) * P],
                                qry_t[:, r, tt * P:(tt + 1) * P], keys_t[:, r, :], True, True)
                ins.then_inc(key_scores, 1)

            pe.wait_ge(free_d, 111)
            pe.wait_ge(got_keys, 16)
            scores_of_keys(0)
            r0 = ROUND0["peer_down"]

            def down_blocks(i, after_block=None):
                for j in range(4):
                    pe.wait_ge(free_a, i * 4 + (71 + j - 3))
                    t_block(i * 2 + (r0 + j // 2), 2 * (j % 2), j)
                    if after_block:
                        after_block(i, j)

            for j in range(4):
                t_block(r0 + j // 2, 2 * (j % 2), j)
            with pe.Fori(1, 3) as i:
                down_blocks(i)
            pe.wait_ge(lists_read, 16)
            scores_of_keys(1)
            with pe.Fori(3, 8) as i:
                down_blocks(i)
            pe.wait_ge(route_ready, 1)
            for k in range(3):
                for tt in range(TT):
                    ins = M.transpose(ps[:, 4 + k, tt * P:(tt + 1) * P],
                                      route[:, k, tt * P:(tt + 1) * P], ident)
            ins.then_inc(route_turned, 1)
            with pe.Fori(8, 16) as i:
                down_blocks(i)

            def gate_products(g, i, k, first=False):
                for n in range(4 * k, 4 * k + 4):
                    pe.wait_ge(hot_done, i * 16 + (g * T + n + 1))
                    if n % 8 == 0 and not first:
                        pe.wait_ge(gated_done, i * 2 + (32 * g + n // 8 - 1))
                    for part in range(3):
                        ins = plain(ps[:, 4 + n // 8, (n % 8) * 64:(n % 8 + 1) * 64],
                                    hot_i[:, n % HOTS, :], hot_j[:, n % HOTS, part, :], part == 0,
                                    part == 2)
                    ins.then_inc(gmat_done, 1)

            pe.wait_ge(routed, 1)
            down_blocks(16, lambda i, k: gate_products(0, 0, k, True))
            with pe.Fori(17, 32) as i:
                down_blocks(i, lambda i, k: gate_products(0, i - 16, k))

            def up_piece(i, k, half, first=False, last=False):
                pe.wait_ge(hl_done, i * 4 + (k + 1))
                for n in range(2):
                    ready(i + r0, k, n)
                    for tt in range(TT):
                        ins = exact(ps[:, 4 * half + 2 * tt + n, :],
                                    [m[:, k, tt * P:(tt + 1) * P] for m in (hg_h, hg_l)],
                                    [m[:, q, n * NCH:(n + 1) * NCH]
                                     for m, q in ((hi, k), (lo, k % 2))], NCH, first, last)
                        if tt == 1:
                            ins.then_inc((half_used, unit_used)[n], 1)

            r0 = ROUND0["peer_up"]
            pe.wait_ge(free_a, 71 + 128)
            for k in range(4):
                up_piece(0, k, 0, first=k == 0)
                gate_products(1, 0, k)
            with pe.Fori(1, 16) as i:
                for k in range(4):
                    up_piece(i, k, 0)
                    gate_products(1, i, k)
            with pe.Fori(16, 31) as i:
                for k in range(4):
                    up_piece(i, k, 0)
            for k in range(4):
                up_piece(31, k, 0, last=k == 3)
            for k in range(4):
                up_piece(32, k, 1, first=k == 0)
            with pe.Fori(33, 63) as i:
                for k in range(4):
                    up_piece(i, k, 1)
            for k in range(4):
                up_piece(63, k, 1, last=k == 3)


def pieces_t(w, blocks):
    w = w.reshape(2, 8, P, -1, P)[:, :, :, blocks]
    return w.transpose(3, 0, 2, 1, 4).reshape(-1, P, PIECE)


def pieces_n(w, first, chunks):
    w = w[:, first:first + chunks * NCH].reshape(-1, 2, P, chunks, NCH)
    return w.transpose(3, 0, 2, 1, 4).reshape(-1, P, PIECE)


def lay_out(x, p, g_mix_pre, w_in, rpb, conv_w, conv_b, w_rg_a, b_rg_a, w_rg_i, b_rg_i, lam,
            g_attn_out, g_rec_out, w_out, g_mix_post, g_ffn_pre, w_ffn_gate, w_ffn_up, w_ffn_down,
            g_ffn_post, g_ple_pre, w_ple_gate, w_ple_proj, g_ple_post, norm1_g_2, w_in_2,
            gla_up_f_2, gla_bias_f_2, gla_up_b_2, gla_bias_b_2, gla_out_g_2, q_norm_g_2,
            k_norm_g_2, w_out_2, norm2_g_2, peer_w_query_2, peer_sub_keys_2, peer_down_2,
            peer_up_2):
    c, band, dil = shape_constants()
    win, win2 = w_in[0], w_in_2[0]
    gate_up = np.stack([pieces_t(w_ffn_gate[0], np.arange(FB)).reshape(FB, 2, P, PIECE),
                        pieces_t(w_ffn_up[0], np.arange(FB)).reshape(FB, 2, P, PIECE)], 1)
    rest = np.concatenate([win2[:, 512:1024], win2[:, 1056:]], 1)
    down = peer_down_2[0].reshape(P, NKEY, 2, 8, P).transpose(1, 2, 4, 3, 0)
    up = peer_up_2[0].reshape(P, NKEY, 2, PIECE).transpose(2, 1, 0, 3)
    stream = np.concatenate([
        pieces_t(win, np.r_[24:40]), pieces_n(win, 2048, 2),
        pieces_t(win, np.stack([np.arange(8), np.arange(8, 16)], 1).reshape(-1)),
        pieces_n(w_out[0], 0, 4), gate_up.reshape(-1, P, PIECE), pieces_n(w_ffn_down[0], 0, 4),
        pieces_n(w_ple_gate[0], 0, 4), pieces_t(win2[:, 0:512], np.arange(4)),
        pieces_n(rest, 0, 11), pieces_n(w_out_2[0], 0, 4),
        pieces_t(peer_w_query_2[0], np.arange(KB)), down.reshape(-1, P, PIECE),
        up.reshape(-1, P, PIECE)])
    assert stream.shape[0] == PIECES

    def columns(*vectors):
        return np.concatenate([v.reshape(-1, P) for v in vectors]).T

    cols = columns(g_mix_pre, g_ffn_pre, g_ple_pre, norm1_g_2, norm2_g_2, g_attn_out, g_rec_out,
                   gla_out_g_2, conv_w, conv_b, b_rg_a, b_rg_i, lam, gla_bias_f_2, gla_bias_b_2)
    col_, row = np.arange(64), np.arange(4)
    gap = col_[None, :] - col_[:, None] + 15
    wide = rpb[0][:, (row[None, :] - row[:, None] + 7)[:, :, None, None],
                  np.clip(gap, 0, 30)[None, None]]
    wide = np.where((gap >= 0) & (gap <= 30), wide, np.zeros((), rpb.dtype))
    wide = wide.transpose(1, 3, 0, 2, 4).reshape(TT, P, HEADS1, T).transpose(1, 2, 0, 3)
    up_fb = np.zeros((32, 512), np.float32)
    up_fb[0:16, 0:256] = gla_up_f_2[0]
    up_fb[16:32, 256:512] = gla_up_b_2[0]
    gains = np.stack([np.broadcast_to(g[0], (P, D)) for g in (g_mix_post, g_ffn_post, g_ple_post)])
    return {
        "stream": stream,
        "cols": cols,
        "cons": c,
        "band": band,
        "dil": dil,
        "x": x[0],
        "rpb": wide,
        "w_gates": np.concatenate([w_rg_a[0].reshape(16, P, P), w_rg_i[0].reshape(16, P, P)])
        .transpose(1, 0, 2),
        "gains": gains,
        "p_t": p[0, 0].T.reshape(2, P, T).transpose(1, 0, 2),
        "w_proj": w_ple_proj[0].reshape(2, P, D).transpose(1, 0, 2),
        "w_gd": win2[:, 1024:1056].reshape(KB, P, 32).transpose(1, 0, 2),
        "up_fb": up_fb,
        "qk_gain": np.broadcast_to(np.stack([q_norm_g_2[0], k_norm_g_2[0]]), (P, 2, HD)),
        "sub_keys": peer_sub_keys_2[0].transpose(3, 0, 1, 2).reshape(P, KB, NKEY),
    }


def kernel(**inputs):
    import concourse.bacc as bacc
    from concourse.bass_utils import run_bass_kernel_spmd

    nc = bacc.Bacc("TRN2", target_bir_lowering=False, num_devices=1)
    laid = lay_out(**{k: np.asarray(v) for k, v in inputs.items()})
    arrays, args = {}, {}
    for name, a in laid.items():
        a = np.ascontiguousarray(a)
        arrays[f"in_{name}"] = a
        args[name] = nc.dram_tensor(f"in_{name}", a.shape, mybir.dt.from_np(a.dtype),
                                    kind="ExternalInput").ap()
    spill = nc.dram_tensor("spill", [P, TT, D], F32).ap()
    out = nc.dram_tensor("out", [T, D], F32, kind="ExternalOutput").ap()
    build(nc, spill=spill, out=out, **args)
    r = run_bass_kernel_spmd(nc, [arrays], core_ids=[0])
    return r.results[0]["out"].reshape(1, T, D)
```
